# Optimizing a Trainium2 kernel written in Bass

```python
import math
import jax, jax.numpy as jnp
from jax import lax
import numpy as np
import jax
import jax.numpy as jnp

D_MODEL = 1024
BATCH = 1
SEQ = 256
DEPTH = 2

D_FF = 2816
FFN_HALF = 0.5
DN_HEAD_DIM = 128
DN_HEADS = D_MODEL // 128
DN_WIDTH = DN_HEADS * DN_HEAD_DIM
DN_CONV = 4
DN_CHUNK = 64
SB_HEAD_DIM = 128
SB_HEADS = D_MODEL // 128
SB_WIDTH = SB_HEADS * SB_HEAD_DIM
SB_BLOCK = 128
IN_SIZES = (3 * DN_WIDTH, DN_WIDTH, DN_HEADS, DN_HEADS, SB_WIDTH, SB_WIDTH, SB_WIDTH, D_MODEL, D_MODEL)
N_IN = 4 * DN_WIDTH + 2 * DN_HEADS + 3 * SB_WIDTH + 2 * D_MODEL
RMS_EPS = 1e-6
L2_EPS = 1e-6


def rmsnorm(x, gain):
    xf = x.astype(jnp.float32)
    y = xf * lax.rsqrt(jnp.mean(xf * xf, axis=-1, keepdims=True) + RMS_EPS)
    return (y * gain.astype(jnp.float32)).astype(x.dtype)

def l2norm(x):
    xf = x.astype(jnp.float32)
    return xf * lax.rsqrt(jnp.sum(xf * xf, axis=-1, keepdims=True) + L2_EPS)

def swiglu(h, w_in, w_out):
    gate, up = jnp.split(h @ w_in, 2, axis=-1)
    return (jax.nn.silu(gate) * up) @ w_out

def causal_depthwise_conv(x, w):
    width, ch = w.shape
    return lax.conv_general_dilated(
        x, w[:, None, :], window_strides=(1,), padding=((width - 1, 0),),
        dimension_numbers=("NWC", "WIO", "NWC"), feature_group_count=ch)

def split_cols(proj):
    parts, start = [], 0
    for size in IN_SIZES:
        parts.append(proj[..., start:start + size])
        start += size
    return parts

def to_heads(t, n_heads, head_dim):
    b, s, _ = t.shape
    return t.reshape(b, s, n_heads, head_dim).transpose(0, 2, 1, 3)

def gated_delta_rule_chunked(q, k, v, g, beta):
    b, h, t, dk = q.shape
    dv = v.shape[-1]
    c = DN_CHUNK
    n = t // c
    q = (q * (dk ** -0.5)).reshape(b, h, n, c, dk)
    k = k.reshape(b, h, n, c, dk)
    v = v.astype(jnp.float32).reshape(b, h, n, c, dv)
    beta = beta.reshape(b, h, n, c)
    g = lax.cumsum(g.reshape(b, h, n, c), axis=3)
    idx = jnp.arange(c)
    lower_incl = idx[:, None] >= idx[None, :]
    strict = idx[:, None] > idx[None, :]
    decay = jnp.exp(jnp.where(lower_incl, g[..., :, None] - g[..., None, :], -jnp.inf))
    k_beta = k * beta[..., None]
    lmat = jnp.where(strict, jnp.einsum("bhnid,bhnjd->bhnij", k_beta, k) * decay, 0.0)
    amat = lmat + jnp.eye(c, dtype=jnp.float32)
    rhs = jnp.concatenate([v * beta[..., None], k_beta * jnp.exp(g)[..., None]], axis=-1)
    sol = lax.linalg.triangular_solve(amat, rhs, left_side=True, lower=True, unit_diagonal=True)
    u, w = sol[..., :dv], sol[..., dv:]
    attn_intra = jnp.einsum("bhnid,bhnjd->bhnij", q, k) * decay
    q_dec = q * jnp.exp(g)[..., None]
    g_last = g[..., -1]
    k_dec = k * jnp.exp(g_last[..., None] - g)[..., None]

    def chunk_step(state, inp):
        q_i, k_i, u_i, w_i, a_i, gl_i = inp
        v_new = u_i - jnp.einsum("bhcd,bhdv->bhcv", w_i, state)
        o_i = jnp.einsum("bhcd,bhdv->bhcv", q_i, state) + jnp.einsum("bhij,bhjv->bhiv", a_i, v_new)
        state = state * jnp.exp(gl_i)[..., None, None] + jnp.einsum("bhcd,bhcv->bhdv", k_i, v_new)
        return state, o_i

    chunk_first = lambda arr: jnp.moveaxis(arr, 2, 0)
    s0 = jnp.zeros((b, h, dk, dv), jnp.float32)
    _, o = lax.scan(chunk_step, s0, (chunk_first(q_dec), chunk_first(k_dec), chunk_first(u),
                                     chunk_first(w), chunk_first(attn_intra), chunk_first(g_last)))
    return jnp.moveaxis(o, 0, 2).reshape(b, h, t, dv)

def stick_breaking_attention(q, k, v):
    t = q.shape[2]
    scale = q.shape[-1] ** -0.5
    outs = []
    for blk in range(t // SB_BLOCK):
        t0, t1 = blk * SB_BLOCK, (blk + 1) * SB_BLOCK
        z = jnp.einsum("bhqd,bhkd->bhqk", q[:, :, t0:t1], k[:, :, :t1]).astype(jnp.float32) * scale
        causal = jnp.arange(t1)[None, :] < (t0 + jnp.arange(SB_BLOCK))[:, None]
        log_1mb = jnp.where(causal, -jax.nn.softplus(z), 0.0)
        survive = lax.cumsum(log_1mb, axis=3, reverse=True) - log_1mb
        weights = jnp.where(causal, jnp.exp(jax.nn.log_sigmoid(z) + survive), 0.0)
        outs.append(jnp.einsum("bhqk,bhkd->bhqd", weights.astype(v.dtype), v[:, :, :t1]))
    return jnp.concatenate(outs, axis=2)

def hybrid_mixer(h, w_in, conv_w, a_log, dt_bias, dn_out_norm, sb_q_norm, sb_k_norm,
                 w_branch_a, w_branch_b, w_out):
    b, t, _ = h.shape
    dn_qkv, dn_z, dn_b, dn_a, sb_q, sb_k, sb_v, gate_a, gate_b = split_cols(h @ w_in)
    qkv = jax.nn.silu(causal_depthwise_conv(dn_qkv, conv_w))
    q, k, v = jnp.split(qkv, 3, axis=-1)
    q = l2norm(to_heads(q, DN_HEADS, DN_HEAD_DIM))
    k = l2norm(to_heads(k, DN_HEADS, DN_HEAD_DIM))
    v = to_heads(v, DN_HEADS, DN_HEAD_DIM)
    beta = jax.nn.sigmoid(dn_b.astype(jnp.float32)).transpose(0, 2, 1)
    g = (-jnp.exp(a_log.astype(jnp.float32))
         * jax.nn.softplus(dn_a.astype(jnp.float32) + dt_bias.astype(jnp.float32))).transpose(0, 2, 1)
    o_a = gated_delta_rule_chunked(q, k, v, g, beta).transpose(0, 2, 1, 3)
    o_a = rmsnorm(o_a, dn_out_norm) * jax.nn.silu(dn_z.reshape(b, t, DN_HEADS, DN_HEAD_DIM).astype(jnp.float32))
    y_a = o_a.reshape(b, t, DN_WIDTH).astype(h.dtype) @ w_branch_a
    qb = rmsnorm(to_heads(sb_q, SB_HEADS, SB_HEAD_DIM), sb_q_norm)
    kb = rmsnorm(to_heads(sb_k, SB_HEADS, SB_HEAD_DIM), sb_k_norm)
    vb = to_heads(sb_v, SB_HEADS, SB_HEAD_DIM)
    o_b = stick_breaking_attention(qb, kb, vb).transpose(0, 2, 1, 3).reshape(b, t, SB_WIDTH)
    y_b = o_b @ w_branch_b
    merged = jax.nn.sigmoid(gate_a) * y_a + jax.nn.sigmoid(gate_b) * y_b
    return merged @ w_out

def first_inputs(seed: int = 0) -> dict:
    key = jax.random.key(seed)
    ks = jax.random.split(key, 20)
    L = DEPTH

    def dense(k, shape, fan_in):
        return jax.random.normal(k, shape, jnp.float32) * (fan_in ** -0.5)

    def gain(k, shape):
        return 1.0 + 0.1 * jax.random.normal(k, shape, jnp.float32)

    dt = jnp.exp(jax.random.uniform(ks[8], (L, DN_HEADS), jnp.float32, math.log(1e-3), math.log(1e-1)))
    return {
        "x": jax.random.normal(ks[0], (BATCH, SEQ, D_MODEL), jnp.float32),
        "ffn1_norm": gain(ks[1], (L, D_MODEL)),
        "ffn1_w_in": dense(ks[2], (L, D_MODEL, 2 * D_FF), D_MODEL),
        "ffn1_w_out": dense(ks[3], (L, D_FF, D_MODEL), D_FF),
        "mix_norm": gain(ks[4], (L, D_MODEL)),
        "w_in": dense(ks[5], (L, D_MODEL, N_IN), D_MODEL),
        "dn_conv_w": dense(ks[6], (L, DN_CONV, 3 * DN_WIDTH), DN_CONV),
        "dn_a_log": jnp.log(jax.random.uniform(ks[7], (L, DN_HEADS), jnp.float32, 1.0, 16.0)),
        "dn_dt_bias": dt + jnp.log(-jnp.expm1(-dt)),
        "dn_out_norm": gain(ks[9], (L, DN_HEAD_DIM)),
        "sb_q_norm": gain(ks[10], (L, SB_HEAD_DIM)),
        "sb_k_norm": gain(ks[11], (L, SB_HEAD_DIM)),
        "w_branch_a": dense(ks[12], (L, DN_WIDTH, D_MODEL), DN_WIDTH),
        "w_branch_b": dense(ks[13], (L, SB_WIDTH, D_MODEL), SB_WIDTH),
        "w_out": dense(ks[14], (L, D_MODEL, D_MODEL), D_MODEL),
        "ffn2_norm": gain(ks[15], (L, D_MODEL)),
        "ffn2_w_in": dense(ks[16], (L, D_MODEL, 2 * D_FF), D_MODEL),
        "ffn2_w_out": dense(ks[17], (L, D_FF, D_MODEL), D_FF),
    }

def first_block(x, ffn1_norm, ffn1_w_in, ffn1_w_out, mix_norm, w_in, dn_conv_w, dn_a_log, dn_dt_bias,
              dn_out_norm, sb_q_norm, sb_k_norm, w_branch_a, w_branch_b, w_out,
              ffn2_norm, ffn2_w_in, ffn2_w_out):
    for l in range(DEPTH):
        x = x + FFN_HALF * swiglu(rmsnorm(x, ffn1_norm[l]), ffn1_w_in[l], ffn1_w_out[l])
        x = x + hybrid_mixer(rmsnorm(x, mix_norm[l]), w_in[l], dn_conv_w[l], dn_a_log[l], dn_dt_bias[l],
                             dn_out_norm[l], sb_q_norm[l], sb_k_norm[l],
                             w_branch_a[l], w_branch_b[l], w_out[l])
        x = x + FFN_HALF * swiglu(rmsnorm(x, ffn2_norm[l]), ffn2_w_in[l], ffn2_w_out[l])
    return x


HEAD_DIM = 64
MLA_HEADS = 6
MLA_NOPE = 64
MLA_ROPE = 32
MLA_V = 64
MLA_Q_RANK = 256
MLA_KV_RANK = 128
ROPE_THETA = 10000.0
MLA_Q_BLOCK = 128
MOBA_HEADS = 6
MOBA_BLOCK = 256
MOBA_TOPK = 3
MOBA_Q_CHUNK = 32
DIL_PATTERNS = ((128, 1), (512, 4), (2048, 16))
DIL_GROUP_HEADS = 4
DIL_HEADS = DIL_GROUP_HEADS * len(DIL_PATTERNS)
N_ALIBI = DIL_HEADS + MOBA_HEADS
N_BRANCHES = 3
NORM_EPS = 1e-6
NEG_INF = -1e30
MLA_IN = MLA_Q_RANK + MLA_KV_RANK + MLA_ROPE
MOBA_IN = 3 * MOBA_HEADS * HEAD_DIM
DIL_IN = 3 * DIL_HEADS * HEAD_DIM
GATE_IN = N_BRANCHES * D_MODEL
IN_COLS = MLA_IN + MOBA_IN + DIL_IN + GATE_IN
MLA_OUT = MLA_HEADS * MLA_V
MOBA_OUT = MOBA_HEADS * HEAD_DIM
DIL_OUT = DIL_GROUP_HEADS * HEAD_DIM


def rms_norm(x, gain):
    xf = x.astype(jnp.float32)
    y = xf * lax.rsqrt(jnp.mean(xf * xf, axis=-1, keepdims=True) + NORM_EPS)
    return (y * gain.astype(jnp.float32)).astype(x.dtype)

def swiglu_2(h, w_gate, w_up, w_down):
    a = jnp.einsum('bsd,df->bsf', h, w_gate)
    u = jnp.einsum('bsd,df->bsf', h, w_up)
    return jnp.einsum('bsf,fd->bsd', jax.nn.silu(a) * u, w_down)

def alibi_slopes():
    return 2.0 ** (-8.0 * jnp.arange(1, N_ALIBI + 1, dtype=jnp.float32) / N_ALIBI)

def rope_tables(seq):
    pos = jnp.arange(seq, dtype=jnp.float32)
    inv = ROPE_THETA ** (-jnp.arange(0, MLA_ROPE, 2, dtype=jnp.float32) / MLA_ROPE)
    ang = pos[:, None] * inv[None, :]
    return jnp.cos(ang), jnp.sin(ang)

def apply_rope(t, cos, sin):
    cos = cos.astype(t.dtype)
    sin = sin.astype(t.dtype)
    t1, t2 = jnp.split(t, 2, axis=-1)
    return jnp.concatenate([t1 * cos - t2 * sin, t1 * sin + t2 * cos], axis=-1)

def mla_attention(h_cq, h_ckv, h_krope, q_norm, w_uq, kv_norm, w_ukv):
    B, S, _ = h_cq.shape
    cos, sin = rope_tables(S)
    c_q = rms_norm(h_cq, q_norm)
    q = jnp.einsum('bsr,rk->bsk', c_q, w_uq).reshape(B, S, MLA_HEADS, MLA_NOPE + MLA_ROPE)
    q = jnp.concatenate([q[..., :MLA_NOPE], apply_rope(q[..., MLA_NOPE:], cos[:, None], sin[:, None])], axis=-1)
    c_kv = rms_norm(h_ckv, kv_norm)
    kv = jnp.einsum('bsr,rk->bsk', c_kv, w_ukv).reshape(B, S, MLA_HEADS, MLA_NOPE + MLA_V)
    k_rope = apply_rope(h_krope, cos, sin)
    k = jnp.concatenate([kv[..., :MLA_NOPE], jnp.broadcast_to(k_rope[:, :, None, :], (B, S, MLA_HEADS, MLA_ROPE))], axis=-1)
    v = kv[..., MLA_NOPE:]
    q, k, v = (t.transpose(0, 2, 1, 3) for t in (q, k, v))
    scale = (MLA_NOPE + MLA_ROPE) ** -0.5
    nb = S // MLA_Q_BLOCK
    q_blocks = q.reshape(B, MLA_HEADS, nb, MLA_Q_BLOCK, MLA_NOPE + MLA_ROPE).transpose(2, 0, 1, 3, 4)
    kpos = jnp.arange(S)

    def block(args):
        qi, i = args
        s = jnp.einsum('bhqd,bhkd->bhqk', qi, k).astype(jnp.float32) * scale
        qpos = i * MLA_Q_BLOCK + jnp.arange(MLA_Q_BLOCK)
        s = jnp.where(kpos[None, :] <= qpos[:, None], s, NEG_INF)
        p = jax.nn.softmax(s, axis=-1).astype(v.dtype)
        return jnp.einsum('bhqk,bhkd->bhqd', p, v)

    o = lax.map(block, (q_blocks, jnp.arange(nb)))
    return o.transpose(1, 0, 3, 2, 4).reshape(B, S, MLA_OUT)

def moba_attention(q, k, v, slopes):
    B, H, S, D = q.shape
    nb = -(-S // MOBA_BLOCK)
    sp = nb * MOBA_BLOCK
    pad = ((0, 0), (0, 0), (0, sp - S), (0, 0))
    qp, kp, vp = (jnp.pad(t, pad) for t in (q, k, v))
    kb = kp.reshape(B, H, nb, MOBA_BLOCK, D)
    vb = vp.reshape(B, H, nb, MOBA_BLOCK, D)
    k_mean = jnp.mean(kb, axis=3)
    k_sel_n = min(MOBA_TOPK, nb)
    scale = D ** -0.5
    bi = jnp.arange(B)[:, None, None, None]
    hi = jnp.arange(H)[None, :, None, None]
    blk_ids = jnp.arange(nb)
    offs = jnp.arange(MOBA_BLOCK)
    slope5 = slopes[None, :, None, None, None]

    def chunk(c):
        start = c * MOBA_Q_CHUNK
        qc = lax.dynamic_slice_in_dim(qp, start, MOBA_Q_CHUNK, axis=2)
        b_own = start // MOBA_BLOCK
        tpos = start + jnp.arange(MOBA_Q_CHUNK)
        gate = jnp.einsum('bhqd,bhnd->bhqn', qc, k_mean).astype(jnp.float32)
        gate = jnp.where(blk_ids < b_own, gate, NEG_INF)
        _, idx = lax.top_k(gate, k_sel_n)
        sel_ok = idx < b_own
        k_sel = kb[bi, hi, idx]
        v_sel = vb[bi, hi, idx]
        s_sel = jnp.einsum('bhqd,bhqnpd->bhqnp', qc, k_sel).astype(jnp.float32) * scale
        kpos_sel = idx[..., None] * MOBA_BLOCK + offs
        dist_sel = (tpos[None, None, :, None, None] - kpos_sel).astype(jnp.float32)
        s_sel = jnp.where(sel_ok[..., None], s_sel - slope5 * dist_sel, NEG_INF)
        k_own = lax.dynamic_index_in_dim(kb, b_own, axis=2, keepdims=False)
        v_own = lax.dynamic_index_in_dim(vb, b_own, axis=2, keepdims=False)
        kpos_own = b_own * MOBA_BLOCK + offs
        dist_own = (tpos[:, None] - kpos_own[None, :]).astype(jnp.float32)
        s_own = jnp.einsum('bhqd,bhpd->bhqp', qc, k_own).astype(jnp.float32) * scale
        s_own = jnp.where(dist_own >= 0, s_own - slopes[None, :, None, None] * dist_own, NEG_INF)
        n_sel = k_sel_n * MOBA_BLOCK
        s = jnp.concatenate([s_sel.reshape(B, H, MOBA_Q_CHUNK, n_sel), s_own], axis=-1)
        p = jax.nn.softmax(s, axis=-1).astype(v.dtype)
        p_sel = p[..., :n_sel].reshape(B, H, MOBA_Q_CHUNK, k_sel_n, MOBA_BLOCK)
        p_own = p[..., n_sel:]
        return (jnp.einsum('bhqnp,bhqnpd->bhqd', p_sel, v_sel)
                + jnp.einsum('bhqp,bhpd->bhqd', p_own, v_own))

    o = lax.map(chunk, jnp.arange(sp // MOBA_Q_CHUNK))
    return o.transpose(1, 0, 3, 2, 4).reshape(B, sp, H * D)[:, :S]

def dilated_group_attention(q, k, v, window, dilation, slopes):
    B, H, S, D = q.shape
    L = window // dilation
    span = dilation * L
    P = -(-S // span) * span
    M = P // dilation
    nbk = M // L

    def to_blocks(t):
        t = jnp.pad(t, ((0, 0), (0, 0), (0, P - S), (0, 0)))
        return t.reshape(B, H, M, dilation, D).transpose(0, 1, 3, 2, 4).reshape(B, H, dilation, nbk, L, D)

    def window_keys(t):
        prev = jnp.pad(t[:, :, :, :-1], ((0, 0), (0, 0), (0, 0), (1, 0), (0, 0), (0, 0)))
        return jnp.concatenate([prev, t], axis=4)

    qb = to_blocks(q)
    kw = window_keys(to_blocks(k))
    vw = window_keys(to_blocks(v))
    s = jnp.einsum('bhrnqd,bhrnkd->bhrnqk', qb, kw).astype(jnp.float32) * (D ** -0.5)
    steps = L + jnp.arange(L)[:, None] - jnp.arange(2 * L)[None, :]
    band = (steps >= 0) & (steps <= L)
    before_start = (jnp.arange(nbk)[:, None, None] == 0) & (jnp.arange(2 * L) < L)[None, None, :]
    valid = band[None] & ~before_start
    dist = (steps * dilation).astype(jnp.float32)
    s = jnp.where(valid, s - slopes[None, :, None, None, None, None] * dist, NEG_INF)
    m = jnp.max(s, axis=-1, keepdims=True)
    e = jnp.exp(s - m)
    den = jnp.sum(e, axis=-1)
    o = jnp.einsum('bhrnqk,bhrnkd->bhrnqd', (e / den[..., None]).astype(v.dtype), vw)
    lse = m[..., 0] + jnp.log(den)
    o = o.reshape(B, H, dilation, M, D).transpose(0, 1, 3, 2, 4).reshape(B, H, P, D)[:, :, :S]
    lse = lse.reshape(B, H, dilation, M).transpose(0, 1, 3, 2).reshape(B, H, P)[:, :, :S]
    return o, lse

def hybrid_mixer_2(h, w_in, q_norm, w_uq, kv_norm, w_ukv, w_br_mla, w_br_moba, w_br_dil, w_out):
    B, S, _ = h.shape
    proj = jnp.einsum('bsd,dk->bsk', h, w_in)
    i0 = MLA_Q_RANK
    i1 = i0 + MLA_KV_RANK
    i2 = i1 + MLA_ROPE
    i3 = i2 + MOBA_IN
    i4 = i3 + DIL_IN
    h_cq, h_ckv, h_kr, h_moba, h_dil, h_gate = jnp.split(proj, [i0, i1, i2, i3, i4], axis=-1)
    slopes = alibi_slopes()
    a = mla_attention(h_cq, h_ckv, h_kr, q_norm, w_uq, kv_norm, w_ukv)
    mqkv = h_moba.reshape(B, S, 3, MOBA_HEADS, HEAD_DIM).transpose(2, 0, 3, 1, 4)
    b = moba_attention(mqkv[0], mqkv[1], mqkv[2], slopes[DIL_HEADS:])
    dqkv = h_dil.reshape(B, S, 3, DIL_HEADS, HEAD_DIM).transpose(2, 0, 3, 1, 4)
    outs, lses = [], []
    for g, (window, dilation) in enumerate(DIL_PATTERNS):
        hs = slice(g * DIL_GROUP_HEADS, (g + 1) * DIL_GROUP_HEADS)
        o_g, l_g = dilated_group_attention(dqkv[0][:, hs], dqkv[1][:, hs], dqkv[2][:, hs], window, dilation, slopes[hs])
        outs.append(o_g)
        lses.append(l_g)
    alpha = jax.nn.softmax(jnp.stack(lses), axis=0)
    c = jnp.einsum('gbhs,gbhsd->bhsd', alpha.astype(outs[0].dtype), jnp.stack(outs))
    c = c.transpose(0, 2, 1, 3).reshape(B, S, DIL_OUT)
    gates = jax.nn.sigmoid(h_gate).reshape(B, S, N_BRANCHES, D_MODEL)
    merged = (gates[:, :, 0] * jnp.einsum('bsk,kd->bsd', a, w_br_mla)
              + gates[:, :, 1] * jnp.einsum('bsk,kd->bsd', b, w_br_moba)
              + gates[:, :, 2] * jnp.einsum('bsk,kd->bsd', c, w_br_dil))
    return jnp.einsum('bsd,de->bse', merged, w_out)

def second_inputs(seed: int = 0) -> dict:
    key = jax.random.key(seed)
    ks = jax.random.split(key, 20)

    def nrm(k, shape, fan_in):
        return jax.random.normal(k, shape, jnp.float32) * (fan_in ** -0.5)

    def gain(k, shape):
        return 1.0 + 0.01 * jax.random.normal(k, shape, jnp.float32)

    return {
        'x': jax.random.normal(ks[0], (BATCH, SEQ, D_MODEL), jnp.float32),
        'ffn1_norm': gain(ks[1], (DEPTH, D_MODEL)),
        'ffn1_w_gate': nrm(ks[2], (DEPTH, D_MODEL, D_FF), D_MODEL),
        'ffn1_w_up': nrm(ks[3], (DEPTH, D_MODEL, D_FF), D_MODEL),
        'ffn1_w_down': nrm(ks[4], (DEPTH, D_FF, D_MODEL), D_FF),
        'mix_norm': gain(ks[5], (DEPTH, D_MODEL)),
        'w_in': nrm(ks[6], (DEPTH, D_MODEL, IN_COLS), D_MODEL),
        'q_norm': gain(ks[7], (DEPTH, MLA_Q_RANK)),
        'w_uq': nrm(ks[8], (DEPTH, MLA_Q_RANK, MLA_HEADS * (MLA_NOPE + MLA_ROPE)), MLA_Q_RANK),
        'kv_norm': gain(ks[9], (DEPTH, MLA_KV_RANK)),
        'w_ukv': nrm(ks[10], (DEPTH, MLA_KV_RANK, MLA_HEADS * (MLA_NOPE + MLA_V)), MLA_KV_RANK),
        'w_br_mla': nrm(ks[11], (DEPTH, MLA_OUT, D_MODEL), MLA_OUT),
        'w_br_moba': nrm(ks[12], (DEPTH, MOBA_OUT, D_MODEL), MOBA_OUT),
        'w_br_dil': nrm(ks[13], (DEPTH, DIL_OUT, D_MODEL), DIL_OUT),
        'w_out': nrm(ks[14], (DEPTH, D_MODEL, D_MODEL), D_MODEL),
        'ffn2_norm': gain(ks[15], (DEPTH, D_MODEL)),
        'ffn2_w_gate': nrm(ks[16], (DEPTH, D_MODEL, D_FF), D_MODEL),
        'ffn2_w_up': nrm(ks[17], (DEPTH, D_MODEL, D_FF), D_MODEL),
        'ffn2_w_down': nrm(ks[18], (DEPTH, D_FF, D_MODEL), D_FF),
        'final_norm': gain(ks[19], (D_MODEL,)),
    }

def second_block(x, ffn1_norm, ffn1_w_gate, ffn1_w_up, ffn1_w_down, mix_norm, w_in, q_norm, w_uq,
              kv_norm, w_ukv, w_br_mla, w_br_moba, w_br_dil, w_out, ffn2_norm, ffn2_w_gate,
              ffn2_w_up, ffn2_w_down, final_norm):
    for l in range(DEPTH):
        x = x + 0.5 * swiglu_2(rms_norm(x, ffn1_norm[l]), ffn1_w_gate[l], ffn1_w_up[l], ffn1_w_down[l])
        x = x + hybrid_mixer_2(rms_norm(x, mix_norm[l]), w_in[l], q_norm[l], w_uq[l], kv_norm[l], w_ukv[l],
                             w_br_mla[l], w_br_moba[l], w_br_dil[l], w_out[l])
        x = x + 0.5 * swiglu_2(rms_norm(x, ffn2_norm[l]), ffn2_w_gate[l], ffn2_w_up[l], ffn2_w_down[l])
    return rms_norm(x, final_norm)


def setup_inputs(seed=0):
    out = dict(first_inputs(seed))
    for name, value in second_inputs(seed + 1).items():
        if name != "x":
            out[name + "_2"] = value
    return out


def reference(
    x, ffn1_norm, ffn1_w_in, ffn1_w_out, mix_norm, w_in, dn_conv_w, dn_a_log, dn_dt_bias,
    dn_out_norm, sb_q_norm, sb_k_norm, w_branch_a, w_branch_b, w_out, ffn2_norm, ffn2_w_in,
    ffn2_w_out, ffn1_norm_2, ffn1_w_gate_2, ffn1_w_up_2, ffn1_w_down_2, mix_norm_2, w_in_2,
    q_norm_2, w_uq_2, kv_norm_2, w_ukv_2, w_br_mla_2, w_br_moba_2, w_br_dil_2, w_out_2,
    ffn2_norm_2, ffn2_w_gate_2, ffn2_w_up_2, ffn2_w_down_2, final_norm_2,
):
    x = first_block(
        x, ffn1_norm, ffn1_w_in, ffn1_w_out, mix_norm, w_in, dn_conv_w, dn_a_log, dn_dt_bias,
        dn_out_norm, sb_q_norm, sb_k_norm, w_branch_a, w_branch_b, w_out, ffn2_norm, ffn2_w_in,
        ffn2_w_out,
    )
    return second_block(
        x, ffn1_norm_2, ffn1_w_gate_2, ffn1_w_up_2, ffn1_w_down_2, mix_norm_2, w_in_2, q_norm_2,
        w_uq_2, kv_norm_2, w_ukv_2, w_br_mla_2, w_br_moba_2, w_br_dil_2, w_out_2, ffn2_norm_2,
        ffn2_w_gate_2, ffn2_w_up_2, ffn2_w_down_2, final_norm_2,
    )


_drawn_inputs = setup_inputs


def setup_inputs(seed=0):
    import zlib

    import numpy as np

    out = dict(_drawn_inputs(seed))
    spreads = {}
    factors = {'ffn1_norm_2': 8.0,
     'mix_norm_2': 8.0,
     'q_norm_2': 8.0,
     'kv_norm_2': 8.0,
     'ffn2_norm_2': 8.0,
     'final_norm_2': 5.171}
    for name, (base, spread) in spreads.items():
        noise = np.random.default_rng([zlib.crc32(name.encode()), seed]).standard_normal(out[name].shape)
        drawn = base * np.exp(spread * noise) if base else spread * noise
        out[name] = jnp.asarray(drawn.astype(out[name].dtype))
    for name, factor in factors.items():
        out[name] = (out[name] * factor).astype(out[name].dtype)
    return out
```

```python
from contextlib import ExitStack

import numpy as np

import concourse.bass as bass
from concourse import mybir

F32 = mybir.dt.float32
F32R = mybir.dt.float32r
ACT = mybir.ActivationFunctionType
ALU = mybir.AluOpType
AX = mybir.AxisListType
ds = bass.ds

P = 128
D = 1024
KC = D // P
T = 256
NT = T // P
F = 2816
LAYERS = 2
UNITS = F // 256
ITEM = 2048
RING = 3
FFN_ITEMS = 3 * UNITS
EPS = 1e-6
NEG = -1e30
HEADS = 8



def const_table():
    j = np.arange(P)[:, None]
    i = np.arange(P)[None, :]
    parts = {
        "ident": (i == j),
        "ones": np.ones((P, P)),
        "triu": (j <= i),
        "decay_mask": np.where(j <= i, 0.0, NEG),
        "neg_tri": -1.0 * (j >= i),
        "neg_ones": -np.ones((P, P)),
        "sb_neg": np.where(np.concatenate([j < i, np.ones((P, P)), j < i], axis=1) > 0, 0.0, NEG),
        "sb_mask": np.concatenate([j < i, np.ones((P, P)), j < i], axis=1),
    }
    for s in range(7):
        parts[f"level{s}"] = ((j >> s) + 1 == (i >> s)) & ((i >> s) % 2 == 1)
    pos = np.arange(T, dtype=np.float32)
    inv = (10000.0 ** (-np.arange(0, 32, 2, dtype=np.float32) / 32)).astype(np.float32)
    ang = np.zeros((P, T), np.float32)
    ang[64:80] = ang[80:96] = inv[:, None] * pos[None, :]
    parts["cos"] = np.cos(ang)
    parts["sin"] = np.sin(ang)
    turn = np.zeros((P, 96))
    for m in range(64, 80):
        turn[m + 16, m] = -1.0
        turn[m, m + 16] = 1.0
    parts["turn"] = turn
    q = np.arange(P)[:, None]
    tiles = [(0, 0), (1, 0), (1, 1)]
    dist = np.concatenate([(P * a + q) - (P * b + i) for a, b in tiles], axis=1).astype(np.float64)
    parts["causal"] = np.where(dist >= 0, 0.0, NEG)
    parts["all"] = np.where(dist >= 0, -dist, NEG)
    parts["window"] = np.where((dist >= 0) & (dist <= 128), -dist, NEG)
    parts["step4"] = np.where((dist >= 0) & (dist % 4 == 0), -dist, NEG)
    parts["step16"] = np.where((dist >= 0) & (dist % 16 == 0), -dist, NEG)
    at, where = 0, {}
    for name, value in parts.items():
        where[name] = (at, at + value.shape[1])
        at += value.shape[1]
    return np.concatenate([v.astype(np.float32) for v in parts.values()], axis=1), where


INPUTS = [
    "x", "ffn1_norm", "ffn1_w_in", "ffn1_w_out", "mix_norm", "w_in", "dn_conv_w", "dn_a_log", "dn_dt_bias",
    "dn_out_norm", "sb_q_norm", "sb_k_norm", "w_branch_a", "w_branch_b", "w_out", "ffn2_norm", "ffn2_w_in",
    "ffn2_w_out", "ffn1_norm_2", "ffn1_w_gate_2", "ffn1_w_up_2", "ffn1_w_down_2", "mix_norm_2", "w_in_2",
    "q_norm_2", "w_uq_2", "kv_norm_2", "w_ukv_2", "w_br_mla_2", "w_br_moba_2", "w_br_dil_2", "w_out_2",
    "ffn2_norm_2", "ffn2_w_gate_2", "ffn2_w_up_2", "ffn2_w_down_2", "final_norm_2",
]

V_FFN1, V_MIX, V_FFN2 = 0, KC, 2 * KC
V_DN_OUT, V_SBQ, V_SBK, V_CONV = 24, 25, 26, 27
ROWS1 = V_CONV + 4 * 24
V_QN, V_KVN, V_FINAL = 24, 26, 27
ROWS2 = V_FINAL + KC

MIX1 = ([("k", 1024 + 256 * i) for i in range(4)] + [("q", 256 * i) for i in range(4)]
        + [("v", 2048 + 256 * i) for i in range(4)] + [("ba", 4096)]
        + [("z", 3072 + 256 * i) for i in range(4)]
        + [("sbq", 4112 + 256 * i) for i in range(4)] + [("sbk", 5136 + 256 * i) for i in range(4)]
        + [("sbv", 6160 + 256 * i) for i in range(4)]
        + [("gate", 7184 + 256 * i) for i in range(8)])
OUT1 = [(("a", "b")[i % 2], 256 * (i // 2)) for i in range(8)] + [("out", 256 * i) for i in range(4)]
MIX2 = ([("cq", 0), ("ckv", 256)] + [("mob", 416 + 256 * i) for i in range(3)] + [("mv", 1184), ("mv2", 1440)]
        + [("dil", 1568 + 256 * i) for i in range(6)] + [("dv", 3104 + 256 * i) for i in range(3)] + [("up", 0)]
        + [("gate", 3872 + 256 * i) for i in range(12)])
OUT2 = [("br", 256 * i) for i in range(4)] + [("out", 256 * i) for i in range(4)]


def width(kind):
    return {"ba": KC * 16, "mv2": KC * 128, "up": 2 * 576 + 768}.get(kind, ITEM)


def copies(kind):
    return {"up": 2, "br": 3}.get(kind, 1)


LO_START = 1


class Phase:

    def __init__(self, base, loads, items):
        self.base, self.loads, self.items, self.n = base, list(loads), items, len(items)

    def item(self, j):
        return self.base + j + 1

    def loaded(self, j):
        s = j % RING
        return 16 * (self.loads[s] + sum(copies(self.items[i][0]) for i in range(s, j + 1, RING)))

    def after(self):
        return [self.loads[s] + sum(copies(k) for k, _ in self.items[s::RING]) for s in range(RING)]


FFN_LIST = [("ffn", 0)] * FFN_ITEMS


def plan(first, second):
    out = []
    base0, loads0 = 0, [0] * RING
    for lists in (first, second):
        base, loads, phases = 0, [0] * RING, []
        for items in lists:
            phases.append(Phase(base, loads, items))
            loads, base = phases[-1].after(), base + len(items)
        out.append((phases, base, loads, base0, loads0))
        base0 += LAYERS * base
        loads0 = [a + LAYERS * b for a, b in zip(loads0, loads)]
    return out


def in_layer(block_plan, k, layer):
    phases, n, loads, base0, loads0 = block_plan
    p = phases[k]
    return Phase(layer * n + (base0 + p.base), [layer * loads[s] + (loads0[s] + p.loads[s]) for s in range(RING)],
                 p.items)


def build(nc, a, consts_dram, out_dram):
    where = const_table()[1]
    ncol = max(b for _, b in where.values())
    with ExitStack() as ctx:
        top = [(nc.sbuf_base + 63) // 64 * 64]

        def put(name, shape, dt=F32, at=None):
            here = top[0] if at is None else at
            t = nc.alloc_sbuf_tensor_at(name, [P] + shape, dt, offset=here)
            size = 4 * int(np.prod(shape))
            if at is None:
                top[0] = (here + size + 63) // 64 * 64
            assert here + size <= nc.sbuf_usable_end, (name, here + size, nc.sbuf_usable_end)
            return t

        x = put("x_fm", [KC, T])
        consts = put("consts", [ncol])
        vecs = put("vecs", [4, P])
        vec = put("vec_layer", [P])
        eps_col = put("eps_col", [4])
        dta = put("dt_alog", [LAYERS, 2, HEADS])
        spare = put("spare", [1])
        zeros = put("zeros", [P], F32R)
        raw = [put(f"raw{s}", [ITEM]) for s in range(RING)]
        w_hi = [put(f"w_hi{s}", [ITEM], F32R) for s in range(RING)]
        w_lo = [put(f"w_lo{s}", [ITEM], F32R) for s in range(RING)]
        xn_at = top[0]
        xn_hi = put("xn_hi", [KC, T], F32R)
        xn_lo = put("xn_lo", [KC, T], F32R)
        shared = top[0]
        gate_act = put("gate_act", [2, T], at=shared)
        hidden = [put(f"hidden{u}", [2, T], at=shared + 2048 + 20480 * u) for u in range(2)]
        hid_hi = [put(f"hid_hi{u}", [2, T], F32R, at=shared + 4096 + 2048 * u) for u in range(2)]
        hid_lo = [put(f"hid_lo{u}", [2, T], F32R, at=shared + 8192 + 2048 * u) for u in range(2)]
        work = put("work", [KC, T], at=shared + 12288)
        root = put("root", [T], at=shared + 20480)
        rstd = put("rstd", [T], at=shared + 21504)
        stage = put("stage", [NT, D], at=shared)
        vrows = put("vrows", [4, P], at=shared + 8192)

        C = {k: consts[:, lo:hi] for k, (lo, hi) in where.items()}
        ident, ones = C["ident"], C["ones"]
        bank = [ctx.enter_context(nc.psum_tensor(f"bank{b}", [P, 512], F32)) for b in range(8)]
        pair = [b[:, :].rearrange("p (c t) -> p c t", c=2) for b in bank]

        def sem(name):
            return ctx.enter_context(nc.semaphore(name))

        s_const = sem("const_loaded")
        s_setup = sem("setup_done")
        s_xT = sem("x_transposed")
        s_vT = sem("vecs_transposed")
        s_vecs = sem("vecs_ready")
        loaded = [sem(f"slot{s}_loaded") for s in range(RING)]
        s_hi = sem("item_hi")
        s_lo = sem("item_lo")
        s_used = sem("item_used")
        s_x = sem("x_updated")
        s_sq = sem("squares")
        s_ss = sem("square_sums")
        s_root = sem("root_ready")
        s_xn = sem("normed")
        s_xhi = sem("normed_hi")
        s_xlo = sem("normed_lo")
        s_gact = sem("gate_activated")
        s_hid = sem("hidden_ready")
        s_hhi = sem("hidden_hi")
        s_hlo = sem("hidden_lo")
        s_yT = sem("out_transposed")
        s_y = sem("out_copied")
        s_stored = sem("stored")

        first = [FFN_LIST, MIX1, OUT1, FFN_LIST]
        second = [FFN_LIST, MIX2, OUT2, FFN_LIST]
        plans = plan(first, second)
        blocks = range(2)

        def norm_index(block, layer, k):
            return layer * 3 + (LAYERS * 3 * block + k)

        def ffn_index(block, layer, k):
            return layer * 2 + (LAYERS * 2 * block + k)

        last_norm = norm_index(2, 0, 0)

        def rows(w):
            return w.rearrange("(k p) n -> p k n", p=P)

        def cols(w, at, n=256):
            return rows(w)[:, :, at:at + n] if isinstance(at, int) else rows(w)[:, :, ds(at, n)]

        def slot_view(t, k, n):
            return t[:, 0:k * n].rearrange("p (k n) -> p k n", k=k)

        def bring(sp, slot, dst, src, split=None):
            sp.lower_val(src.offset * 4)
            if split is not None:
                sp.wait_ge(s_lo, split + LO_START)
            sp.dma_start(dst, src).then_inc(loaded[slot], 16)

        def split_hi(act, p, j, slot, load_count, free=True):
            n = width(p.items[j][0]) if isinstance(j, int) else ITEM
            act.wait_ge(loaded[slot], load_count)
            if free:
                act.wait_ge(s_used, p.base + (j - 2))
            act.activation(w_hi[slot][:, 0:n], raw[slot][:, 0:n], ACT.Copy).then_inc(s_hi, 1)

        def split_lo(dve, p, j, slot):
            n = width(p.items[j][0]) if isinstance(j, int) else ITEM
            dve.wait_ge(s_hi, p.base + (j + 1))
            dve.tensor_tensor(w_lo[slot][:, 0:n], raw[slot][:, 0:n], w_hi[slot][:, 0:n].bitcast(F32),
                              ALU.subtract).then_inc(s_lo, 1)

        def product(pe, out, a_hi, a_lo, b_hi, b_lo, start, stop, check=False):
            pe.matmul(out, a_hi, b_hi, start=start, stop=False, skip_group_check=check)
            pe.matmul(out, a_hi, b_lo, start=False, stop=False, skip_group_check=check)
            return pe.matmul(out, a_lo, b_hi, start=False, stop=stop, skip_group_check=check)

        def features(pe, slot, out, in_hi, in_lo, k=KC, n=256, off=0, m=P):
            hi = slot_view(w_hi[slot][:, off:off + k * n], k, n)
            lo = slot_view(w_lo[slot][:, off:off + k * n], k, n)
            for c in range(n // m):
                for kc in range(k):
                    mm = product(pe, out[:, c, :], hi[:, kc, m * c:m * c + m], lo[:, kc, m * c:m * c + m],
                                 in_hi[:, kc, :], in_lo[:, kc, :], kc == 0, kc == k - 1)
            return mm

        def tokens(pe, slot, out, in_hi, in_lo, k=KC, n=256, off=0):
            hi = slot_view(w_hi[slot][:, off:off + k * n], k, n)
            lo = slot_view(w_lo[slot][:, off:off + k * n], k, n)
            for t in range(NT):
                for kc in range(k):
                    mm = product(pe, out[:, t, 0:n], in_hi[:, kc, P * t:P * t + P], in_lo[:, kc, P * t:P * t + P],
                                 hi[:, kc, :], lo[:, kc, :], kc == 0, kc == k - 1)
            return mm

        def norm_act(act, q, prologue):
            for g in range(4):
                act.wait_ge(s_x, q * 4 + (g + 1))
                act.activation(work[:, 2 * g:2 * g + 2, :], x[:, 2 * g:2 * g + 2, :], ACT.Square).then_inc(s_sq, 1)
            prologue[0]()
            act.wait_ge(s_ss, q + 1)
            act.activation(root[:, :], bank[4][:, 0:T], ACT.Sqrt, bias=eps_col[:, 0:1],
                           scale=1.0 / D).then_inc(s_root, 1)
            for h in range(2):
                act.wait_ge(s_xn, q * 2 + (h + 1))
                act.activation(xn_hi[:, 4 * h:4 * h + 4, :], work[:, 4 * h:4 * h + 4, :], ACT.Copy).then_inc(s_xhi, 1)
            prologue[1]()

        def norm_pe(pe, q):
            for kc in range(KC):
                if kc % 2 == 0:
                    pe.wait_ge(s_sq, q * 4 + (kc // 2 + 1))
                mm = pe.matmul(bank[4][:, 0:T], ones, work[:, kc, :], start=(kc == 0), stop=(kc == KC - 1))
            mm.then_inc(s_ss, 1)

        def norm_dve(dve, q, gain, prologue, out=None):
            dve.wait_ge(s_root, q + 1)
            dve.reciprocal(rstd[:, :], root[:, :])
            dve.drain()
            for kc in range(KC):
                ins = dve.scalar_tensor_tensor(out=work[:, kc, :], in0=x[:, kc, :],
                                               scalar=vec[:, gain + kc:gain + kc + 1], in1=rstd[:, :],
                                               op0=ALU.mult, op1=ALU.mult)
                if kc % 4 == 3:
                    ins.then_inc(s_xn, 1)
            prologue()
            for h in range(2):
                dve.wait_ge(s_xhi, q * 2 + (h + 1))
                s = slice(4 * h, 4 * h + 4)
                dve.tensor_tensor(xn_lo[:, s, :], work[:, s, :], xn_hi[:, s, :].bitcast(F32),
                                  ALU.subtract).then_inc(s_xlo, 1)

        def ffn_sp(sp, p, gate_w, gate_at, up_w, up_at, down_w):
            def put_in(slot, src, k, n, split=None):
                bring(sp, slot, slot_view(raw[slot], k, n), src, split)

            def unit(u, slots):
                j = u * 3 - 1
                put_in(slots[0], cols(gate_w, u * 256 + gate_at), KC, 256, p.base + (j - 2))
                put_in(slots[1], cols(up_w, u * 256 + up_at), KC, 256, p.base + (j - 1))
                put_in(slots[2], rows(down_w)[:, ds((u - 1) * 2, 2), :], 2, D, p.base + j)

            put_in(0, cols(gate_w, gate_at), KC, 256, p.base)
            put_in(1, cols(up_w, up_at), KC, 256)
            put_in(2, cols(gate_w, gate_at + 256), KC, 256)
            put_in(0, cols(up_w, up_at + 256), KC, 256, p.base + 1)
            put_in(1, rows(down_w)[:, 0:2, :], 2, D, p.base + 2)
            with sp.Fori(2, UNITS, 1) as u:
                unit(u, (2, 0, 1))
            put_in(2, rows(down_w)[:, 2 * UNITS - 2:2 * UNITS, :], 2, D, p.base + (FFN_ITEMS - 3))

        def ffn_pe(pe, p, q, f):
            norm_pe(pe, q)
            pe.wait_ge(s_setup, 2)
            for b in range(4):
                pe.matmul(bank[b][:, 0:P], zeros[:, :], zeros[:, :], start=True, stop=False, skip_group_check=True)
            pe.wait_ge(s_xlo, q * 2 + 2)

            def project(j, slot, b):
                pe.wait_ge(s_lo, p.base + (j + 1 + LO_START))
                features(pe, slot, pair[b], xn_hi, xn_lo).then_inc(s_used, 1)

            def down(j, slot, u, par, last=False):
                pe.wait_ge(s_hlo, f * UNITS + (u + 1))
                pe.wait_ge(s_lo, p.base + (j + 1 + LO_START))
                for kk in range(2):
                    hi = slot_view(w_hi[slot], 2, D)[:, kk, :]
                    lo = slot_view(w_lo[slot], 2, D)[:, kk, :]
                    for m in range(KC):
                        mm = product(pe, pair[m // 2][:, m % 2, :], hi[:, P * m:P * m + P], lo[:, P * m:P * m + P],
                                     hid_hi[par][:, kk, :], hid_lo[par][:, kk, :], False, last and kk == 1, True)
                mm.then_inc(s_used, 1)

            project(0, 0, 4)
            project(1, 1, 5)
            with pe.Fori(1, UNITS, 2) as u:
                project(u * 3 - 1, 2, 6)
                project(u * 3, 0, 7)
                down(u * 3 + 1, 1, u - 1, 0)
                project(u * 3 + 2, 2, 4)
                project(u * 3 + 3, 0, 5)
                down(u * 3 + 4, 1, u, 1)
            down(FFN_ITEMS - 1, 2, UNITS - 1, 0, True)

        def ffn_act(act, p, q, f):
            def hi_first(j):
                split_hi(act, p, j, j, p.loaded(j), free=False)
            norm_act(act, q, (lambda: hi_first(0), lambda: (hi_first(1), hi_first(2))))

            def turn(u, j, par, slots):
                act.wait_ge(s_used, p.base + (j + 1))
                act.activation(gate_act[:, :, :], pair[4 + 2 * par], ACT.Silu).then_inc(s_gact, 1)

            def hi_hidden(u, par):
                act.wait_ge(s_hid, f * UNITS + (u + 1))
                act.activation(hid_hi[par][:, :, :], hidden[par][:, :, :], ACT.Copy).then_inc(s_hhi, 1)

            def next_hi(j, slot, n_loaded):
                act.wait_ge(loaded[slot], n_loaded)
                act.wait_ge(s_used, p.base + (j - 2))
                act.activation(w_hi[slot][:, :], raw[slot][:, :], ACT.Copy).then_inc(s_hi, 1)

            L = p.loads
            turn(0, 0, 0, None)
            next_hi(3, 0, (L[0] + 2) * 16)
            hi_hidden(0, 0)
            next_hi(4, 1, (L[1] + 2) * 16)

            def unit(u, par, ahead=3):
                turn(u, u * 3 - 1, par, None)
                next_hi(u * 3 + 2, 2, (L[2] + (u + 1)) * 16)
                hi_hidden(u, par)
                if ahead == 3:
                    next_hi(u * 3 + 3, 0, (L[0] + (u + 2)) * 16)
                    next_hi(u * 3 + 4, 1, (L[1] + (u + 2)) * 16)
            with act.Fori(1, UNITS - 2, 2) as u:
                unit(u, 1)
                unit(u + 1, 0)
            unit(UNITS - 2, 1)
            unit(UNITS - 1, 0, 1)
            act.wait_ge(s_used, p.base + FFN_ITEMS)

        def ffn_dve(dve, p, q, f, gain):
            def lo(j, slot):
                dve.wait_ge(s_hi, p.base + (j + 1))
                dve.tensor_tensor(w_lo[slot][:, :], raw[slot][:, :], w_hi[slot][:, :].bitcast(F32),
                                  ALU.subtract).then_inc(s_lo, 1)
            norm_dve(dve, q, gain, lambda: lo(0, 0))
            lo(1, 1)
            lo(2, 2)

            def unit(u, j, par, slots):
                dve.wait_ge(s_gact, f * UNITS + (u + 1))
                dve.wait_ge(s_used, p.base + (j + 2))
                dve.tensor_tensor(hidden[par][:, :, :], gate_act[:, :, :], pair[5 + 2 * par], ALU.mult).then_inc(s_hid, 1)
                lo(j + 3, slots[0])
                dve.wait_ge(s_hhi, f * UNITS + (u + 1))
                dve.tensor_tensor(hid_lo[par][:, :, :], hidden[par][:, :, :], hid_hi[par][:, :, :].bitcast(F32),
                                  ALU.subtract).then_inc(s_hlo, 1)
                for i in range(1, len(slots)):
                    lo(j + 3 + i, slots[i])
            unit(0, 0, 0, (0, 1))
            with dve.Fori(1, UNITS - 2, 2) as u:
                unit(u, u * 3 - 1, 1, (2, 0, 1))
                unit(u + 1, u * 3 + 2, 0, (2, 0, 1))
            unit(UNITS - 2, (UNITS - 2) * 3 - 1, 1, (2, 0, 1))
            unit(UNITS - 1, (UNITS - 1) * 3 - 1, 0, (2,))
            dve.wait_ge(s_used, p.base + FFN_ITEMS)
            for b in range(4):
                s = slice(2 * b, 2 * b + 2)
                dve.scalar_tensor_tensor(out=x[:, s, :], in0=pair[b], scalar=0.5, in1=x[:, s, :],
                                         op0=ALU.mult, op1=ALU.add).then_inc(s_x, 1)

        tail = shared + 73728
        kT = put("dn_kT", [HEADS, T], at=shared)
        qT = put("dn_qT", [HEADS, T], at=shared + 8192)
        vT = put("dn_vT", [HEADS, T], at=shared + 16384)
        zs = put("dn_z", [HEADS, T], at=shared + 24576)
        sq_ = put("sb_qT", [HEADS, T], at=shared + 32768)
        sk_ = put("sb_kT", [HEADS, T], at=shared + 40960)
        sv = put("sb_v", [NT, D], at=shared + 49152)
        gates = put("gates1", [2 * KC, T], at=shared + 57344)
        small_at = tail + 14336
        small = {}
        for i, name in enumerate(("beta", "y", "absy", "softp", "graw", "gcum", "gend", "egc", "dend", "nbeg",
                                  "alog_e")):
            small[name] = put("sm_" + name, [2, HEADS], at=small_at + 64 * i)
        ba = put("sm_ba", [NT, 16], at=small_at + 704)
        assert small_at + 832 <= nc.sbuf_usable_end - 256
        conv_in = [put(f"conv_in{r}", [2, T], at=tail + 2048 * r) for r in range(2)]
        conv_acc = [put(f"conv_acc{r}", [2, T], at=tail + 4096 + 2048 * r) for r in range(2)]
        hsq = [put(f"head_sq{r}", [2, T], at=tail + 2048 * r) for r in range(2)]
        hinv = [put(f"head_inv{r}", [2, T], at=tail + 4096 + 2048 * r) for r in range(2)]
        hroot = [put(f"head_root{r}", [2, T], at=tail + 8192 + 2048 * r) for r in range(2)]
        Ti = put("inv", [2, 4, P], at=xn_at)
        Ui = put("inv_t", [2, 4, P], at=xn_at + 4096)
        Xi = put("coupled", [2, 4, P], at=xn_at + 8192)
        Ms = put("level_part", [2, 4, P], at=xn_at + 12288)
        Mi = put("l_t", [2, 4, P], at=tail)
        De = put("decay", [2, 4, P], at=tail + 4096)
        At = put("attn_t", [2, 4, P], at=tail + 8192)
        egb = put("decay_rows", [4, P], at=tail + 12288)
        gt, bt = Xi, Ms
        vn0, st1, vn1, qd = Xi[:, 0], Xi[:, 1], Ms[:, 0], De[:, 0]
        osq = [put(f"o_sq{r}", [2, T], at=tail + 2048 * r) for r in range(2)]
        oroot = [put(f"o_root{r}", [2, T], at=tail + 4096 + 2048 * r) for r in range(2)]
        oinv = [put(f"o_inv{r}", [2, T], at=tail + 8192 + 2048 * r) for r in range(2)]
        oa_hi = put("oa_hi", [KC, T], F32R, at=shared)
        oa_lo = put("oa_lo", [KC, T], F32R, at=shared + 16384)
        lg = put("stick_log", [4, 384], at=xn_at)
        sp_ = put("stick_sp", [4, 384], at=xn_at + 6144)
        ob_hi = put("ob_hi", [KC, T], F32R, at=shared + 40960)
        ob_lo = put("ob_lo", [KC, T], F32R, at=shared + 32768)
        merged = put("merged1", [KC, T], at=shared + 24576)
        branch = [put(f"branch{r}", [2, T], at=tail + 2048 * r) for r in range(4)]

        s_read = sem("proj_read")
        s_conv = sem("conv_done")
        s_silu = sem("conv_silu")
        s_hsq = sem("head_squares")
        s_hss = sem("head_sums")
        s_hroot = sem("head_root")
        s_hnorm = sem("head_normed")
        s_sm_d = sem("gates_dve")
        s_sm_a = sem("gates_act")
        s_sm_p = sem("gates_pe")
        s_gbt = sem("rows_ready")
        s_gb = sem("rows_spread")
        s_kkq = sem("kk_kq")
        s_dm = sem("decay_logs")
        s_De = sem("decays")
        s_qd = sem("q_decayed")
        s_tu = sem("inverse_step")
        s_ms = sem("level_part_ready")
        s_xm = sem("coupled_product")
        s_xs = sem("coupled_copied")
        s_tum = sem("step_products")
        s_vt = sem("v_transposed")
        s_r = sem("rhs_ready")
        s_vn0m = sem("v_new_pe")
        s_vn0 = sem("v_new_act")
        s_r1 = sem("rhs1_ready")
        s_o = sem("o_product")
        s_oev = sem("o_copied")
        s_osq = sem("o_squares")
        s_oss = sem("o_sums")
        s_oroot = sem("o_root")
        s_oa = sem("oa_ready")
        s_oahi = sem("oa_upper")
        s_oalo = sem("oa_lower")
        s_z = sem("stick_scores")
        s_ln = sem("stick_logs")
        s_sp = sem("stick_softplus")
        s_R = sem("stick_sums")
        s_w = sem("stick_weights")
        s_pv = sem("stick_out")
        s_obhi = sem("ob_upper")
        s_oblo = sem("ob_lower")
        s_mg = sem("merged_ready")
        s_mhi = sem("merged_upper")
        s_mlo = sem("merged_lower")

        N1 = len(MIX1)

        def bc(ap, n):
            return ap.unsqueeze(2).to_broadcast([P, ap.shape[1], n])

        def over(ap, n):
            return ap.unsqueeze(1).to_broadcast([P, n, ap.shape[1]])

        def bring_phase(sp, p, parts):
            for j, (kind, arg) in enumerate(p.items):
                split = p.base if j == 0 else (p.base + (j - 2) if j >= RING else None)
                for dst, src in parts(kind, arg, raw[j % RING]):
                    bring(sp, j % RING, dst, src, split)
                    split = None

        def mixer1_sp(sp, pm, po, l):
            def proj(kind, at, slot):
                n = 16 if kind == "ba" else 256
                return [(slot_view(slot, KC, n), cols(a["w_in"][l], at, n))]

            def way_out(kind, at, slot):
                w = {"a": "w_branch_a", "b": "w_branch_b", "out": "w_out"}[kind]
                return [(slot_view(slot, KC, 256), cols(a[w][l], at))]
            bring_phase(sp, pm, proj)
            bring_phase(sp, po, way_out)

        def proj_out(kind, j):
            first = [k for k, _ in MIX1].index(kind)
            i = j - first
            s = slice(2 * i, 2 * i + 2)
            if kind == "sbv":
                return sv[:, :, 256 * i:256 * i + 256]
            return {"k": kT, "q": qT, "v": vT, "z": zs, "sbq": sq_, "sbk": sk_, "gate": gates}[kind][:, s, :]

        def head_pair(n):
            return (kT[:, n, :], qT[:, n, :]) if n < HEADS else (sk_[:, n - HEADS, :], sq_[:, n - HEADS, :])

        STEP0 = 14

        def mixer1_proj_pe(pe, pm, q, l):
            norm_pe(pe, q)
            pe.wait_ge(s_xlo, q * 2 + 2)

            def item(j, slot, kind="feature", first=False):
                if not first:
                    pe.wait_ge(s_read, l * N1 + (j - 2))
                pe.wait_ge(s_lo, pm.base + (j + 1 + LO_START))
                if kind == "ba":
                    mm = tokens(pe, slot, pair[slot], xn_hi, xn_lo, n=16)
                elif kind == "sbv":
                    mm = tokens(pe, slot, pair[slot], xn_hi, xn_lo)
                else:
                    mm = features(pe, slot, pair[slot], xn_hi, xn_lo)
                mm.then_inc(s_used, 1)

            def sums(n):
                pe.wait_ge(s_hsq, l * 16 + (n + 1))
                pe.matmul(bank[4 + n % 2][:, :], ones, hsq[n % 2][:, :, :], start=True,
                          stop=True).then_inc(s_hss, 1)
            for j in range(3):
                item(j, j, first=True)
            with pe.Fori(3, 12, 3) as j:
                for i in range(3):
                    item(j + i, i)
            for j in range(12, N1):
                item(j, j % RING, MIX1[j][0])
                if 0 <= j - 1 - STEP0 < 16:
                    sums(j - 1 - STEP0)

        def mixer1_proj_act(act, pm, q, l):
            def hi(j):
                split_hi(act, pm, j, j % RING, pm.loaded(j), free=j >= RING)
            norm_act(act, q, (lambda: hi(0), lambda: (hi(1), hi(2))))

            def silu(j):
                act.wait_ge(s_conv, l * 12 + (j + 1))
                act.activation(proj_out(MIX1[j][0], j), conv_acc[j % 2][:, :, :], ACT.Silu).then_inc(s_silu, 1)
            for j, (kind, _) in enumerate(MIX1):
                act.wait_ge(s_used, pm.base + (j + 1))
                b = pair[j % RING]
                if kind in "kqv":
                    act.activation(conv_in[j % 2][:, :, :], b, ACT.Copy).then_inc(s_read, 1)
                elif kind == "ba":
                    act.activation(ba[:, :, :], b[:, :, 0:16], ACT.Copy).then_inc(s_read, 1)
                else:
                    act.activation(proj_out(kind, j), b, ACT.Silu if kind == "z" else ACT.Copy).then_inc(s_read, 1)
                if 1 <= j <= 12:
                    silu(j - 1)
                n = j - STEP0 - 2
                if 0 <= n < 16:
                    act.wait_ge(s_hss, l * 16 + (n + 1))
                    if n >= 2:
                        act.wait_ge(s_hnorm, l * 16 + (n - 1))
                    if n < HEADS:
                        act.activation(hroot[n % 2][:, :, :], pair[4 + n % 2], ACT.Sqrt,
                                       bias=eps_col[:, 0:1]).then_inc(s_hroot, 1)
                    else:
                        act.activation(hroot[n % 2][:, 0, :], pair[4 + n % 2][:, 0, :], ACT.Sqrt,
                                       bias=eps_col[:, 0:1], scale=1.0 / P)
                        act.activation(hroot[n % 2][:, 1, :], pair[4 + n % 2][:, 1, :], ACT.Sqrt,
                                       bias=eps_col[:, 1:2]).then_inc(s_hroot, 1)
                n = j - STEP0
                if 0 <= n < 16:
                    act.drain()
                    if n == 0:
                        act.wait_ge(s_conv, l * 12 + 12)
                    for i, t in enumerate(head_pair(n)):
                        ins = act.activation(hsq[n % 2][:, i, :], t, ACT.Square)
                    ins.then_inc(s_hsq, 1)
                if j + 3 < N1:
                    hi(j + 3)

        def mixer1_proj_dve(dve, pm, q, l):
            norm_dve(dve, q, V_MIX, lambda: split_lo(dve, pm, 0, 0))
            split_lo(dve, pm, 1, 1)
            split_lo(dve, pm, 2, 2)
            for j, (kind, _) in enumerate(MIX1):
                if kind in "kqv":
                    tile0 = {"q": 0, "k": 8, "v": 16}[kind] + 2 * (j % 4)
                    src, acc = conv_in[j % 2], conv_acc[j % 2]
                    dve.wait_ge(s_read, l * N1 + (j + 1))
                    if j >= 2:
                        dve.wait_ge(s_silu, l * 12 + (j - 1))
                    for back in range(4):
                        for c in range(2):
                            col = V_CONV + 24 * (3 - back) + tile0 + c
                            w = vec[:, col:col + 1]
                            if back == 0:
                                ins = dve.tensor_scalar(acc[:, c, :], src[:, c, :], w, None, ALU.mult)
                            else:
                                ins = dve.scalar_tensor_tensor(
                                    out=acc[:, c, back:T], in0=src[:, c, 0:T - back], scalar=w,
                                    in1=acc[:, c, back:T], op0=ALU.mult, op1=ALU.add)
                        if back < 3:
                            dve.drain()
                    ins.then_inc(s_conv, 1)
                n = j - STEP0 - 2
                if 0 <= n < 16:
                    k, qq = head_pair(n)
                    dve.wait_ge(s_hroot, l * 16 + (n + 1))
                    dve.reciprocal(hinv[n % 2][:, :, :], hroot[n % 2][:, :, :])
                    dve.drain()
                    if n < HEADS:
                        dve.tensor_tensor(k, k, hinv[n % 2][:, 0, :], ALU.mult)
                        dve.scalar_tensor_tensor(out=qq, in0=qq, scalar=float(P) ** -0.5,
                                                 in1=hinv[n % 2][:, 1, :], op0=ALU.mult,
                                                 op1=ALU.mult).then_inc(s_hnorm, 1)
                    else:
                        dve.scalar_tensor_tensor(out=k, in0=k, scalar=vec[:, V_SBK:V_SBK + 1],
                                                 in1=hinv[n % 2][:, 0, :], op0=ALU.mult, op1=ALU.mult)
                        dve.scalar_tensor_tensor(out=qq, in0=qq, scalar=vec[:, V_SBQ:V_SBQ + 1],
                                                 in1=hinv[n % 2][:, 1, :], op0=ALU.mult,
                                                 op1=ALU.mult).then_inc(s_hnorm, 1)
                if j + 3 < N1:
                    split_lo(dve, pm, j + 3, (j + 3) % RING)

        def delta_gates_act(act, l):
            act.drain()
            act.activation(small["beta"][:, :, :], ba[:, :, 0:HEADS], ACT.Sigmoid)
            act.wait_ge(s_sm_d, l * 3 + 1)
            act.activation(small["absy"][:, :, :], small["y"][:, :, :], ACT.Abs)
            act.activation(small["alog_e"][:, 0:1, :], dta[:, ds(l, 1), 1, :], ACT.Exp)
            act.drain()
            act.activation(small["softp"][:, :, :], small["absy"][:, :, :], ACT.Exp, scale=-1.0)
            act.drain()
            act.activation(small["absy"][:, :, :], small["softp"][:, :, :], ACT.Ln,
                           bias=eps_col[:, 2:3]).then_inc(s_sm_a, 1)
            act.wait_ge(s_sm_d, l * 3 + 3)
            act.activation(small["egc"][:, :, :], small["gcum"][:, :, :], ACT.Exp)
            act.activation(small["dend"][:, :, :], small["gend"][:, :, :], ACT.Exp).then_inc(s_sm_a, 1)

        def delta_gates_dve(dve, l):
            dve.wait_ge(s_read, l * N1 + 13)
            dve.tensor_tensor(small["y"][:, :, :], ba[:, :, HEADS:2 * HEADS],
                              dta[:, ds(l, 1), 0, :].to_broadcast([P, 2, HEADS]), ALU.add).then_inc(s_sm_d, 1)
            dve.wait_ge(s_sm_a, l * 2 + 1)
            dve.scalar_tensor_tensor(out=small["softp"][:, :, :], in0=small["y"][:, :, :], scalar=0.0,
                                     in1=small["absy"][:, :, :], op0=ALU.max, op1=ALU.add)
            dve.drain()
            dve.scalar_tensor_tensor(out=small["graw"][:, :, :], in0=small["softp"][:, :, :], scalar=-1.0,
                                     in1=small["alog_e"][:, 0:1, :].to_broadcast([P, 2, HEADS]),
                                     op0=ALU.mult, op1=ALU.mult).then_inc(s_sm_d, 1)
            dve.wait_ge(s_sm_p, l + 1)
            dve.tensor_copy(small["gcum"][:, :, :], bank[6][:, 0:16].rearrange("p (c h) -> p c h", c=2))
            dve.drain()
            dve.tensor_tensor(small["gend"][:, :, :], bank[6][:, 16:32].rearrange("p (c h) -> p c h", c=2),
                              small["gcum"][:, :, :], ALU.subtract).then_inc(s_sm_d, 1)
            dve.wait_ge(s_sm_a, l * 2 + 2)
            dve.scalar_tensor_tensor(out=small["nbeg"][:, :, :], in0=small["egc"][:, :, :], scalar=-1.0,
                                     in1=small["beta"][:, :, :], op0=ALU.mult, op1=ALU.mult)

        def delta_gates_pe(pe, l):
            pe.wait_ge(s_sm_d, l * 3 + 2)
            g = small["graw"][:, :, :]
            pe.matmul(bank[6][:, 0:16], C["triu"], g, start=True, stop=True)
            pe.matmul(bank[6][:, 16:32], ones, g, start=True, stop=True).then_inc(s_sm_p, 1)

        def tok(c):
            return slice(P * c, P * c + P)

        def heads4(G):
            return slice(4 * G, 4 * G + 4)

        def delta_pe(pe, l, G):
            g = l * 2 + G
            b4 = [b[:, :].rearrange("p (h n) -> p h n", h=4) for b in bank]
            if G:
                pe.wait_ge(s_oev, g)
            else:
                pe.wait_ge(s_read, l * N1 + N1)
                pe.wait_ge(s_hnorm, l * 16 + HEADS)
            for c in range(2):
                pe.wait_ge(s_gbt, g * 2 + (c + 1))
                pe.matmul(bank[c][:, :], ones, gt[:, c], start=True, stop=True)
                pe.matmul(bank[2 + c][:, :], ones, bt[:, c], start=True, stop=True).then_inc(s_gb, 1)
            for c in range(2):
                for h in range(4):
                    kc = kT[:, 4 * G + h, tok(c)]
                    o = bank[4 + 2 * c + h // 2][:, :].rearrange("p (h a n) -> p h a n", h=2, a=2)[:, h % 2]
                    pe.matmul(o[:, 0, :], kc, kc, start=True, stop=True)
                    mm = pe.matmul(o[:, 1, :], kc, qT[:, 4 * G + h, tok(c)], start=True, stop=True)
                mm.then_inc(s_kkq, 1)
            pe.wait_ge(s_tu, g * 16 + 2)
            for c in range(2):
                for h in range(4):
                    mm = pe.transpose(b4[6 + c][:, h, :], vT[:, 4 * G + h, tok(c)], ident)
                mm.then_inc(s_vt, 1)

            def level(s):
                for c in range(2):
                    pe.wait_ge(s_ms, g * 14 + (s * 2 + (c + 1)))
                    pe.wait_ge(s_tu, g * 16 + (s * 2 + (c + 1)))
                    for h in range(4):
                        mm = pe.matmul(b4[c][:, h, :], Ms[:, c, h, :], Ti[:, c, h, :], start=True, stop=True)
                    mm.then_inc(s_xm, 1)
                for c in range(2):
                    pe.wait_ge(s_xs, g * 14 + (s * 2 + (c + 1)))
                    for h in range(4):
                        pe.matmul(b4[2 + c][:, h, :], Ui[:, c, h, :], Xi[:, c, h, :], start=True, stop=True)
                        mm = pe.matmul(b4[4 + c][:, h, :], Xi[:, c, h, :], Ui[:, c, h, :], start=True, stop=True)
                    mm.then_inc(s_tum, 1)
            with pe.Fori(0, 7, 1) as s:
                level(s)
            pe.wait_ge(s_r, g * 3 + 1)
            for h in range(4):
                mm = pe.transpose(b4[6][:, h, :], kT[:, 4 * G + h, tok(0)], ident)
            mm.then_inc(s_vt, 1)
            pe.wait_ge(s_tu, g * 16 + 16)
            for h in range(4):
                mm = pe.matmul(b4[0][:, h, :], Ui[:, 0, h, :], vT[:, 4 * G + h, tok(0)], start=True, stop=True)
            mm.then_inc(s_vn0m, 1)
            pe.wait_ge(s_r, g * 3 + 3)
            pe.wait_ge(s_vn0, g * 3 + 1)
            for h in range(4):
                mm = pe.matmul(b4[1][:, h, :], kT[:, 4 * G + h, tok(0)], vn0[:, h, :], start=True, stop=True)
            mm.then_inc(s_vn0m, 1)
            pe.wait_ge(s_vn0, g * 3 + 2)
            for h in range(4):
                mm = pe.matmul(b4[2][:, h, :], kT[:, 4 * G + h, tok(1)], st1[:, h, :], start=True, stop=True)
            mm.then_inc(s_vn0m, 1)
            pe.wait_ge(s_r1, g + 1)
            for h in range(4):
                mm = pe.matmul(b4[3][:, h, :], Ui[:, 1, h, :], vT[:, 4 * G + h, tok(1)], start=True, stop=True)
            mm.then_inc(s_vn0m, 1)
            pe.wait_ge(s_qd, g + 1)
            for h in range(4):
                pe.matmul(b4[4][:, h, :], vn0[:, h, :], At[:, 0, h, :], start=True, stop=True)
            pe.wait_ge(s_vn0, g * 3 + 3)
            for h in range(4):
                pe.matmul(b4[5][:, h, :], st1[:, h, :], qd[:, h, :], start=True, stop=False)
                mm = pe.matmul(b4[5][:, h, :], vn1[:, h, :], At[:, 1, h, :], start=False, stop=True)
            mm.then_inc(s_o, 1)

        def delta_act(act, l, G):
            g = l * 2 + G
            b4 = [b[:, :].rearrange("p (h n) -> p h n", h=4) for b in bank]
            act.wait_ge(s_dm, g * 2 + 1)
            act.activation(De[:, 0], De[:, 0], ACT.Exp).then_inc(s_De, 1)
            act.wait_ge(s_dm, g * 2 + 2)
            act.activation(egb[:, :, :], b4[1], ACT.Exp)
            act.activation(De[:, 1], De[:, 1], ACT.Exp).then_inc(s_De, 1)
            with act.Fori(0, 7, 1) as s:
                for c in range(2):
                    act.wait_ge(s_xm, g * 14 + (s * 2 + (c + 1)))
                    act.activation(Xi[:, c], b4[c], ACT.Copy).then_inc(s_xs, 1)
            act.wait_ge(s_vn0m, g * 4 + 1)
            act.activation(vn0, b4[0], ACT.Copy).then_inc(s_vn0, 1)
            act.wait_ge(s_vn0m, g * 4 + 2)
            act.activation(st1, b4[1], ACT.Copy).then_inc(s_vn0, 1)
            act.wait_ge(s_vn0m, g * 4 + 4)
            act.activation(vn1, b4[3], ACT.Copy).then_inc(s_vn0, 1)
            act.wait_ge(s_o, g + 1)
            act.activation(qT[:, heads4(G), tok(0)], b4[4], ACT.Copy)
            act.activation(qT[:, heads4(G), tok(1)], b4[5], ACT.Copy).then_inc(s_oev, 1)

        def delta_dve(dve, l, G):
            g = l * 2 + G
            b4 = [b[:, :].rearrange("p (h n) -> p h n", h=4) for b in bank]
            if G:
                dve.wait_ge(s_o, g)
            for c in range(2):
                dve.tensor_tensor(gt[:, c], over(C["triu"], 4), bc(small["graw"][:, c, heads4(G)], P), ALU.mult)
                dve.tensor_tensor(bt[:, c], over(ident, 4), bc(small["beta"][:, c, heads4(G)], P),
                                  ALU.mult).then_inc(s_gbt, 1)
            for c in range(2):
                dve.wait_ge(s_gb, g * 2 + (c + 1))
                for h in range(4):
                    ins = dve.scalar_tensor_tensor(
                        out=De[:, c, h, :], in0=b4[c][:, h, :],
                        scalar=small["gcum"][:, c, 4 * G + h:4 * G + h + 1], in1=C["decay_mask"],
                        op0=ALU.subtract, op1=ALU.add)
                ins.then_inc(s_dm, 1)
            for c in range(2):
                dve.wait_ge(s_De, g * 2 + (c + 1))
                dve.wait_ge(s_kkq, g * 2 + (c + 1))
                for h in (0, 2):
                    o = bank[4 + 2 * c + h // 2][:, :].rearrange("p (h a n) -> p h a n", h=2, a=2)
                    dve.tensor_tensor(Mi[:, c, h:h + 2, :], o[:, :, 0, :], De[:, c, h:h + 2, :], ALU.mult)
                    dve.tensor_tensor(At[:, c, h:h + 2, :], o[:, :, 1, :], De[:, c, h:h + 2, :], ALU.mult)
                dve.drain()
                dve.tensor_tensor(Mi[:, c], Mi[:, c], b4[2 + c], ALU.mult)
                dve.tensor_copy(Ti[:, c], over(ident, 4))
                dve.tensor_copy(Ui[:, c], over(ident, 4)).then_inc(s_tu, 1)
            for c in range(2):
                dve.wait_ge(s_vt, g * 3 + (c + 1))
                dve.tensor_tensor(vT[:, heads4(G), tok(c)], b4[6 + c], bc(small["beta"][:, c, heads4(G)], P),
                                  ALU.mult).then_inc(s_r, 1)
            with dve.Fori(0, 7, 1) as s:
                for c in range(2):
                    dve.wait_ge(s_tum, g * 14 + (s * 2 + (c + 1)))
                    dve.tensor_tensor(Ti[:, c], Ti[:, c], b4[2 + c], ALU.subtract)
                    dve.tensor_tensor(Ui[:, c], Ui[:, c], b4[4 + c], ALU.subtract).then_inc(s_tu, 1)
            dve.wait_ge(s_vt, g * 3 + 3)
            dve.tensor_tensor(kT[:, heads4(G), tok(0)], b4[6], bc(small["dend"][:, 0, heads4(G)], P),
                              ALU.mult).then_inc(s_r, 1)
            dve.wait_ge(s_vn0m, g * 4 + 3)
            for h in range(4):
                r1 = vT[:, 4 * G + h, tok(1)]
                ins = dve.scalar_tensor_tensor(out=r1, in0=b4[2][:, h, :],
                                               scalar=small["nbeg"][:, 1, 4 * G + h:4 * G + h + 1], in1=r1,
                                               op0=ALU.mult, op1=ALU.add)
            ins.then_inc(s_r1, 1)

        def delta_pool(pool, l, G):
            g = l * 2 + G
            pool.wait_ge(s_tu, g * 16 + 2)
            pool.tensor_tensor(qd, qT[:, heads4(G), tok(1)], egb[:, :, :], ALU.mult).then_inc(s_qd, 1)
            for s in range(7):
                for c in range(2):
                    if s:
                        pool.wait_ge(s_xm, g * 14 + (s * 2 + (c - 1)))
                    pool.tensor_tensor(Ms[:, c], Mi[:, c], over(C[f"level{s}"], 4), ALU.mult).then_inc(s_ms, 1)

        def onorm_pe(pe, l):
            for i in range(4):
                pe.wait_ge(s_osq, l * 4 + (i + 1))
                pe.matmul(bank[6 + i % 2][:, :], ones, osq[i % 2][:, :, :], start=True, stop=True).then_inc(s_oss, 1)

        def onorm_act(act, l):
            def square(i):
                act.activation(osq[i % 2][:, :, :], qT[:, 2 * i:2 * i + 2, :], ACT.Square).then_inc(s_osq, 1)
            act.drain()
            act.wait_ge(s_o, l * 2 + 2)
            square(0)
            square(1)
            for i in range(4):
                act.wait_ge(s_oss, l * 4 + (i + 1))
                if i >= 2:
                    act.wait_ge(s_oa, l * 4 + (i - 1))
                act.activation(oroot[i % 2][:, :, :], pair[6 + i % 2], ACT.Sqrt, bias=eps_col[:, 0:1],
                               scale=1.0 / P).then_inc(s_oroot, 1)
                if i < 2:
                    square(i + 2)
            for i in range(4):
                act.wait_ge(s_oa, l * 4 + (i + 1))
                act.activation(oa_hi[:, 2 * i:2 * i + 2, :], zs[:, 2 * i:2 * i + 2, :], ACT.Copy).then_inc(s_oahi, 1)

        def onorm_dve(dve, l):
            for i in range(4):
                dve.wait_ge(s_oroot, l * 4 + (i + 1))
                s = slice(2 * i, 2 * i + 2)
                dve.reciprocal(oinv[i % 2][:, :, :], oroot[i % 2][:, :, :])
                dve.drain()
                dve.tensor_tensor(oinv[i % 2][:, :, :], qT[:, s, :], oinv[i % 2][:, :, :], ALU.mult)
                dve.drain()
                dve.scalar_tensor_tensor(out=zs[:, s, :], in0=oinv[i % 2][:, :, :], scalar=vec[:, V_DN_OUT:V_DN_OUT + 1],
                                         in1=zs[:, s, :], op0=ALU.mult, op1=ALU.mult).then_inc(s_oa, 1)
            for i in range(4):
                s = slice(2 * i, 2 * i + 2)
                dve.wait_ge(s_oahi, l * 4 + (i + 1))
                dve.tensor_tensor(oa_lo[:, s, :], zs[:, s, :], oa_hi[:, s, :].bitcast(F32),
                                  ALU.subtract).then_inc(s_oalo, 1)

        def stick_pe(pe, l):
            pe.wait_ge(s_hnorm, l * 16 + 16)
            for r in range(2):
                if r:
                    pe.wait_ge(s_w, l * 8 + 4)
                for i in range(4):
                    h = 4 * r + i
                    pe.matmul(bank[i][:, 0:256], sk_[:, h, 0:P], sq_[:, h, :], start=True, stop=False,
                              skip_group_check=True)
                    pe.matmul(bank[i][:, 256:384], sk_[:, h, P:T], sq_[:, h, P:T], start=False, stop=False,
                              skip_group_check=True).then_inc(s_z, 1)
                for i in range(4):
                    pe.wait_ge(s_sp, l * 8 + (4 * r + i + 1))
                    for out, m, src in ((slice(0, 256), "neg_tri", sp_[:, i, 0:256]),
                                        (slice(128, 256), "neg_ones", sp_[:, i, 256:384]),
                                        (slice(256, 384), "neg_tri", sp_[:, i, 256:384]),
                                        (slice(0, 384), "ident", C["sb_neg"])):
                        mm = pe.matmul(bank[i][:, out], C[m], src, start=False, stop=(m == "ident"),
                                       skip_group_check=True)
                    mm.then_inc(s_R, 1)
                for i in range(4):
                    h = 4 * r + i
                    pe.wait_ge(s_w, l * 8 + (h + 1))
                    if r:
                        pe.wait_ge(s_oblo, l * 8 + (i + 1))
                    v = sv[:, :, P * h:P * h + P]
                    pe.matmul(bank[4 + i][:, 0:256], v[:, 0, :], lg[:, i, 0:256], start=True, stop=False,
                              skip_group_check=True)
                    pe.matmul(bank[4 + i][:, 128:256], v[:, 1, :], lg[:, i, 256:384], start=False, stop=True,
                              skip_group_check=True).then_inc(s_pv, 1)

        def stick_act(act, l):
            for r in range(2):
                for i in range(4):
                    act.wait_ge(s_z, l * 8 + (4 * r + i + 1))
                    if r:
                        act.wait_ge(s_pv, l * 8 + (i + 1))
                    act.activation(lg[:, i, :], bank[i][:, 0:384], ACT.Abs)
                act.drain()
                act.activation(lg[:, :, :], lg[:, :, :], ACT.Exp, scale=-1.0)
                act.drain()
                act.activation(lg[:, :, :], lg[:, :, :], ACT.Ln, bias=eps_col[:, 2:3]).then_inc(s_ln, 1)
                for i in range(4):
                    act.wait_ge(s_R, l * 8 + (4 * r + i + 1))
                    act.activation(lg[:, i, :], bank[i][:, 0:384], ACT.Exp).then_inc(s_w, 1)
                for i in range(4):
                    act.wait_ge(s_pv, l * 8 + (4 * r + i + 1))
                    act.activation(ob_hi[:, 4 * r + i, :], bank[4 + i][:, 0:256], ACT.Copy).then_inc(s_obhi, 1)

        def stick_dve(dve, l):
            for r in range(2):
                dve.wait_ge(s_ln, l * 2 + (r + 1))
                for i in range(4):
                    if r:
                        dve.wait_ge(s_R, l * 8 + 4)
                    dve.scalar_tensor_tensor(out=sp_[:, i, :], in0=bank[i][:, 0:384], scalar=0.0,
                                             in1=lg[:, i, :], op0=ALU.max, op1=ALU.add)
                dve.drain()
                for i in range(4):
                    dve.tensor_tensor(sp_[:, i, :], sp_[:, i, :], C["sb_mask"], ALU.mult).then_inc(s_sp, 1)
                for i in range(4):
                    h = 4 * r + i
                    dve.wait_ge(s_obhi, l * 8 + (h + 1))
                    dve.tensor_tensor(ob_lo[:, h, :], bank[4 + i][:, 0:256], ob_hi[:, h, :].bitcast(F32),
                                      ALU.subtract).then_inc(s_oblo, 1)

        def out1_pe(pe, po, l):
            pe.wait_ge(s_oalo, l * 4 + 4)
            pe.wait_ge(s_oblo, l * 8 + 8)
            for j in range(8):
                i = j // 2
                pe.wait_ge(s_lo, po.base + (j + 1 + LO_START))
                if i >= 2:
                    pe.wait_ge(s_mg, l * 4 + (i - 1))
                hi, lo = (ob_hi, ob_lo) if j % 2 else (oa_hi, oa_lo)
                features(pe, j % RING, pair[j % 4], hi, lo).then_inc(s_used, 1)
            pe.wait_ge(s_mlo, l * 4 + 4)
            for j in range(8, 12):
                pe.wait_ge(s_lo, po.base + (j + 1 + LO_START))
                features(pe, j % RING, pair[j - 4], xn_hi, xn_lo).then_inc(s_used, 1)

        def out1_act(act, po, l):
            for j in range(12):
                if j + 3 < 12:
                    split_hi(act, po, j + 3, j % RING, po.loaded(j + 3))
                if j % 2 and j < 8:
                    i = j // 2
                    act.wait_ge(s_mg, l * 4 + (i + 1))
                    act.activation(xn_hi[:, 2 * i:2 * i + 2, :], merged[:, 2 * i:2 * i + 2, :],
                                   ACT.Copy).then_inc(s_mhi, 1)
            act.wait_ge(s_used, po.base + 12)

        def out1_dve(dve, po, l):
            for j in range(12):
                if j % 2 and j < 8:
                    i = j // 2
                    s = slice(2 * i, 2 * i + 2)
                    ta, tb = branch[2 * (i % 2)], branch[2 * (i % 2) + 1]
                    dve.wait_ge(s_used, po.base + (j + 1))
                    dve.tensor_tensor(ta[:, :, :], pair[(j - 1) % 4], gates[:, s, :], ALU.mult)
                    dve.tensor_tensor(tb[:, :, :], pair[j % 4], gates[:, 8 + 2 * i:10 + 2 * i, :], ALU.mult)
                    dve.drain()
                    dve.tensor_tensor(merged[:, s, :], ta[:, :, :], tb[:, :, :], ALU.add).then_inc(s_mg, 1)
                if j + 3 < 12:
                    split_lo(dve, po, j + 3, j % RING)
                if j % 2 and j < 8:
                    dve.wait_ge(s_mhi, l * 4 + (i + 1))
                    dve.tensor_tensor(xn_lo[:, s, :], merged[:, s, :], xn_hi[:, s, :].bitcast(F32),
                                      ALU.subtract).then_inc(s_mlo, 1)
            for i in range(4):
                s = slice(2 * i, 2 * i + 2)
                dve.wait_ge(s_used, po.base + (9 + i))
                dve.tensor_tensor(x[:, s, :], pair[4 + i], x[:, s, :], ALU.add).then_inc(s_x, 1)

        def mixer1_pe(pe, pm, po, q, l):
            mixer1_proj_pe(pe, pm, q, l)
            delta_gates_pe(pe, l)
            for G in range(2):
                delta_pe(pe, l, G)
            onorm_pe(pe, l)
            stick_pe(pe, l)
            out1_pe(pe, po, l)

        def mixer1_act(act, pm, po, q, l):
            mixer1_proj_act(act, pm, q, l)
            delta_gates_act(act, l)
            for G in range(2):
                delta_act(act, l, G)
                if G == 0:
                    for i in range(2):
                        gate = gates[:, KC * i:KC * i + KC, :]
                        act.activation(gate, gate, ACT.Sigmoid)
                    act.wait_ge(s_used, pm.base + N1)
                    for j in range(3):
                        split_hi(act, po, j, j, po.loaded(j), free=False)
            onorm_act(act, l)
            stick_act(act, l)
            out1_act(act, po, l)

        def mixer1_dve(dve, pm, po, q, l):
            mixer1_proj_dve(dve, pm, q, l)
            delta_gates_dve(dve, l)
            for G in range(2):
                delta_dve(dve, l, G)
                if G == 0:
                    for j in range(3):
                        split_lo(dve, po, j, j)
            onorm_dve(dve, l)
            stick_dve(dve, l)
            out1_dve(dve, po, l)

        def mixer1_pool(pool, l):
            for G in range(2):
                delta_pool(pool, l, G)

        mixer_sp, mixer_pe, mixer_act, mixer_dve = [mixer1_sp], [mixer1_pe], [mixer1_act], [mixer1_dve]

        slopes = [2.0 ** (-8.0 * (i + 1) / 18) for i in range(18)]
        gates2 = put("gates2", [3 * KC, T], at=shared)
        v2 = put("values2", [NT, 24 * 64], at=shared + 24576)
        mob = put("moba_qk", [6, T], at=shared + 36864)
        dil = put("dil_qk", [12, T], at=shared + 43008)
        qm = put("mla_q", [6, T], at=shared + 55296)
        km = put("mla_k", [6, T], at=shared + 61440)
        o_mob = [put(f"o_mob{i}", [3, T], F32R, at=shared + 67584 + 3072 * i) for i in range(2)]
        o_mla = [put(f"o_mla{i}", [3, T], F32R, at=shared + 73728 + 3072 * i) for i in range(2)]
        o_dil = [put(f"o_dil{i}", [2, T], F32R, at=shared + 36864 + 2048 * i) for i in range(2)]
        turned = put("turned", [2, T], at=shared + 40960)
        S = put("scores", [3, 384], at=shared + 79872)
        PT = put("probs_t", [3, 384], at=shared + 84480)
        kr = put("mla_k_rope", [T], at=shared + 89088)
        stat_at = shared + 90112
        nmax = put("neg_max", [2], at=stat_at)
        den = put("denominator", [2], at=stat_at + 64)
        rden = put("reciprocal", [2], at=stat_at + 128)
        latent = put("latent", [3, T], at=shared + 55296)
        lsq = put("latent_sq", [3, T], at=shared + 58368)
        lroot = put("latent_root", [2, T], at=shared + 61440)
        linv = put("latent_inv", [2, T], at=shared + 63488)
        c_hi = put("latent_hi", [3, T], F32R, at=shared + 73728)
        c_lo = put("latent_lo", [3, T], F32R, at=shared + 76800)
        merged2 = put("merged2", [KC, T], at=shared + 43008)
        part = [put(f"part{i}", [2, T], at=shared + 55296 + 2048 * i) for i in range(6)]

        s2_read = sem("proj2_read")
        s_lsq = sem("latent_squares")
        s_lss = sem("latent_sums")
        s_lroot = sem("latent_root")
        s_lat = sem("latent_normed")
        s_lhi = sem("latent_upper")
        s_llo = sem("latent_lower")
        s_up = sem("up_products")
        s_upr = sem("up_read")
        s_turn = sem("turned_pe")
        s_rope = sem("rope_done")
        s_A = sem("unit_scores")
        s_B = sem("unit_max")
        s_C = sem("unit_exp")
        s_D = sem("unit_probs")
        s_E = sem("unit_transposed")
        s_F = sem("unit_copied")
        s_G = sem("unit_out")
        s_H = sem("unit_out_hi")
        s_L = sem("unit_out_lo")
        s2_mg = sem("merged2_ready")
        s2_mhi = sem("merged2_upper")
        s2_mlo = sem("merged2_lower")
        N2 = len(MIX2)
        UP = 16

        def unit_plan():
            units = []
            for h in range(6):
                lo = 64 * (h % 2)
                units.append((8 + h, [(mob[lo:lo + 64, h // 2, :], mob[lo:lo + 64, 3 + h // 2, :], 384 + 64 * h,
                                       "all", slopes[12 + h])], o_mob, h // 2))
            for h in range(6):
                units.append((UP + 2 + h, [(qm[0:96, h, :], km[0:96, h, :], 64 * h, "causal", 1.0)], o_mla, h // 2))
            for i in range(4):
                heads = []
                for g, table in enumerate(("window", "step4", "step16")):
                    h = 4 * g + i
                    lo = 64 * (h % 2)
                    heads.append((dil[lo:lo + 64, h // 2, :], dil[lo:lo + 64, 6 + h // 2, :], 768 + 64 * h, table,
                                  slopes[h]))
                units.append((UP + 8 + i, heads, o_dil, i // 2))
            return units
        units = unit_plan()

        def unit_at(j):
            return [n for n, u in enumerate(units) if u[0] == j]

        def mixer2_sp(sp, pm, po, l):
            def proj(kind, at, slot):
                if kind == "up":
                    return [(slot_view(slot, 2, 576), rows(a["w_uq_2"][l])),
                            (slot[:, 1152:1920], a["w_ukv_2"][l])]
                n = 128 if kind == "mv2" else 256
                return [(slot_view(slot, KC, n), cols(a["w_in_2"][l], at, n))]

            def way_out(kind, at, slot):
                v = slot_view(slot, KC, 256)
                if kind == "out":
                    return [(v, cols(a["w_out_2"][l], at))]
                return [(v[:, 0:3, :], cols(a["w_br_mla_2"][l], at)), (v[:, 3:6, :], cols(a["w_br_moba_2"][l], at)),
                        (v[:, 6:8, :], cols(a["w_br_dil_2"][l], at))]
            bring_phase(sp, pm, proj)
            bring_phase(sp, po, way_out)

        def scores_pe(pe, l, n):
            if n:
                pe.wait_ge(s_B, l * 16 + n)
            if n == 6:
                pe.wait_ge(s_rope, l * 4 + 4)
            for b, (q, k, _, _, _) in enumerate(units[n][1]):
                pe.matmul(bank[3 + b][:, 0:P], q[:, 0:P], k[:, 0:P], start=True, stop=True)
                mm = pe.matmul(bank[3 + b][:, P:384], q[:, P:T], k[:, 0:T], start=True, stop=True)
            mm.then_inc(s_A, 1)

        T_BANK = (6, 4, 5)

        def transposes_pe(pe, l, n):
            pe.wait_ge(s_D, l * 16 + (n + 1))
            for b in range(len(units[n][1])):
                for i in range(3):
                    mm = pe.transpose(bank[T_BANK[b]][:, P * i:P * i + P], S[:, b, P * i:P * i + P], ident)
            mm.then_inc(s_E, 1)

        def values_pe(pe, l, n):
            _, heads, _, _ = units[n]
            lo = 64 * (n % 2)
            if n >= 2 and n % 2 == 0:
                pe.wait_ge(s_L, l * 8 + n // 2)
            pe.wait_ge(s_F, l * 16 + (n + 1))
            for b, (_, _, v, _, _) in enumerate(heads):
                last = b == len(heads) - 1
                pe.matmul(bank[7][lo:lo + 64, 0:T], v2[:, 0, v:v + 64], PT[:, b, 0:T], start=(b == 0), stop=False,
                          skip_group_check=True)
                mm = pe.matmul(bank[7][lo:lo + 64, P:T], v2[:, 1, v:v + 64], PT[:, b, T:384], start=False, stop=last,
                               skip_group_check=True)
            mm.then_inc(s_G, 1)

        def exp_act(act, l, n):
            k = len(units[n][1])
            act.wait_ge(s_B, l * 16 + (n + 1))
            act.activation(S[:, 0:k, 0:P], S[:, 0:k, 0:P], ACT.Exp, bias=nmax[:, 0:1], accum_out=den[:, 0:1])
            act.activation(S[:, 0:k, P:384], S[:, 0:k, P:384], ACT.Exp, bias=nmax[:, 1:2],
                           accum_out=den[:, 1:2]).then_inc(s_C, 1)

        def copy_act(act, l, n):
            act.wait_ge(s_E, l * 16 + (n + 1))
            for b in range(len(units[n][1])):
                ins = act.activation(PT[:, b, :], bank[T_BANK[b]][:, 0:384], ACT.Copy)
            ins.then_inc(s_F, 1)

        def out_hi_act(act, l, n):
            act.wait_ge(s_G, l * 16 + (n + 1))
            act.activation(units[n][2][0][:, units[n][3], :], bank[7][:, 0:T], ACT.Copy).then_inc(s_H, 1)

        def out_lo_dve(dve, l, n):
            hi, lo = units[n][2]
            i = units[n][3]
            dve.wait_ge(s_H, l * 8 + (n // 2 + 1))
            dve.tensor_tensor(lo[:, i, :], bank[7][:, 0:T], hi[:, i, :].bitcast(F32), ALU.subtract).then_inc(s_L, 1)

        def max_dve(dve, l, n):
            heads = units[n][1]
            k = len(heads)
            dve.wait_ge(s_A, l * 16 + (n + 1))
            for b, (_, _, _, table, slope) in enumerate(heads):
                dve.scalar_tensor_tensor(out=S[:, b, :], in0=C[table], scalar=float(slope), in1=bank[3 + b][:, 0:384],
                                         op0=ALU.mult, op1=ALU.add)
            dve.drain()
            axis = AX.X if k == 1 else AX.XY
            cut = (lambda s: S[:, 0, s]) if k == 1 else (lambda s: S[:, 0:k, s])
            dve.tensor_reduce(nmax[:, 0:1], cut(slice(0, P)), axis, ALU.max, negate=True)
            dve.tensor_reduce(nmax[:, 1:2], cut(slice(P, 384)), axis, ALU.max, negate=True).then_inc(s_B, 1)

        def probs_dve(dve, l, n):
            k = len(units[n][1])
            dve.wait_ge(s_C, l * 16 + (n + 1))
            dve.reciprocal(rden[:, :], den[:, :])
            dve.drain()
            dve.tensor_scalar(S[:, 0:k, 0:P], S[:, 0:k, 0:P], rden[:, 0:1], None, ALU.mult)
            dve.tensor_scalar(S[:, 0:k, P:384], S[:, 0:k, P:384], rden[:, 1:2], None, ALU.mult).then_inc(s_D, 1)

        def mixer2_pe(pe, pm, po, q, l):
            norm_pe(pe, q)
            pe.wait_ge(s_xlo, q * 2 + 2)
            for j, (kind, _) in enumerate(MIX2):
                slot = j % RING
                before, now = unit_at(j - 1), unit_at(j)
                pe.wait_ge(s_lo, pm.base + (j + 1 + LO_START))
                if kind == "up":
                    up_pe(pe, l)
                    continue
                if j >= RING:
                    done = sum(1 for i in range(j - 2) if i != UP)
                    pe.wait_ge(s2_read, l * (N2 - 1) + done)
                for half in range(2):
                    mm = project2(pe, kind, slot, half)
                    if half == 1:
                        mm.then_inc(s_used, 1)
                    for n in before:
                        (transposes_pe, values_pe)[half](pe, l, n)
                for n in now:
                    scores_pe(pe, l, n)
                if j == 3:
                    pe.wait_ge(s_lsq, l + 1)
                    pe.matmul(bank[7][:, 0:T], ones, lsq[:, 0, :], start=True, stop=False)
                    pe.matmul(bank[7][:, 0:T], ones, lsq[:, 1, :], start=False, stop=True)
                    pe.matmul(bank[7][:, T:2 * T], ones, lsq[:, 2, :], start=True, stop=True).then_inc(s_lss, 1)
                if j == UP + 1:
                    turn = C["turn"][0:96, :]
                    pe.wait_ge(s_upr, l * 8 + 8)
                    pe.matmul(bank[3][0:96, 0:T], turn, kr[0:96, :], start=True, stop=True).then_inc(s_turn, 1)
                    for i in range(3):
                        pe.matmul(bank[4 + i][0:96, :], turn, qm[0:96, 2 * i:2 * i + 2, :], start=True,
                                  stop=True).then_inc(s_turn, 1)
            out2_pe(pe, po, l)

        def project2(pe, kind, slot, half):
            n = 128 if kind == "mv2" else 256
            hi, lo = slot_view(w_hi[slot], KC, n), slot_view(w_lo[slot], KC, n)
            out = pair[slot][:, half, 0:n] if kind in ("mv", "mv2", "dv") else pair[slot][:, half, :]
            for kc in range(KC):
                if kind in ("mv", "mv2", "dv"):
                    tk = slice(P * half, P * half + P)
                    mm = product(pe, out, xn_hi[:, kc, tk], xn_lo[:, kc, tk], hi[:, kc, :], lo[:, kc, :],
                                 kc == 0, kc == KC - 1)
                else:
                    at = 64 if kind == "ckv" and half else P * half
                    mm = product(pe, out, hi[:, kc, at:at + P], lo[:, kc, at:at + P], xn_hi[:, kc, :],
                                 xn_lo[:, kc, :], kc == 0, kc == KC - 1)
            return mm

        def up_pe(pe, l):
            slot = UP % RING
            pe.wait_ge(s_llo, l + 1)
            pe.wait_ge(s_L, l * 8 + 3)
            def window(t, at):
                return t[slot][:, at:at + P]
            for i in range(6):
                b = (3, 4, 5, 6, 7, 3)[i]
                if i == 5:
                    pe.wait_ge(s_upr, l * 8 + 1)
                for hh in range(2):
                    h = 2 * (i % 3) + hh
                    out = pair[b][:, hh, :]
                    if i < 3:
                        for kc in range(2):
                            at = 576 * kc + 96 * h
                            mm = product(pe, out, window(w_hi, at), window(w_lo, at), c_hi[:, kc, :], c_lo[:, kc, :],
                                         kc == 0, kc == 1)
                    else:
                        at = 1152 + P * h
                        mm = product(pe, out, window(w_hi, at), window(w_lo, at), c_hi[:, 2, :], c_lo[:, 2, :],
                                     True, True)
                mm.then_inc(s_up, 1)
            for t in range(NT):
                pe.wait_ge(s_upr, l * 8 + (t + 2))
                w = [x_[slot][:, 1152:1920].rearrange("p (h n) -> p h n", h=6)[:, :, 64:128] for x_ in (w_hi, w_lo)]
                tk = slice(P * t, P * t + P)
                mm = product(pe, bank[4 + t][:, 0:384].rearrange("p (h n) -> p h n", h=6), c_hi[:, 2, tk],
                             c_lo[:, 2, tk], w[0], w[1], True, True)
                mm.then_inc(s_used if t else s_up, 1)

        def mixer2_act(act, pm, po, q, l):
            def hi(j):
                split_hi(act, pm, j, j % RING, pm.loaded(j), free=j >= RING)
            norm_act(act, q, (lambda: hi(0), lambda: (hi(1), hi(2))))
            for j, (kind, _) in enumerate(MIX2):
                b = pair[j % RING]
                before, now = unit_at(j - 1), unit_at(j)
                for n in before:
                    copy_act(act, l, n)
                if kind == "up":
                    for i in range(8):
                        if i < 7:
                            act.wait_ge(s_up, l * 7 + (i + 1))
                        else:
                            act.wait_ge(s_used, pm.base + (j + 1))
                        if i < 6:
                            dst, src = (qm, km)[i // 3], pair[(3, 4, 5, 6, 7, 3)[i]]
                            act.activation(dst[:, 2 * (i % 3):2 * (i % 3) + 2, :], src, ACT.Copy).then_inc(s_upr, 1)
                        else:
                            act.activation(v2[:, i - 6, 0:384], bank[i - 2][:, 0:384], ACT.Copy).then_inc(s_upr, 1)
                else:
                    act.wait_ge(s_used, pm.base + (j + 1))
                    if kind == "cq":
                        act.activation(latent[:, 0:2, :], b, ACT.Copy)
                        ins = act.activation(lsq[:, 0:2, :], b, ACT.Square)
                    elif kind == "ckv":
                        act.activation(latent[:, 2, :], b[:, 0, :], ACT.Copy)
                        act.activation(lsq[:, 2, :], b[:, 0, :], ACT.Square).then_inc(s_lsq, 1)
                        ins = act.activation(kr[:, :], b[:, 1, :], ACT.Copy)
                    elif kind == "mob":
                        for c in range(2):
                            t = 2 * (j - 2) + c
                            ins = act.activation(mob[:, t, :], b[:, c, :], ACT.Copy, scale=0.125 if t < 3 else 1.0)
                    elif kind == "dil":
                        t = 2 * (j - 7)
                        ins = act.activation(dil[:, t:t + 2, :], b, ACT.Copy, scale=0.125 if t < 6 else 1.0)
                    elif kind in ("mv", "mv2", "dv"):
                        n = 128 if kind == "mv2" else 256
                        at = {"mv": 384, "mv2": 640}.get(kind, 768 + 256 * (j - 13))
                        ins = act.activation(v2[:, :, at:at + n], b[:, :, 0:n], ACT.Copy)
                    else:
                        t = 2 * (j - UP - 1)
                        ins = act.activation(gates2[:, t:t + 2, :], b, ACT.Copy)
                    ins.then_inc(s2_read, 1)
                for n in before:
                    if n % 2:
                        out_hi_act(act, l, n)
                for n in now:
                    exp_act(act, l, n)
                if j + 3 < N2:
                    hi(j + 3)
                if j == 3:
                    act.wait_ge(s_lss, l + 1)
                    act.activation(lroot[:, 0, :], bank[7][:, 0:T], ACT.Sqrt, bias=eps_col[:, 3:4], scale=96.0 / 256)
                    act.activation(lroot[:, 1, :], bank[7][:, T:2 * T], ACT.Sqrt, bias=eps_col[:, 0:1],
                                   scale=1.0 / P).then_inc(s_lroot, 1)
                if j == 5:
                    act.wait_ge(s_lat, l + 1)
                    act.activation(c_hi[:, :, :], latent[:, :, :], ACT.Copy).then_inc(s_lhi, 1)
            act.wait_ge(s_used, pm.base + N2)
            out2_act(act, po, l)

        def mixer2_dve(dve, pm, po, q, l):
            norm_dve(dve, q, V_MIX, lambda: split_lo(dve, pm, 0, 0))
            split_lo(dve, pm, 1, 1)
            split_lo(dve, pm, 2, 2)
            for j, (kind, _) in enumerate(MIX2):
                before, now = unit_at(j - 1), unit_at(j)
                for n in before:
                    if n % 2:
                        out_lo_dve(dve, l, n)
                if j == UP + 1:
                    for i in range(4):
                        if i:
                            dve.drain()
                        dve.wait_ge(s_turn, l * 4 + (i + 1))
                        m = 1 if i == 0 else 2
                        t = kr[0:96, :].unsqueeze(1) if i == 0 else qm[0:96, 2 * i - 2:2 * i, :]
                        src = pair[3 + i][0:96, 0:m, :]
                        dve.tensor_tensor(turned[0:96, 0:m, :], src, over(C["sin"], m)[0:96], ALU.mult)
                        dve.tensor_tensor(t, t, over(C["cos"], m)[0:96], ALU.mult)
                        dve.drain()
                        ins = dve.tensor_tensor(t, t, turned[0:96, 0:m, :], ALU.add)
                        if i == 0:
                            dve.drain()
                            ins = dve.tensor_copy(km[64:96, :, :], kr[64:96, :].unsqueeze(1).to_broadcast([32, 6, T]))
                        ins.then_inc(s_rope, 1)
                for n in now:
                    max_dve(dve, l, n)
                    probs_dve(dve, l, n)
                if j + 3 < N2:
                    split_lo(dve, pm, j + 3, (j + 3) % RING)
                if j == 3:
                    dve.wait_ge(s_lroot, l + 1)
                    dve.reciprocal(linv[:, :, :], lroot[:, :, :])
                    dve.drain()
                    for i in range(3):
                        ins = dve.scalar_tensor_tensor(out=latent[:, i, :], in0=latent[:, i, :],
                                                       scalar=vec[:, V_QN + i:V_QN + i + 1], in1=linv[:, i // 2, :],
                                                       op0=ALU.mult, op1=ALU.mult)
                    ins.then_inc(s_lat, 1)
                if j == 5:
                    dve.wait_ge(s_lhi, l + 1)
                    dve.tensor_tensor(c_lo[:, :, :], latent[:, :, :], c_hi[:, :, :].bitcast(F32),
                                      ALU.subtract).then_inc(s_llo, 1)
            out2_dve(dve, po, l)

        def out2_pe(pe, po, l):
            pe.wait_ge(s_L, l * 8 + 8)
            outs = ((o_mla, 0, 3), (o_mob, 3, 3), (o_dil, 6, 2))
            for j in range(4):
                pe.wait_ge(s_lo, po.base + (j + 1 + LO_START))
                if j >= 2:
                    pe.wait_ge(s2_mg, l * 4 + (j - 1))
                for b, ((hi, lo), k0, k) in enumerate(outs):
                    mm = features(pe, j % RING, pair[3 * (j % 2) + b], hi, lo, k=k, off=256 * k0)
                mm.then_inc(s_used, 1)
            pe.wait_ge(s2_mlo, l * 4 + 4)
            for j in range(4, 8):
                pe.wait_ge(s_lo, po.base + (j + 1 + LO_START))
                features(pe, j % RING, pair[(6, 7, 0, 1)[j - 4]], xn_hi, xn_lo).then_inc(s_used, 1)

        def out2_act(act, po, l):
            for j in range(3):
                split_hi(act, po, j, j, po.loaded(j), free=False)
            act.drain()
            for i in range(3):
                gate = gates2[:, KC * i:KC * i + KC, :]
                act.activation(gate, gate, ACT.Sigmoid).then_inc(s2_gate, 1)
            for j in range(8):
                if j + 3 < 8:
                    split_hi(act, po, j + 3, j % RING, po.loaded(j + 3))
                if j < 4:
                    s = slice(2 * j, 2 * j + 2)
                    act.wait_ge(s2_mg, l * 4 + (j + 1))
                    act.activation(xn_hi[:, s, :], merged2[:, s, :], ACT.Copy).then_inc(s2_mhi, 1)
            act.wait_ge(s_used, po.base + 8)

        def out2_dve(dve, po, l):
            for j in range(3):
                split_lo(dve, po, j, j)
            dve.wait_ge(s2_gate, l * 3 + 3)
            for j in range(8):
                s = slice(2 * j, 2 * j + 2)
                if j < 4:
                    dve.wait_ge(s_used, po.base + (j + 1))
                    p = part[3 * (j % 2):3 * (j % 2) + 3]
                    for i in range(3):
                        dve.tensor_tensor(p[i][:, :, :], pair[3 * (j % 2) + i],
                                          gates2[:, KC * i + 2 * j:KC * i + 2 * j + 2, :], ALU.mult)
                    dve.drain()
                    dve.tensor_tensor(p[0][:, :, :], p[0][:, :, :], p[1][:, :, :], ALU.add)
                    dve.drain()
                    dve.tensor_tensor(merged2[:, s, :], p[0][:, :, :], p[2][:, :, :], ALU.add).then_inc(s2_mg, 1)
                if j + 3 < 8:
                    split_lo(dve, po, j + 3, j % RING)
                if j < 4:
                    dve.wait_ge(s2_mhi, l * 4 + (j + 1))
                    dve.tensor_tensor(xn_lo[:, s, :], merged2[:, s, :], xn_hi[:, s, :].bitcast(F32),
                                      ALU.subtract).then_inc(s2_mlo, 1)
            for i in range(4):
                s = slice(2 * i, 2 * i + 2)
                dve.wait_ge(s_used, po.base + (5 + i))
                dve.tensor_tensor(x[:, s, :], pair[(6, 7, 0, 1)[i]], x[:, s, :], ALU.add).then_inc(s_x, 1)

        s2_gate = sem("gates2_ready")
        mixer_sp.append(mixer2_sp)
        mixer_pe.append(mixer2_pe)
        mixer_act.append(mixer2_act)
        mixer_dve.append(mixer2_dve)

        W = a
        ffn_weights = {
            (0, 0): lambda l: (W["ffn1_w_in"][l], 0, W["ffn1_w_in"][l], F, W["ffn1_w_out"][l]),
            (0, 1): lambda l: (W["ffn2_w_in"][l], 0, W["ffn2_w_in"][l], F, W["ffn2_w_out"][l]),
            (1, 0): lambda l: (W["ffn1_w_gate_2"][l], 0, W["ffn1_w_up_2"][l], 0, W["ffn1_w_down_2"][l]),
            (1, 1): lambda l: (W["ffn2_w_gate_2"][l], 0, W["ffn2_w_up_2"][l], 0, W["ffn2_w_down_2"][l]),
        }
        gain_rows = {0: [("ffn1_norm", KC), ("mix_norm", KC), ("ffn2_norm", KC), ("dn_out_norm", 1),
                         ("sb_q_norm", 1), ("sb_k_norm", 1)],
                     1: [("ffn1_norm_2", KC), ("mix_norm_2", KC), ("ffn2_norm_2", KC), ("q_norm_2", 2),
                         ("kv_norm_2", 1)]}
        n_setup = 2 + 2 * (6 + 1) + 2 * 6 + 2

        block = ctx.enter_context(nc.Block())

        @block.sync
        def _(sp):
            sp.dma_start(consts[:, :], consts_dram).then_inc(s_const, 16)
            sp.dma_start(stage[:, :, :], W["x"].rearrange("b (t p) d -> p (b t) d", p=P)).then_inc(s_const, 16)
            for b in (0, 1):
                for l in range(LAYERS):
                    at = 0
                    for name, n in gain_rows[b]:
                        sp.dma_start(vrows[at:at + n, 2 * b + l, :],
                                     W[name][l].rearrange("(k p) -> k p", p=P)).then_inc(s_const, 16)
                        at += n
                    if b == 0:
                        sp.dma_start(vrows[at:at + 96, l, :],
                                     W["dn_conv_w"][l].rearrange("j (k p) -> (j k) p", p=P)).then_inc(s_const, 16)
                    else:
                        sp.dma_start(vrows[at:at + KC, 2 + l, :],
                                     W["final_norm_2"].rearrange("(k p) -> k p", p=P)).then_inc(s_const, 16)
            for i, name in enumerate(("dn_dt_bias", "dn_a_log")):
                sp.dma_start(dta[:, :, i, :], W[name].partition_broadcast(P)).then_inc(s_const, 16)
            for b in blocks:
                with sp.Fori(0, LAYERS, 1) as l:
                    ffn_sp(sp, in_layer(plans[b], 0, l), *ffn_weights[b, 0](l))
                    mixer_sp[b](sp, in_layer(plans[b], 1, l), in_layer(plans[b], 2, l), l)
                    ffn_sp(sp, in_layer(plans[b], 3, l), *ffn_weights[b, 1](l))
            for t in range(NT):
                sp.wait_ge(s_y, 2 * t + 2)
                sp.dma_start(out_dram.rearrange("b (t p) d -> p (b t) d", p=P)[:, t, :],
                             stage[:, t, :]).then_inc(s_stored, 16)
            sp.wait_ge(s_stored, 16 * NT)

        @block.tensor
        def _(pe):
            pe.wait_ge(s_const, 16 * n_setup)
            for b in range(4):
                n = ROWS1 if b < 2 else ROWS2
                mm = pe.transpose(bank[7][:, P * b:P * b + n], vrows[0:n, b, :], ident[0:n, 0:n])
            mm.then_inc(s_vT, 1)
            for g in range(4):
                if g >= 2:
                    pe.wait_ge(s_x, g - 1)
                for kc in (2 * g, 2 * g + 1):
                    for t in range(NT):
                        mm = pe.transpose(pair[g % 2][:, kc % 2, P * t:P * t + P],
                                          stage[:, t, P * kc:P * kc + P], ident)
                mm.then_inc(s_xT, 1)
            for b in blocks:
                with pe.Fori(0, LAYERS, 1) as l:
                    ffn_pe(pe, in_layer(plans[b], 0, l), norm_index(b, l, 0), ffn_index(b, l, 0))
                    mixer_pe[b](pe, in_layer(plans[b], 1, l), in_layer(plans[b], 2, l), norm_index(b, l, 1), l)
                    ffn_pe(pe, in_layer(plans[b], 3, l), norm_index(b, l, 2),
                           ffn_index(b, l, 1))
            q = last_norm
            norm_pe(pe, q)
            for g in range(4):
                t, h = g // 2, g % 2
                pe.wait_ge(s_xn, 2 * q + h + 1)
                for kc in range(4):
                    mm = pe.transpose(bank[g][:, P * kc:P * kc + P], work[:, 4 * h + kc, P * t:P * t + P], ident)
                mm.then_inc(s_yT, 1)

        @block.scalar
        def _(act):
            act.wait_ge(s_setup, 1)
            for b in blocks:
                with act.Fori(0, LAYERS, 1) as l:
                    ffn_act(act, in_layer(plans[b], 0, l), norm_index(b, l, 0), ffn_index(b, l, 0))
                    mixer_act[b](act, in_layer(plans[b], 1, l), in_layer(plans[b], 2, l), norm_index(b, l, 1), l)
                    ffn_act(act, in_layer(plans[b], 3, l), norm_index(b, l, 2),
                            ffn_index(b, l, 1))
            q = last_norm
            for g in range(4):
                act.wait_ge(s_x, 4 * q + g + 1)
                act.activation(work[:, 2 * g:2 * g + 2, :], x[:, 2 * g:2 * g + 2, :], ACT.Square).then_inc(s_sq, 1)
            act.wait_ge(s_ss, q + 1)
            act.activation(root[:, :], bank[4][:, 0:T], ACT.Sqrt, bias=eps_col[:, 0:1],
                           scale=1.0 / D).then_inc(s_root, 1)
            for g in range(4):
                act.wait_ge(s_yT, g + 1)
                act.activation(stage[:, g // 2, 512 * (g % 2):512 * (g % 2) + 512], bank[g][:, :],
                               ACT.Copy).then_inc(s_y, 1)

        @block.vector
        def _(dve):
            for i, v in enumerate((EPS, P * EPS, 1.0, 96 * EPS)):
                ins = dve.memset(eps_col[:, i:i + 1], v)
            ins.then_inc(s_setup, 1)
            dve.memset(zeros[:, :].bitcast(F32), 0.0).then_inc(s_setup, 1)
            dve.memset(spare[:, :], 0.0).then_inc(s_lo, LO_START)
            dve.wait_ge(s_vT, 1)
            for b in range(4):
                n = ROWS1 if b < 2 else ROWS2
                ins = dve.tensor_copy(vecs[:, b, 0:n], bank[7][:, P * b:P * b + n])
            ins.then_inc(s_vecs, 1)
            for g in range(4):
                dve.wait_ge(s_xT, g + 1)
                dve.tensor_copy(x[:, 2 * g:2 * g + 2, :], pair[g % 2]).then_inc(s_x, 1)
            for b in blocks:
                with dve.Fori(0, LAYERS, 1) as l:
                    n = ROWS1 if b == 0 else ROWS2
                    dve.drain()
                    dve.tensor_copy(vec[:, 0:n], vecs[:, ds(l + 2 * b, 1), 0:n].rearrange("p a n -> p (a n)"))
                    dve.drain()
                    ffn_dve(dve, in_layer(plans[b], 0, l), norm_index(b, l, 0), ffn_index(b, l, 0), V_FFN1)
                    mixer_dve[b](dve, in_layer(plans[b], 1, l), in_layer(plans[b], 2, l), norm_index(b, l, 1), l)
                    ffn_dve(dve, in_layer(plans[b], 3, l), norm_index(b, l, 2),
                            ffn_index(b, l, 1), V_FFN2)
            q = last_norm
            dve.drain()
            dve.tensor_copy(vec[:, 0:ROWS2], vecs[:, 3, 0:ROWS2])
            dve.wait_ge(s_root, q + 1)
            dve.drain()
            dve.reciprocal(rstd[:, :], root[:, :])
            dve.drain()
            for kc in range(KC):
                ins = dve.scalar_tensor_tensor(out=work[:, kc, :], in0=x[:, kc, :],
                                               scalar=vec[:, V_FINAL + kc:V_FINAL + kc + 1], in1=rstd[:, :],
                                               op0=ALU.mult, op1=ALU.mult)
                if kc % 4 == 3:
                    ins.then_inc(s_xn, 1)

        @block.gpsimd
        def _(pool):
            with pool.Fori(0, LAYERS, 1) as l:
                mixer1_pool(pool, l)

def kernel(**inputs):
    import concourse.bacc as bacc
    from concourse.bass_utils import run_bass_kernel_spmd

    nc = bacc.Bacc("TRN2", target_bir_lowering=False, num_devices=1)
    arrays = {f"in_{n}": np.ascontiguousarray(inputs[n]) for n in INPUTS}
    arrays["in_consts"] = const_table()[0]
    drams = {n: nc.dram_tensor(n, v.shape, mybir.dt.from_np(v.dtype), kind="ExternalInput").ap()
             for n, v in arrays.items()}
    out = nc.dram_tensor("out_0", (1, T, D), F32, kind="ExternalOutput").ap()
    build(nc, {n: drams[f"in_{n}"] for n in INPUTS}, drams["in_consts"], out)
    return run_bass_kernel_spmd(nc, [arrays], core_ids=[0]).results[0]["out_0"]
```

```python
from contextlib import ExitStack

import numpy as np

import concourse.bass as bass
from concourse import mybir

F32 = mybir.dt.float32
F32R = mybir.dt.float32r
ACT = mybir.ActivationFunctionType
ALU = mybir.AluOpType
AX = mybir.AxisListType
ds = bass.ds

P = 128
D = 1024
KC = D // P
T = 256
NT = T // P
F = 2816
LAYERS = 2
UNITS = F // 256
ITEM = 2048
RING = 3
FFN_ITEMS = 3 * UNITS
EPS = 1e-6
NEG = -1e30
HEADS = 8



def const_table():
    j = np.arange(P)[:, None]
    i = np.arange(P)[None, :]
    parts = {
        "ident": (i == j),
        "ones": np.ones((P, P)),
        "triu": (j <= i),
        "decay_mask": np.where(j <= i, 0.0, NEG),
        "neg_tri": -1.0 * (j >= i),
        "neg_ones": -np.ones((P, P)),
        "sb_neg": np.where(j < i, 0.0, NEG),
        "sb_mask": (j < i),
    }
    for s in range(7):
        parts[f"level{s}"] = ((j >> s) + 1 == (i >> s)) & ((i >> s) % 2 == 1)
    pos = np.arange(T, dtype=np.float32)
    inv = (10000.0 ** (-np.arange(0, 32, 2, dtype=np.float32) / 32)).astype(np.float32)
    ang = np.zeros((P, T), np.float32)
    ang[64:80] = ang[80:96] = inv[:, None] * pos[None, :]
    parts["cos"] = np.cos(ang)
    parts["sin"] = np.sin(ang)
    turn = np.zeros((P, 96))
    for m in range(64, 80):
        turn[m + 16, m] = -1.0
        turn[m, m + 16] = 1.0
    parts["turn"] = turn
    q = np.arange(P)[:, None]
    tiles = [(0, 0), (1, 0), (1, 1)]
    dist = np.concatenate([(P * a + q) - (P * b + i) for a, b in tiles], axis=1).astype(np.float64)
    parts["causal"] = np.where(dist >= 0, 0.0, NEG)
    parts["all"] = np.where(dist >= 0, -dist, NEG)
    parts["window"] = np.where((dist >= 0) & (dist <= 128), -dist, NEG)
    parts["step4"] = np.where((dist >= 0) & (dist % 4 == 0), -dist, NEG)
    parts["step16"] = np.where((dist >= 0) & (dist % 16 == 0), -dist, NEG)
    at, where = 0, {}
    for name, value in parts.items():
        where[name] = (at, at + value.shape[1])
        at += value.shape[1]
    return np.concatenate([v.astype(np.float32) for v in parts.values()], axis=1), where


INPUTS = [
    "x", "ffn1_norm", "ffn1_w_in", "ffn1_w_out", "mix_norm", "w_in", "dn_conv_w", "dn_a_log", "dn_dt_bias",
    "dn_out_norm", "sb_q_norm", "sb_k_norm", "w_branch_a", "w_branch_b", "w_out", "ffn2_norm", "ffn2_w_in",
    "ffn2_w_out", "ffn1_norm_2", "ffn1_w_gate_2", "ffn1_w_up_2", "ffn1_w_down_2", "mix_norm_2", "w_in_2",
    "q_norm_2", "w_uq_2", "kv_norm_2", "w_ukv_2", "w_br_mla_2", "w_br_moba_2", "w_br_dil_2", "w_out_2",
    "ffn2_norm_2", "ffn2_w_gate_2", "ffn2_w_up_2", "ffn2_w_down_2", "final_norm_2",
]

V_FFN1, V_MIX, V_FFN2 = 0, KC, 2 * KC
V_DN_OUT, V_SBQ, V_SBK, V_CONV = 24, 25, 26, 27
ROWS1 = V_CONV + 4 * 24
V_QN, V_KVN, V_FINAL = 24, 26, 27
ROWS2 = V_FINAL + KC

MIX1 = ([("k", 1024 + 256 * i) for i in range(4)] + [("q", 256 * i) for i in range(4)]
        + [("v", 2048 + 256 * i) for i in range(4)] + [("ba", 4096)]
        + [("z", 3072 + 256 * i) for i in range(4)]
        + [("sbq", 4112 + 256 * i) for i in range(4)] + [("sbk", 5136 + 256 * i) for i in range(4)]
        + [("sbv", 6160 + 256 * i) for i in range(4)]
        + [("gate", 7184 + 256 * i) for i in range(8)])
OUT1 = [(kind, 256 * i) for kind in ("b", "a", "out") for i in range(4)]
MIX2 = ([("cq", 0), ("ckv", 256)] + [("mob", 416 + 256 * i) for i in range(3)] + [("mv", 1184), ("mv2", 1440)]
        + [("dil", 1568 + 256 * i) for i in range(6)] + [("dv", 3104 + 256 * i) for i in range(3)] + [("up", 0)]
        + [("gate", 3872 + 256 * i) for i in range(12)])
OUT2 = [("br", 256 * i) for i in range(4)] + [("out", 256 * i) for i in range(4)]


def width(kind):
    return {"ba": KC * 16, "mv2": KC * 128, "up": 2 * 576 + 768}.get(kind, ITEM)


def copies(kind):
    return {"up": 2, "br": 3}.get(kind, 1)


START = RING


class Phase:

    def __init__(self, base, loads, items, before):
        self.base, self.loads, self.items, self.before = base, list(loads), items, before

    def freed(self, j):
        if not isinstance(j, int) or j >= RING:
            return self.base + (j - 2 + START)
        former = max(i for i in range(self.before) if i % RING == j)
        return self.base + (former + 1 - self.before + START)

    def loaded(self, j):
        s = j % RING
        return 16 * (self.loads[s] + sum(copies(self.items[i][0]) for i in range(s, j + 1, RING)))

    def after(self):
        return [self.loads[s] + sum(copies(k) for k, _ in self.items[s::RING]) for s in range(RING)]


FFN_LIST = [("ffn", 0)] * FFN_ITEMS


def plan(first, second):
    out = []
    base0, loads0 = 0, [0] * RING
    for lists in (first, second):
        base, loads, phases = 0, [0] * RING, []
        for k, items in enumerate(lists):
            phases.append(Phase(base, loads, items, len(lists[k - 1])))
            loads, base = phases[-1].after(), base + len(items)
        out.append((phases, base, loads, base0, loads0))
        base0 += LAYERS * base
        loads0 = [a + LAYERS * b for a, b in zip(loads0, loads)]
    return out


def in_layer(block_plan, k, layer):
    phases, n, loads, base0, loads0 = block_plan
    p = phases[k]
    return Phase(layer * n + (base0 + p.base), [layer * loads[s] + (loads0[s] + p.loads[s]) for s in range(RING)],
                 p.items, p.before)


def build(nc, a, consts_dram, out_dram):
    where = const_table()[1]
    ncol = max(b for _, b in where.values())
    with ExitStack() as ctx:
        top = [(nc.sbuf_base + 63) // 64 * 64]

        def put(name, shape, dt=F32, at=None):
            here = top[0] if at is None else at
            t = nc.alloc_sbuf_tensor_at(name, [P] + shape, dt, offset=here)
            size = 4 * int(np.prod(shape))
            if at is None:
                top[0] = (here + size + 63) // 64 * 64
            assert here + size <= nc.sbuf_usable_end, (name, here + size, nc.sbuf_usable_end)
            return t

        x = put("x_fm", [KC, T])
        consts = put("consts", [ncol])
        vecs = put("vecs", [4, P])
        vec = put("vec_layer", [P])
        eps_col = put("eps_col", [4])
        dta = put("dt_alog", [LAYERS, 2, HEADS])
        spare = put("spare", [START])
        zeros = put("zeros", [P], F32R)
        raw = [put(f"raw{s}", [ITEM]) for s in range(RING)]
        w_hi = [put(f"w_hi{s}", [ITEM], F32R) for s in range(RING)]
        w_lo = [put(f"w_lo{s}", [ITEM], F32R) for s in range(RING)]
        xn_at = top[0]
        xn_hi = put("xn_hi", [KC, T], F32R)
        xn_lo = put("xn_lo", [KC, T], F32R)
        shared = top[0]
        gate_act = put("gate_act", [2, T], at=shared)
        hidden = [put(f"hidden{u}", [2, T], at=shared + 2048 + 20480 * u) for u in range(2)]
        hid_hi = [put(f"hid_hi{u}", [2, T], F32R, at=shared + 4096 + 2048 * u) for u in range(2)]
        hid_lo = [put(f"hid_lo{u}", [2, T], F32R, at=shared + 8192 + 2048 * u) for u in range(2)]
        work = put("work", [KC, T], at=shared + 12288)
        root = put("root", [NT], at=shared + 20480)
        rstd = put("rstd", [NT], at=shared + 20544)
        diag = put("rstd_diag", [NT, P], at=shared + 20608)
        stage = put("stage", [NT, D], at=shared)
        vrows = put("vrows", [4, P], at=shared + 8192)

        C = {k: consts[:, lo:hi] for k, (lo, hi) in where.items()}
        ident, ones = C["ident"], C["ones"]
        bank = [ctx.enter_context(nc.psum_tensor(f"bank{b}", [P, 512], F32)) for b in range(8)]
        pair = [b[:, :].rearrange("p (c t) -> p c t", c=2) for b in bank]

        def sem(name):
            return ctx.enter_context(nc.semaphore(name))

        s_const = sem("x_loaded")
        s_gains = sem("gains_loaded")
        s_rest = sem("rest_loaded")
        s_setup = sem("setup_done")
        s_xT = sem("x_transposed")
        s_vT = sem("vecs_transposed")
        s_vecs = sem("vecs_ready")
        loaded = [sem(f"slot{s}_loaded") for s in range(RING)]
        s_hi = sem("item_hi")
        s_lo = sem("item_lo")
        s_used = sem("item_used")
        s_down = sem("way_down")
        s_x = sem("x_updated")
        s_sq = sem("squares")
        s_ss = sem("square_sums")
        s_diag = sem("root_diagonal")
        s_root = sem("root_ready")
        s_xn = sem("normed")
        s_xhi = sem("normed_hi")
        s_xlo = sem("normed_lo")
        s_gact = sem("gate_activated")
        s_hid = sem("hidden_ready")
        s_hhi = sem("hidden_hi")
        s_hlo = sem("hidden_lo")
        s_yT = sem("out_transposed")
        s_y = sem("out_copied")
        s_stored = sem("stored")

        first = [FFN_LIST, MIX1, OUT1, FFN_LIST]
        second = [FFN_LIST, MIX2, OUT2, FFN_LIST]
        plans = plan(first, second)
        blocks = range(2)

        n_gains, n_rest = 6 + 1 + 5 + 2, 3

        def norm_index(block, layer, k):
            return layer * 3 + (LAYERS * 3 * block + k)

        def ffn_index(block, layer, k):
            return layer * 2 + (LAYERS * 2 * block + k)

        last_norm = norm_index(2, 0, 0)

        def bc(ap, n):
            return ap.unsqueeze(2).to_broadcast([P, ap.shape[1], n])

        def over(ap, n):
            return ap.unsqueeze(1).to_broadcast([P, n, ap.shape[1]])

        first_bank_of = {"ffn": 4, "k": 0, "cq": 0}

        def rows(w):
            return w.rearrange("(k p) n -> p k n", p=P)

        def cols(w, at, n=256):
            return rows(w)[:, :, at:at + n] if isinstance(at, int) else rows(w)[:, :, ds(at, n)]

        def slot_view(t, k, n):
            return t[:, 0:k * n].rearrange("p (k n) -> p k n", k=k)

        def bring(sp, slot, dst, src, free=None):
            sp.lower_val(src.offset * 4)
            if free is not None:
                sp.wait_ge(s_lo, free)
            sp.dma_start(dst, src).then_inc(loaded[slot], 16)

        def split_hi(act, p, j):
            slot, n = j % RING, width(p.items[j][0])
            act.wait_ge(loaded[slot], p.loaded(j))
            act.wait_ge(s_used, p.freed(j))
            act.activation(w_hi[slot][:, 0:n], raw[slot][:, 0:n], ACT.Copy).then_inc(s_hi, 1)

        def split_lo(dve, p, j):
            slot, n = j % RING, width(p.items[j][0])
            dve.wait_ge(s_hi, p.base + (j + 1))
            dve.tensor_tensor(w_lo[slot][:, 0:n], raw[slot][:, 0:n], w_hi[slot][:, 0:n].bitcast(F32),
                              ALU.subtract).then_inc(s_lo, 1)

        def product(pe, out, a_hi, a_lo, b_hi, b_lo, start, stop, check=False):
            pe.matmul(out, a_hi, b_hi, start=start, stop=False, skip_group_check=check)
            pe.matmul(out, a_hi, b_lo, start=False, stop=False, skip_group_check=check)
            return pe.matmul(out, a_lo, b_hi, start=False, stop=stop, skip_group_check=check)

        def first_item(pe, p, q):
            pe.wait_ge(s_lo, p.base + (1 + START))
            hi, lo = slot_view(w_hi[0], KC, 256), slot_view(w_lo[0], KC, 256)
            for kc in range(KC):
                pe.wait_ge(s_xlo, q * KC + (kc + 1))
                for c in range(2):
                    mm = product(pe, pair[first_bank_of[p.items[0][0]]][:, c, :], hi[:, kc, P * c:P * c + P], lo[:, kc, P * c:P * c + P],
                                 xn_hi[:, kc, :], xn_lo[:, kc, :], kc == 0 and c == 0, kc == KC - 1, True)
            mm.then_inc(s_used, 1)

        def features(pe, slot, out, in_hi, in_lo, k=KC, n=256, off=0, m=P):
            hi = slot_view(w_hi[slot][:, off:off + k * n], k, n)
            lo = slot_view(w_lo[slot][:, off:off + k * n], k, n)
            for c in range(n // m):
                for kc in range(k):
                    mm = product(pe, out[:, c, :], hi[:, kc, m * c:m * c + m], lo[:, kc, m * c:m * c + m],
                                 in_hi[:, kc, :], in_lo[:, kc, :], kc == 0, kc == k - 1)
            return mm

        def by_tiles(pe, p, j, out, in_hi, in_lo, ready, count):
            slot = j % RING
            pe.wait_ge(s_lo, p.base + (j + 1 + START))
            hi, lo = slot_view(w_hi[slot], KC, 256), slot_view(w_lo[slot], KC, 256)
            for kc in range(KC):
                if kc % 2 == 0:
                    pe.wait_ge(ready, count + (kc // 2 + 1))
                for c in range(2):
                    mm = product(pe, out[:, c, :], hi[:, kc, P * c:P * c + P], lo[:, kc, P * c:P * c + P],
                                 in_hi[:, kc, :], in_lo[:, kc, :], kc == 0 and c == 0, kc == KC - 1, True)
            mm.then_inc(s_used, 1)

        def tokens(pe, slot, out, in_hi, in_lo, k=KC, n=256, off=0):
            hi = slot_view(w_hi[slot][:, off:off + k * n], k, n)
            lo = slot_view(w_lo[slot][:, off:off + k * n], k, n)
            for t in range(NT):
                for kc in range(k):
                    mm = product(pe, out[:, t, 0:n], in_hi[:, kc, P * t:P * t + P], in_lo[:, kc, P * t:P * t + P],
                                 hi[:, kc, :], lo[:, kc, :], kc == 0, kc == k - 1)
            return mm

        def norm_act(act, p, q):
            split_hi(act, p, 0)
            split_hi(act, p, 1)
            for g in range(4):
                act.wait_ge(s_x, q * 4 + (g + 1))
                act.activation(work[:, 2 * g:2 * g + 2, :], x[:, 2 * g:2 * g + 2, :], ACT.Square).then_inc(s_sq, 1)
            norm_root(act, q)
            for kc in range(KC):
                act.wait_ge(s_xn, q * KC + (kc + 1))
                act.activation(xn_hi[:, kc, :], work[:, kc, :], ACT.Copy).then_inc(s_xhi, 1)
            split_hi(act, p, 2)

        def norm_root(act, q):
            act.wait_ge(s_ss, q * 2 + 1)
            act.activation(root[:, :], bank[4][:, 0:NT], ACT.Sqrt, bias=eps_col[:, 0:1],
                           scale=1.0 / D).then_inc(s_root, 1)

        def keep_warm(pe, b, n):
            for i in range(n):
                pe.matmul(bank[b][:, 0:P], zeros[:, :], zeros[:, :], start=(i == 0), stop=(i == n - 1))

        def norm_pe(pe, q):
            for kc in range(KC):
                if kc % 2 == 0:
                    pe.wait_ge(s_sq, q * 4 + (kc // 2 + 1))
                for t in range(NT):
                    mm = pe.matmul(bank[4][:, t:t + 1], work[:, kc, P * t:P * t + P], ones[:, 0:1],
                                   start=(kc == 0 and t == 0), stop=(kc == KC - 1), skip_group_check=True)
            mm.then_inc(s_ss, 1)
            keep_warm(pe, 5, 6)
            pe.wait_ge(s_diag, q + 1)
            pe.matmul(bank[5][:, 0:T], ones, diag[:, :, :], start=True, stop=True).then_inc(s_ss, 1)
            keep_warm(pe, 4, 8)

        def norm_scale(dve, q):
            dve.wait_ge(s_root, q + 1)
            dve.reciprocal(rstd[:, :], root[:, :])
            dve.drain()
            dve.tensor_tensor(diag[:, :, :], over(ident, NT), bc(rstd[:, :], P), ALU.mult).then_inc(s_diag, 1)
            dve.wait_ge(s_ss, q * 2 + 2)

        def norm_tile(dve, q, gain, kc):
            dve.scalar_tensor_tensor(out=work[:, kc, :], in0=x[:, kc, :], scalar=vec[:, gain + kc:gain + kc + 1],
                                     in1=bank[5][:, 0:T], op0=ALU.mult, op1=ALU.mult).then_inc(s_xn, 1)

        def norm_dve(dve, p, q, gain):
            split_lo(dve, p, 0)
            norm_scale(dve, q)
            for kc in range(KC + 1):
                if kc < KC:
                    norm_tile(dve, q, gain, kc)
                if kc:
                    dve.wait_ge(s_xhi, q * KC + kc)
                    dve.tensor_tensor(xn_lo[:, kc - 1, :], work[:, kc - 1, :], xn_hi[:, kc - 1, :].bitcast(F32),
                                      ALU.subtract).then_inc(s_xlo, 1)
            split_lo(dve, p, 1)
            split_lo(dve, p, 2)

        def ffn_sp(sp, p, gate_w, gate_at, up_w, up_at, down_w):
            def put_in(slot, src, k, n, j):
                bring(sp, slot, slot_view(raw[slot], k, n), src, p.freed(j))

            def unit(u, slots):
                j = u * 3 - 1
                put_in(slots[0], cols(gate_w, u * 256 + gate_at), KC, 256, j)
                put_in(slots[1], cols(up_w, u * 256 + up_at), KC, 256, j + 1)
                put_in(slots[2], rows(down_w)[:, ds((u - 1) * 2, 2), :], 2, D, j + 2)

            put_in(0, cols(gate_w, gate_at), KC, 256, 0)
            put_in(1, cols(up_w, up_at), KC, 256, 1)
            put_in(2, cols(gate_w, gate_at + 256), KC, 256, 2)
            put_in(0, cols(up_w, up_at + 256), KC, 256, 3)
            put_in(1, rows(down_w)[:, 0:2, :], 2, D, 4)
            with sp.Fori(2, UNITS, 1) as u:
                unit(u, (2, 0, 1))
            put_in(2, rows(down_w)[:, 2 * UNITS - 2:2 * UNITS, :], 2, D, FFN_ITEMS - 1)

        def ffn_pe(pe, p, q, f):
            pe.wait_ge(s_x, q * 4 + 4)
            pe.wait_ge(s_setup, 2)
            for b in range(4):
                pe.matmul(bank[b][:, 0:P], zeros[:, :], zeros[:, :], start=True, stop=False, skip_group_check=True)

            def project(j, slot, b):
                pe.wait_ge(s_lo, p.base + (j + 1 + START))
                features(pe, slot, pair[b], xn_hi, xn_lo).then_inc(s_used, 1)

            def down(j, slot, u, par, last=False):
                pe.wait_ge(s_hlo, f * UNITS + (u + 1))
                pe.wait_ge(s_lo, p.base + (j + 1 + START))
                hi, lo = slot_view(w_hi[slot], 2, D), slot_view(w_lo[slot], 2, D)

                def part(kk, m):
                    return product(pe, pair[m // 2][:, m % 2, :], hi[:, kk, P * m:P * m + P],
                                   lo[:, kk, P * m:P * m + P], hid_hi[par][:, kk, :], hid_lo[par][:, kk, :],
                                   False, last and kk == 1, True)
                if last:
                    for g in range(4):
                        for kk in range(2):
                            for m in (2 * g, 2 * g + 1):
                                mm = part(kk, m)
                        mm.then_inc(s_down if g < 3 else s_used, 1)
                else:
                    for kk in range(2):
                        for m in range(KC):
                            mm = part(kk, m)
                    mm.then_inc(s_used, 1)

            norm_pe(pe, q)
            first_item(pe, p, q)
            project(1, 1, 5)
            with pe.Fori(1, UNITS, 2) as u:
                project(u * 3 - 1, 2, 6)
                project(u * 3, 0, 7)
                down(u * 3 + 1, 1, u - 1, 0)
                project(u * 3 + 2, 2, 4)
                project(u * 3 + 3, 0, 5)
                down(u * 3 + 4, 1, u, 1)
            down(FFN_ITEMS - 1, 2, UNITS - 1, 0, True)

        def ffn_act(act, p, q, f):
            norm_act(act, p, q)

            def turn(u, j, par, slots):
                act.wait_ge(s_used, p.base + (j + 1 + START))
                act.activation(gate_act[:, :, :], pair[4 + 2 * par], ACT.Silu).then_inc(s_gact, 1)

            def hi_hidden(u, par):
                act.wait_ge(s_hid, f * UNITS + (u + 1))
                act.activation(hid_hi[par][:, :, :], hidden[par][:, :, :], ACT.Copy).then_inc(s_hhi, 1)

            def next_hi(j, slot, n_loaded):
                act.wait_ge(loaded[slot], n_loaded)
                act.wait_ge(s_used, p.freed(j))
                act.activation(w_hi[slot][:, :], raw[slot][:, :], ACT.Copy).then_inc(s_hi, 1)

            L = p.loads
            turn(0, 0, 0, None)
            next_hi(3, 0, (L[0] + 2) * 16)
            hi_hidden(0, 0)
            next_hi(4, 1, (L[1] + 2) * 16)

            def unit(u, par, ahead=3):
                turn(u, u * 3 - 1, par, None)
                next_hi(u * 3 + 2, 2, (L[2] + (u + 1)) * 16)
                hi_hidden(u, par)
                if ahead == 3:
                    next_hi(u * 3 + 3, 0, (L[0] + (u + 2)) * 16)
                    next_hi(u * 3 + 4, 1, (L[1] + (u + 2)) * 16)
            with act.Fori(1, UNITS - 2, 2) as u:
                unit(u, 1)
                unit(u + 1, 0)
            unit(UNITS - 2, 1)
            unit(UNITS - 1, 0, 1)

        def ffn_dve(dve, p, q, f, gain):
            def lo(j, slot):
                dve.wait_ge(s_hi, p.base + (j + 1))
                dve.tensor_tensor(w_lo[slot][:, :], raw[slot][:, :], w_hi[slot][:, :].bitcast(F32),
                                  ALU.subtract).then_inc(s_lo, 1)
            norm_dve(dve, p, q, gain)

            def unit(u, j, par, slots):
                dve.wait_ge(s_gact, f * UNITS + (u + 1))
                dve.wait_ge(s_used, p.base + (j + 2 + START))
                dve.tensor_tensor(hidden[par][:, :, :], gate_act[:, :, :], pair[5 + 2 * par], ALU.mult).then_inc(s_hid, 1)
                lo(j + 3, slots[0])
                dve.wait_ge(s_hhi, f * UNITS + (u + 1))
                dve.tensor_tensor(hid_lo[par][:, :, :], hidden[par][:, :, :], hid_hi[par][:, :, :].bitcast(F32),
                                  ALU.subtract).then_inc(s_hlo, 1)
                for i in range(1, len(slots)):
                    lo(j + 3 + i, slots[i])
            unit(0, 0, 0, (0, 1))
            with dve.Fori(1, UNITS - 2, 2) as u:
                unit(u, u * 3 - 1, 1, (2, 0, 1))
                unit(u + 1, u * 3 + 2, 0, (2, 0, 1))
            unit(UNITS - 2, (UNITS - 2) * 3 - 1, 1, (2, 0, 1))
            unit(UNITS - 1, (UNITS - 1) * 3 - 1, 0, (2,))
            for b in range(4):
                if b < 3:
                    dve.wait_ge(s_down, f * 3 + (b + 1))
                else:
                    dve.wait_ge(s_used, p.base + (FFN_ITEMS + START))
                s = slice(2 * b, 2 * b + 2)
                dve.scalar_tensor_tensor(out=x[:, s, :], in0=pair[b], scalar=0.5, in1=x[:, s, :],
                                         op0=ALU.mult, op1=ALU.add).then_inc(s_x, 1)

        tail = shared + 73728
        kT = put("dn_kT", [HEADS, T], at=shared)
        qT = put("dn_qT", [HEADS, T], at=shared + 8192)
        vT = put("dn_vT", [HEADS, T], at=shared + 16384)
        zs = put("dn_z", [HEADS, T], at=shared + 24576)
        sq_ = put("sb_qT", [HEADS, T], at=shared + 32768)
        sk_ = put("sb_kT", [HEADS, T], at=shared + 40960)
        sv = put("sb_v", [NT, D], at=shared + 49152)
        gates = put("gates1", [2 * KC, T], at=shared + 57344)
        small_at = tail + 14336
        small = {}
        for i, name in enumerate(("beta", "y", "absy", "softp", "graw", "gcum", "gend", "egc", "dend", "nbeg",
                                  "alog_e")):
            small[name] = put("sm_" + name, [2, HEADS], at=small_at + 64 * i)
        ba = put("sm_ba", [NT, 16], at=small_at + 704)
        assert small_at + 832 <= nc.sbuf_usable_end - 256
        conv_in = [put(f"conv_in{r}", [2, T], at=tail + 2048 * r) for r in range(2)]
        conv_acc = [put(f"conv_acc{r}", [2, T], at=tail + 4096 + 2048 * r) for r in range(2)]
        hsq = [put(f"head_sq{r}", [2, T], at=tail + 2048 * r) for r in range(2)]
        hdiag = [put(f"head_diag{r}", [4, P], at=tail + 4096 + 2048 * r) for r in range(2)]
        hroot = [put(f"head_root{r}", [4], at=tail + 8192 + 64 * r) for r in range(2)]
        hinv = [put(f"head_inv{r}", [4], at=tail + 8320 + 64 * r) for r in range(2)]
        Ti = put("inv", [2, 4, P], at=xn_at)
        Ui = put("inv_t", [2, 4, P], at=xn_at + 4096)
        Xi = put("coupled", [2, 4, P], at=xn_at + 8192)
        Ms = put("level_part", [2, 4, P], at=xn_at + 12288)
        Mi = put("l_t", [2, 4, P], at=tail)
        De = put("decay", [2, 4, P], at=tail + 4096)
        At = put("attn_t", [2, 4, P], at=tail + 8192)
        egb = put("decay_rows", [4, P], at=tail + 12288)
        gt = Mi

        def beta_at(G):
            return Ti if G else At
        vn0, st1, vn1, qd = Xi[:, 0], Xi[:, 1], Ms[:, 0], De[:, 0]
        osq = put("o_sq", [KC, T], at=tail)
        odiag = [put(f"o_diag{r}", [4, P], at=tail + 8192 + 2048 * r) for r in range(2)]
        oroot = put("o_root", [2 * HEADS], at=tail + 12288)
        oinv = put("o_inv", [2 * HEADS], at=tail + 12352)
        oa_hi = put("oa_hi", [KC, T], F32R, at=shared)
        oa_lo = put("oa_lo", [KC, T], F32R, at=shared + 16384)
        lg = raw[0][:, 0:4 * 384].rearrange("p (i n) -> p i n", i=4)
        ob_hi = put("ob_hi", [KC, T], F32R, at=shared + 40960)
        ob_lo = put("ob_lo", [KC, T], F32R, at=shared + 32768)
        merged = put("merged1", [KC, T], at=shared + 24576)

        s_read = sem("proj_read")
        s_conv = sem("conv_done")
        s_silu = sem("conv_silu")
        s_hsq = sem("head_squares")
        s_hss = sem("head_sums")
        s_hdiag = sem("head_diagonal")
        s_hroot = sem("head_root")
        s_hnorm = sem("head_normed")
        s_sm_d = sem("gates_dve")
        s_sm_a = sem("gates_act")
        s_sm_p = sem("gates_pe")
        s_gbt = sem("rows_ready")
        s_gb = sem("rows_spread")
        s_kkq = sem("kk_kq")
        s_dm = sem("decay_logs")
        s_De = sem("decays")
        s_qd = sem("q_decayed")
        s_tu = sem("inverse_step")
        s_ms = sem("level_part_ready")
        s_xm = sem("coupled_product")
        s_xs = sem("coupled_copied")
        s_tum = sem("step_products")
        s_vt = sem("v_transposed")
        s_r = sem("rhs_ready")
        s_vn0m = sem("v_new_pe")
        s_vn0 = sem("v_new_act")
        s_r1 = sem("rhs1_ready")
        s_o = sem("o_product")
        s_oev = sem("o_copied")
        s_osq = sem("o_squares")
        s_oss = sem("o_sums")
        s_oroot = sem("o_root")
        s_odiag = sem("o_diagonal")
        s_orow = sem("o_rows")
        s_oa = sem("oa_ready")
        s_oahi = sem("oa_upper")
        s_oalo = sem("oa_lower")
        s_z = sem("stick_scores")
        s_ln = sem("stick_logs")
        s_sp = sem("stick_softplus")
        s_R = sem("stick_sums")
        s_w = sem("stick_weights")
        s_pv = sem("stick_out")
        s_obhi = sem("ob_upper")
        s_oblo = sem("ob_lower")
        s_mg = sem("merged_ready")
        s_mhi = sem("merged_upper")
        s_mlo = sem("merged_lower")

        N1 = len(MIX1)

        def bring_phase(sp, p, parts, hold=None):
            for j, (kind, arg) in enumerate(p.items):
                free = p.freed(j)
                if hold and j == RING:
                    sp.wait_ge(*hold)
                for dst, src in parts(kind, arg, raw[j % RING]):
                    bring(sp, j % RING, dst, src, free)
                    free = None

        def mixer1_sp(sp, pm, po, l):
            def proj(kind, at, slot):
                n = 16 if kind == "ba" else 256
                return [(slot_view(slot, KC, n), cols(a["w_in"][l], at, n))]

            def way_out(kind, at, slot):
                w = {"a": "w_branch_a", "b": "w_branch_b", "out": "w_out"}[kind]
                return [(slot_view(slot, KC, 256), cols(a[w][l], at))]
            bring_phase(sp, pm, proj)
            bring_phase(sp, po, way_out, (s_pv, l * 8 + 8))

        def proj_out(kind, j):
            first = [k for k, _ in MIX1].index(kind)
            i = j - first
            s = slice(2 * i, 2 * i + 2)
            if kind == "sbv":
                return sv[:, :, 256 * i:256 * i + 256]
            return {"k": kT, "q": qT, "v": vT, "z": zs, "sbq": sq_, "sbk": sk_, "gate": gates}[kind][:, s, :]

        def head_pair(n):
            return (kT[:, n, :], qT[:, n, :]) if n < HEADS else (sk_[:, n - HEADS, :], sq_[:, n - HEADS, :])

        STEP0 = 14
        GATES0 = 17
        DECAYS0 = 33

        def mixer1_proj_pe(pe, pm, q, l):
            pe.wait_ge(s_rest, 16 * n_rest)
            norm_pe(pe, q)
            first_item(pe, pm, q)

            def item(j, slot, kind="feature", first=False):
                if not first:
                    pe.wait_ge(s_read, l * N1 + (j - 2))
                pe.wait_ge(s_lo, pm.base + (j + 1 + START))
                if kind == "ba":
                    mm = tokens(pe, slot, pair[slot], xn_hi, xn_lo, n=16)
                elif kind == "sbv":
                    mm = tokens(pe, slot, pair[slot], xn_hi, xn_lo)
                else:
                    mm = features(pe, slot, pair[slot], xn_hi, xn_lo)
                mm.then_inc(s_used, 1)

            def sums(n):
                pe.wait_ge(s_hsq, l * 16 + (n + 1))
                if n >= 2:
                    pe.wait_ge(s_hnorm, l * 16 + (n - 1))
                for i in range(4):
                    mm = pe.matmul(bank[4 + n % 2][:, i:i + 1], hsq[n % 2][:, i // 2, P * (i % 2):P * (i % 2) + P],
                                   ones[:, 0:1], start=(i == 0), stop=(i == 3), skip_group_check=True)
                mm.then_inc(s_hss, 1)

            def spread(n):
                pe.wait_ge(s_hdiag, l * 16 + (n + 1))
                pe.matmul(bank[4 + n % 2][:, :], ones, hdiag[n % 2][:, :, :], start=True,
                          stop=True).then_inc(s_hss, 1)
            for j in (1, 2):
                item(j, j, first=True)
            with pe.Fori(3, 12, 3) as j:
                for i in range(3):
                    item(j + i, i)
            for j in range(12, N1):
                item(j, j % RING, MIX1[j][0])
                if j == GATES0 + 3:
                    delta_gates_pe(pe, l)
                if j - DECAYS0 in (0, 2, 3):
                    decays_pe(pe, l, 0, j - DECAYS0)
                if 0 <= j - 2 - STEP0 < 16:
                    spread(j - 2 - STEP0)
                if 0 <= j - 1 - STEP0 < 16:
                    sums(j - 1 - STEP0)

        def mixer1_proj_act(act, pm, q, l):
            act.wait_ge(s_rest, 16 * n_rest)
            norm_act(act, pm, q)

            def silu(j):
                act.wait_ge(s_conv, l * 12 + (j + 1))
                act.activation(proj_out(MIX1[j][0], j), conv_acc[j % 2][:, :, :], ACT.Silu).then_inc(s_silu, 1)
            for j, (kind, _) in enumerate(MIX1):
                act.wait_ge(s_used, pm.base + (j + 1 + START))
                b = pair[j % RING]
                if kind in "kqv":
                    act.activation(conv_in[j % 2][:, :, :], b, ACT.Copy).then_inc(s_read, 1)
                elif kind == "ba":
                    act.activation(ba[:, :, :], b[:, :, 0:16], ACT.Copy).then_inc(s_read, 1)
                else:
                    act.activation(proj_out(kind, j), b, ACT.Silu if kind == "z" else ACT.Copy).then_inc(s_read, 1)
                if 1 <= j <= 12:
                    silu(j - 1)
                n = j - STEP0 - 1
                if 0 <= n < 16:
                    act.wait_ge(s_hss, l * 16 * 2 + (2 * n + 1))
                    r, sums = hroot[n % 2], bank[4 + n % 2]
                    if n < HEADS:
                        act.activation(r[:, :], sums[:, 0:4], ACT.Sqrt, bias=eps_col[:, 0:1]).then_inc(s_hroot, 1)
                    else:
                        act.activation(r[:, 0:2], sums[:, 0:2], ACT.Sqrt, bias=eps_col[:, 0:1], scale=1.0 / P)
                        act.activation(r[:, 2:4], sums[:, 2:4], ACT.Sqrt, bias=eps_col[:, 1:2]).then_inc(s_hroot, 1)
                n = j - STEP0
                if 0 <= n < 16:
                    act.drain()
                    if n == 0:
                        act.wait_ge(s_conv, l * 12 + 12)
                    for i, t in enumerate(head_pair(n)):
                        ins = act.activation(hsq[n % 2][:, i, :], t, ACT.Square)
                    ins.then_inc(s_hsq, 1)
                if j == DECAYS0 + 1:
                    decays_act(act, l, 0)
                if j + 3 < N1:
                    split_hi(act, pm, j + 3)
                if j == GATES0:
                    delta_gates_act(act, l)
                if j == GATES0 + 4:
                    delta_decays_act(act, l)

        def mixer1_proj_dve(dve, pm, q, l):
            dve.wait_ge(s_rest, 16 * n_rest)
            norm_dve(dve, pm, q, V_MIX)
            for j, (kind, _) in enumerate(MIX1):
                if kind in "kqv":
                    tile0 = {"q": 0, "k": 8, "v": 16}[kind] + 2 * (j % 4)
                    src, acc = conv_in[j % 2], conv_acc[j % 2]
                    dve.wait_ge(s_read, l * N1 + (j + 1))
                    if j >= 2:
                        dve.wait_ge(s_silu, l * 12 + (j - 1))
                    for back in range(4):
                        for c in range(2):
                            col = V_CONV + 24 * (3 - back) + tile0 + c
                            w = vec[:, col:col + 1]
                            if back == 0:
                                ins = dve.tensor_scalar(acc[:, c, :], src[:, c, :], w, None, ALU.mult)
                            else:
                                ins = dve.scalar_tensor_tensor(
                                    out=acc[:, c, back:T], in0=src[:, c, 0:T - back], scalar=w,
                                    in1=acc[:, c, back:T], op0=ALU.mult, op1=ALU.add)
                        if back < 3:
                            dve.drain()
                    ins.then_inc(s_conv, 1)
                n = j - STEP0 - 1
                if 0 <= n < 16:
                    dve.wait_ge(s_hroot, l * 16 + (n + 1))
                    dve.reciprocal(hinv[n % 2][:, :], hroot[n % 2][:, :])
                    dve.drain()
                    if n >= 2:
                        dve.wait_ge(s_hss, l * 32 + (2 * n - 2))
                    dve.tensor_tensor(hdiag[n % 2][:, :, :], over(ident, 4), bc(hinv[n % 2][:, :], P),
                                      ALU.mult).then_inc(s_hdiag, 1)
                if j >= DECAYS0 - 1:
                    decays_dve(dve, l, 0, j - DECAYS0 + 1)
                if j + 3 < N1:
                    split_lo(dve, pm, j + 3)
                if GATES0 - 3 <= j <= GATES0 + 5:
                    delta_gates_dve(dve, l, j - GATES0)
                n = j - STEP0 - 2
                if 0 <= n < 16:
                    k, qq = head_pair(n)
                    row = pair[4 + n % 2]
                    dve.wait_ge(s_hss, l * 32 + (2 * n + 2))
                    if n < HEADS:
                        dve.tensor_tensor(k, k, row[:, 0, :], ALU.mult)
                        dve.scalar_tensor_tensor(out=qq, in0=qq, scalar=float(P) ** -0.5, in1=row[:, 1, :],
                                                 op0=ALU.mult, op1=ALU.mult).then_inc(s_hnorm, 1)
                    else:
                        dve.scalar_tensor_tensor(out=k, in0=k, scalar=vec[:, V_SBK:V_SBK + 1], in1=row[:, 0, :],
                                                 op0=ALU.mult, op1=ALU.mult)
                        dve.scalar_tensor_tensor(out=qq, in0=qq, scalar=vec[:, V_SBQ:V_SBQ + 1], in1=row[:, 1, :],
                                                 op0=ALU.mult, op1=ALU.mult).then_inc(s_hnorm, 1)

        def delta_gates_act(act, l):
            act.drain()
            act.activation(small["beta"][:, :, :], ba[:, :, 0:HEADS], ACT.Sigmoid)
            act.wait_ge(s_sm_d, l * 3 + 1)
            act.activation(small["absy"][:, :, :], small["y"][:, :, :], ACT.Abs)
            act.activation(small["alog_e"][:, 0:1, :], dta[:, ds(l, 1), 1, :], ACT.Exp)
            act.drain()
            act.activation(small["softp"][:, :, :], small["absy"][:, :, :], ACT.Exp, scale=-1.0)
            act.drain()
            act.activation(small["absy"][:, :, :], small["softp"][:, :, :], ACT.Ln,
                           bias=eps_col[:, 2:3]).then_inc(s_sm_a, 1)

        def delta_decays_act(act, l):
            act.wait_ge(s_sm_d, l * 3 + 3)
            act.activation(small["egc"][:, :, :], small["gcum"][:, :, :], ACT.Exp)
            act.activation(small["dend"][:, :, :], small["gend"][:, :, :], ACT.Exp).then_inc(s_sm_a, 1)

        def delta_gates_dve(dve, l, step):
            if step == -3:
                dve.wait_ge(s_read, l * N1 + 13)
                dve.tensor_tensor(small["y"][:, :, :], ba[:, :, HEADS:2 * HEADS],
                                  dta[:, ds(l, 1), 0, :].to_broadcast([P, 2, HEADS]), ALU.add).then_inc(s_sm_d, 1)
            if step == 1:
                dve.wait_ge(s_sm_a, l * 2 + 1)
                dve.scalar_tensor_tensor(out=small["softp"][:, :, :], in0=small["y"][:, :, :], scalar=0.0,
                                         in1=small["absy"][:, :, :], op0=ALU.max, op1=ALU.add)
                dve.drain()
                dve.scalar_tensor_tensor(out=small["graw"][:, :, :], in0=small["softp"][:, :, :], scalar=-1.0,
                                         in1=small["alog_e"][:, 0:1, :].to_broadcast([P, 2, HEADS]),
                                         op0=ALU.mult, op1=ALU.mult).then_inc(s_sm_d, 1)
            if step == 3:
                dve.wait_ge(s_sm_p, l + 1)
                dve.tensor_copy(small["gcum"][:, :, :], bank[6][:, 0:16].rearrange("p (c h) -> p c h", c=2))
                dve.drain()
                dve.tensor_tensor(small["gend"][:, :, :], bank[6][:, 16:32].rearrange("p (c h) -> p c h", c=2),
                                  small["gcum"][:, :, :], ALU.subtract).then_inc(s_sm_d, 1)
            if step == 5:
                dve.wait_ge(s_sm_a, l * 2 + 2)
                dve.scalar_tensor_tensor(out=small["nbeg"][:, :, :], in0=small["egc"][:, :, :], scalar=-1.0,
                                         in1=small["beta"][:, :, :], op0=ALU.mult, op1=ALU.mult)

        def delta_gates_pe(pe, l):
            pe.wait_ge(s_sm_d, l * 3 + 2)
            g = small["graw"][:, :, :]
            pe.matmul(bank[6][:, 0:16], C["triu"], g, start=True, stop=True)
            pe.matmul(bank[6][:, 16:32], ones, g, start=True, stop=True).then_inc(s_sm_p, 1)

        def tok(c):
            return slice(P * c, P * c + P)

        def heads4(G):
            return slice(4 * G, 4 * G + 4)

        b4 = [b[:, :].rearrange("p (h n) -> p h n", h=4) for b in bank]

        def key_products():
            return [bank[5 + i][:, :].rearrange("p (h a n) -> p h a n", h=2, a=2) for i in range(2)]

        def decays_pe(pe, l, G, step):
            g = l * 2 + G

            def products(c):
                for h in range(4):
                    kc = kT[:, 4 * G + h, tok(c)]
                    o = key_products()[h // 2][:, h % 2]
                    pe.matmul(o[:, 0, :], kc, kc, start=True, stop=True)
                    mm = pe.matmul(o[:, 1, :], kc, qT[:, 4 * G + h, tok(c)], start=True, stop=True)
                mm.then_inc(s_kkq, 1)

            def values(c, b):
                for h in range(4):
                    mm = pe.transpose(b4[b][:, h, :], vT[:, 4 * G + h, tok(c)], ident)
                mm.then_inc(s_vt, 1)
            if step == 0:
                if G:
                    pe.wait_ge(s_oblo, l * 8 + 4)
                pe.wait_ge(s_gbt, g * 2 + 2)
                pe.matmul(b4[3], ones, gt[:, 0], start=True, stop=True).then_inc(s_gb, 1)
                pe.matmul(b4[7], ones, gt[:, 1], start=True, stop=True).then_inc(s_gb, 1)
                if G:
                    pe.wait_ge(s_oev, g)
                pe.matmul(b4[4], ones, beta_at(G)[:, 0], start=True, stop=True)
                products(0)
            if step == 2:
                pe.wait_ge(s_tu, g * 16 + 1)
                pe.matmul(b4[4], ones, beta_at(G)[:, 1], start=True, stop=True)
                products(1)
                values(0, 3)
            if step == 3:
                pe.wait_ge(s_De, g * 2 + 2)
                values(1, 7)

        def decays_act(act, l, G):
            g = l * 2 + G
            act.wait_ge(s_dm, g * 2 + 1)
            act.activation(De[:, 0], De[:, 0], ACT.Exp).then_inc(s_De, 1)
            act.wait_ge(s_dm, g * 2 + 2)
            act.activation(egb[:, :, :], b4[7], ACT.Exp)
            act.activation(De[:, 1], De[:, 1], ACT.Exp).then_inc(s_De, 1)

        def decays_dve(dve, l, G, step):
            g = l * 2 + G

            def logs(c):
                dve.wait_ge(s_gb, g * 2 + (c + 1))
                for h in range(4):
                    ins = dve.scalar_tensor_tensor(
                        out=De[:, c, h, :], in0=b4[(3, 7)[c]][:, h, :],
                        scalar=small["gcum"][:, c, 4 * G + h:4 * G + h + 1], in1=C["decay_mask"],
                        op0=ALU.subtract, op1=ALU.add)
                ins.then_inc(s_dm, 1)

            def l_and_attention(c):
                dve.wait_ge(s_De, g * 2 + (c + 1))
                dve.wait_ge(s_kkq, g * 2 + (c + 1))
                for i, h in enumerate((0, 2)):
                    o = key_products()[i]
                    dve.tensor_tensor(Mi[:, c, h:h + 2, :], o[:, :, 0, :], De[:, c, h:h + 2, :], ALU.mult)
                    dve.tensor_tensor(At[:, c, h:h + 2, :], o[:, :, 1, :], De[:, c, h:h + 2, :], ALU.mult)
                dve.drain()
                dve.tensor_tensor(Mi[:, c], Mi[:, c], b4[4], ALU.mult).then_inc(s_tu, 1)

            def beta_v(c):
                dve.wait_ge(s_vt, g * 3 + (c + 1))
                dve.tensor_tensor(vT[:, heads4(G), tok(c)], b4[(3, 7)[c]], bc(small["beta"][:, c, heads4(G)], P),
                                  ALU.mult).then_inc(s_r, 1)
            if step == 0:
                dve.drain()
                for c in range(2):
                    dve.tensor_tensor(gt[:, c], over(C["triu"], 4), bc(small["graw"][:, c, heads4(G)], P), ALU.mult)
                    dve.tensor_tensor(beta_at(G)[:, c], over(ident, 4), bc(small["beta"][:, c, heads4(G)], P),
                                      ALU.mult).then_inc(s_gbt, 1)
            if step == 1:
                if G:
                    dve.wait_ge(s_o, g)
                logs(0)
                logs(1)
            if step == 2:
                l_and_attention(0)
            if step == 3:
                l_and_attention(1)
                beta_v(0)
            if step == 4:
                beta_v(1)

        STICK_STEP = {1: ("scores", 0), 2: ("sums", 0), 3: ("out", 0), 4: ("scores", 1), 5: ("sums", 1), 6: ("out", 1)}

        def delta_pe(pe, l, G):
            g = l * 2 + G
            if G:
                for step in (0, 2, 3):
                    decays_pe(pe, l, G, step)
            else:
                pe.wait_ge(s_read, l * N1 + N1)

            for c in range(2):
                pe.wait_ge(s_ms, g * 14 + (c + 1))
                for h in range(4):
                    mm = pe.transpose(b4[c][:, h, :], Ms[:, c, h, :], ident)
                mm.then_inc(s_xm, 1)
            pe.wait_ge(s_r, g * 3 + 2)
            for s in range(1, 7):
                for c in range(2):
                    pe.wait_ge(s_ms, g * 14 + (s * 2 + c + 1))
                    pe.wait_ge(s_tu, g * 16 + (s * 2 + c + 1))
                    for h in range(4):
                        mm = pe.matmul(b4[c][:, h, :], Ms[:, c, h, :], Ti[:, c, h, :], start=True, stop=True)
                    mm.then_inc(s_xm, 1)
                for c in range(2):
                    pe.wait_ge(s_xs, g * 12 + (s * 2 + c - 1))
                    for h in range(4):
                        if s < 6:
                            pe.matmul(b4[2 + c][:, h, :], Ui[:, c, h, :], Xi[:, c, h, :], start=True, stop=True)
                        mm = pe.matmul(b4[4 + c][:, h, :], Xi[:, c, h, :], Ui[:, c, h, :], start=True, stop=True)
                    mm.then_inc(s_tum, 1)
                stick_pe(pe, l, 2 * G + STICK_STEP[s][1], STICK_STEP[s][0])
            for h in range(4):
                mm = pe.transpose(b4[1][:, h, :], kT[:, 4 * G + h, tok(0)], ident)
            mm.then_inc(s_vt, 1)
            pe.wait_ge(s_tu, g * 16 + 16)
            for h in range(4):
                mm = pe.matmul(b4[0][:, h, :], Ui[:, 0, h, :], vT[:, 4 * G + h, tok(0)], start=True, stop=True)
            mm.then_inc(s_vn0m, 1)
            pe.wait_ge(s_r, g * 3 + 3)
            pe.wait_ge(s_vn0, g * 3 + 1)
            for h in range(4):
                mm = pe.matmul(b4[1][:, h, :], kT[:, 4 * G + h, tok(0)], vn0[:, h, :], start=True, stop=True)
            mm.then_inc(s_vn0m, 1)
            pe.wait_ge(s_vn0, g * 3 + 2)
            for h in range(4):
                mm = pe.matmul(b4[2][:, h, :], kT[:, 4 * G + h, tok(1)], st1[:, h, :], start=True, stop=True)
            mm.then_inc(s_vn0m, 1)
            pe.wait_ge(s_r1, g + 1)
            for h in range(4):
                mm = pe.matmul(b4[3][:, h, :], Ui[:, 1, h, :], vT[:, 4 * G + h, tok(1)], start=True, stop=True)
            mm.then_inc(s_vn0m, 1)
            pe.wait_ge(s_qd, g + 1)
            for h in range(4):
                pe.matmul(b4[4][:, h, :], vn0[:, h, :], At[:, 0, h, :], start=True, stop=True)
            pe.wait_ge(s_vn0, g * 3 + 3)
            for h in range(4):
                pe.matmul(b4[5][:, h, :], st1[:, h, :], qd[:, h, :], start=True, stop=False)
                mm = pe.matmul(b4[5][:, h, :], vn1[:, h, :], At[:, 1, h, :], start=False, stop=True)
            mm.then_inc(s_o, 1)

        def delta_act(act, po, l, G):
            g = l * 2 + G
            if G:
                decays_act(act, l, G)
            else:
                split_hi(act, po, 0)
                split_hi(act, po, 1)
            for s in range(1, 7):
                for c in range(2):
                    act.wait_ge(s_xm, g * 14 + (s * 2 + c + 1))
                    act.activation(Xi[:, c], b4[c], ACT.Copy).then_inc(s_xs, 1)
                stick_act(act, po, l, 2 * G + STICK_STEP[s][1], STICK_STEP[s][0])
                if G == 0 and s == 2:
                    split_hi(act, po, 2)
            act.wait_ge(s_vn0m, g * 4 + 1)
            act.activation(vn0, b4[0], ACT.Copy).then_inc(s_vn0, 1)
            act.wait_ge(s_vn0m, g * 4 + 2)
            act.activation(st1, b4[1], ACT.Copy).then_inc(s_vn0, 1)
            gate = gates[:, KC * G:KC * G + KC, :]
            act.activation(gate, gate, ACT.Sigmoid)
            act.wait_ge(s_vn0m, g * 4 + 4)
            act.activation(vn1, b4[3], ACT.Copy).then_inc(s_vn0, 1)
            act.wait_ge(s_o, g + 1)
            act.activation(qT[:, heads4(G), tok(0)], b4[4], ACT.Copy)
            act.activation(qT[:, heads4(G), tok(1)], b4[5], ACT.Copy).then_inc(s_oev, 1)

        def delta_dve(dve, po, l, G):
            g = l * 2 + G
            if G:
                for step in range(1, 5):
                    decays_dve(dve, l, G, step)
            else:
                split_lo(dve, po, 0)
            for c in range(2):
                dve.wait_ge(s_xm, g * 14 + (c + 1))
                dve.tensor_tensor(Ui[:, c], over(ident, 4), Ms[:, c], ALU.subtract)
                dve.tensor_tensor(Ti[:, c], over(ident, 4), b4[c], ALU.subtract).then_inc(s_tu, 1)
            if G == 0:
                split_lo(dve, po, 1)
            for s in range(1, 7):
                for c in range(2):
                    dve.wait_ge(s_tum, g * 12 + (s * 2 + c - 1))
                    if s < 6:
                        dve.tensor_tensor(Ti[:, c], Ti[:, c], b4[2 + c], ALU.subtract)
                    dve.tensor_tensor(Ui[:, c], Ui[:, c], b4[4 + c], ALU.subtract).then_inc(s_tu, 1)
                stick_dve(dve, l, 2 * G + STICK_STEP[s][1], STICK_STEP[s][0])
                if G == 0 and s == 2:
                    split_lo(dve, po, 2)
            dve.wait_ge(s_vt, g * 3 + 3)
            dve.tensor_tensor(kT[:, heads4(G), tok(0)], b4[1], bc(small["dend"][:, 0, heads4(G)], P),
                              ALU.mult).then_inc(s_r, 1)
            if G == 0:
                decays_dve(dve, l, 1, 0)
            dve.wait_ge(s_vn0m, g * 4 + 3)
            for h in range(4):
                r1 = vT[:, 4 * G + h, tok(1)]
                ins = dve.scalar_tensor_tensor(out=r1, in0=b4[2][:, h, :],
                                               scalar=small["nbeg"][:, 1, 4 * G + h:4 * G + h + 1], in1=r1,
                                               op0=ALU.mult, op1=ALU.add)
            ins.then_inc(s_r1, 1)

        def delta_pool(pool, l, G):
            g = l * 2 + G
            if G == 0:
                pool.wait_ge(s_read, l * N1 + N1)
            pool.wait_ge(s_tu, g * 16 + 2)
            for s in range(7):
                for c in range(2):
                    if s == 1:
                        pool.wait_ge(s_tu, g * 16 + (c + 3))
                    if s > 1:
                        pool.wait_ge(s_xm, g * 14 + (s * 2 + (c - 1)))
                    pool.tensor_tensor(Ms[:, c], Mi[:, c], over(C[f"level{s}"], 4), ALU.mult).then_inc(s_ms, 1)
                if s == 0:
                    pool.tensor_tensor(qd, qT[:, heads4(G), tok(1)], egb[:, :, :], ALU.mult).then_inc(s_qd, 1)

        def stick_pe(pe, l, r, step):
            for i in range(2):
                h, b, w = 2 * r + i, bank[6 + i], lg[:, 2 * (r % 2) + i, :]
                if step == "scores":
                    if i == 0:
                        pe.wait_ge(s_hnorm, l * 16 + 16)
                        if r % 2:
                            pe.wait_ge(s_oblo, l * 8 + 2 * r)
                    pe.matmul(b[:, 0:256], sk_[:, h, 0:P], sq_[:, h, :], start=True, stop=False,
                              skip_group_check=True)
                    pe.matmul(b[:, 256:384], sk_[:, h, P:T], sq_[:, h, P:T], start=False, stop=False,
                              skip_group_check=True).then_inc(s_z, 1)
                if step == "sums":
                    pe.wait_ge(s_sp, l * 8 + (h + 1))
                    for out, m, src in ((slice(0, 256), "neg_tri", w[:, 0:256]),
                                        (slice(128, 256), "neg_ones", w[:, 256:384]),
                                        (slice(256, 384), "neg_tri", w[:, 256:384]),
                                        (slice(0, 128), "ident", C["sb_neg"][:, 0:P]),
                                        (slice(256, 384), "ident", C["sb_neg"][:, 0:P])):
                        mm = pe.matmul(b[:, out], C[m], src, start=False, stop=(m == "ident"),
                                       skip_group_check=True)
                    mm.then_inc(s_R, 1)
                if step == "out":
                    pe.wait_ge(s_w, l * 8 + (h + 1))
                    v = sv[:, :, P * h:P * h + P]
                    pe.matmul(b[:, 0:256], v[:, 0, :], w[:, 0:256], start=True, stop=False, skip_group_check=True)
                    pe.matmul(b[:, 128:256], v[:, 1, :], w[:, 256:384], start=False, stop=True,
                              skip_group_check=True).then_inc(s_pv, 1)

        def stick_act(act, po, l, r, step):
            both = lg[:, 2 * (r % 2):2 * (r % 2) + 2, :]
            if step == "scores":
                if r == 0:
                    act.wait_ge(s_lo, po.base + (1 + START))
                for i in range(2):
                    act.wait_ge(s_z, l * 8 + (2 * r + i + 1))
                    if r >= 2:
                        act.wait_ge(s_pv, l * 8 + (2 * r + i - 3))
                    act.activation(both[:, i, :], bank[6 + i][:, 0:384], ACT.Abs)
                act.drain()
                act.activation(both, both, ACT.Exp, scale=-1.0)
                act.drain()
                act.activation(both, both, ACT.Ln, bias=eps_col[:, 2:3]).then_inc(s_ln, 1)
            for i in range(2):
                h = 2 * r + i
                if step == "sums":
                    act.wait_ge(s_R, l * 8 + (h + 1))
                    act.activation(both[:, i, :], bank[6 + i][:, 0:384], ACT.Exp).then_inc(s_w, 1)
                if step == "out":
                    act.wait_ge(s_pv, l * 8 + (h + 1))
                    act.activation(ob_hi[:, h, :], bank[6 + i][:, 0:256], ACT.Copy).then_inc(s_obhi, 1)

        def stick_dve(dve, l, r, step):
            if step == "scores":
                dve.wait_ge(s_ln, l * 4 + (r + 1))
                for i in range(2):
                    w = lg[:, 2 * (r % 2) + i, :]
                    dve.scalar_tensor_tensor(out=w, in0=bank[6 + i][:, 0:384], scalar=0.0, in1=w,
                                             op0=ALU.max, op1=ALU.add)
                dve.drain()
                for i in range(2):
                    w = lg[:, 2 * (r % 2) + i, :].rearrange("p (a n) -> p a n", a=3)[:, 0:3:2, :]
                    dve.tensor_tensor(w, w, over(C["sb_mask"][:, 0:P], 2), ALU.mult).then_inc(s_sp, 1)
            if step == "out":
                for i in range(2):
                    h = 2 * r + i
                    dve.wait_ge(s_obhi, l * 8 + (h + 1))
                    dve.tensor_tensor(ob_lo[:, h, :], bank[6 + i][:, 0:256], ob_hi[:, h, :].bitcast(F32),
                                      ALU.subtract).then_inc(s_oblo, 1)

        def out1_pe(pe, po, l):
            def onorm_sums(g):
                pe.wait_ge(s_osq, l * 2 + (g + 1))
                for i in range(8 * g, 8 * g + 8):
                    mm = pe.matmul(bank[6][:, i:i + 1], osq[:, i // 2, P * (i % 2):P * (i % 2) + P], ones[:, 0:1],
                                   start=(i == 0), stop=(i % 8 == 7), skip_group_check=True)
                mm.then_inc(s_oss, 1)

            def onorm_rows(i):
                pe.wait_ge(s_odiag, l * 4 + (i + 1))
                pe.matmul(bank[4 + i][:, :], ones, odiag[i % 2][:, :, :], start=True, stop=True).then_inc(s_orow, 1)
            pe.wait_ge(s_oblo, l * 8 + 8)
            for i in range(4):
                pe.wait_ge(s_lo, po.base + (i + 1 + START))
                features(pe, i % RING, pair[i], ob_hi, ob_lo).then_inc(s_used, 1)
                if i == 0:
                    pe.wait_ge(s_oev, l * 2 + 2)
                    onorm_sums(0)
                    onorm_sums(1)
                if i == 1:
                    onorm_rows(0)
                    onorm_rows(1)
                if i > 1:
                    onorm_rows(i)
            by_tiles(pe, po, 4, pair[4], oa_hi, oa_lo, s_oalo, l * 4)
            for j in range(5, 8):
                pe.wait_ge(s_lo, po.base + (j + 1 + START))
                features(pe, j % RING, pair[j], oa_hi, oa_lo).then_inc(s_used, 1)
            by_tiles(pe, po, 8, pair[4], xn_hi, xn_lo, s_mlo, l * 4)
            for j in range(9, 12):
                pe.wait_ge(s_lo, po.base + (j + 1 + START))
                features(pe, j % RING, pair[j - 4], xn_hi, xn_lo).then_inc(s_used, 1)

        def out1_act(act, po, l):
            act.drain()
            for g in range(2):
                act.activation(osq[:, 4 * g:4 * g + 4, :], qT[:, 4 * g:4 * g + 4, :], ACT.Square).then_inc(s_osq, 1)
            split_hi(act, po, 3)
            act.wait_ge(s_oss, l * 2 + 2)
            act.activation(oroot[:, :], bank[6][:, 0:2 * HEADS], ACT.Sqrt, bias=eps_col[:, 0:1],
                           scale=1.0 / P).then_inc(s_oroot, 1)
            for i in range(4):
                act.wait_ge(s_oa, l * 4 + (i + 1))
                act.activation(oa_hi[:, 2 * i:2 * i + 2, :], zs[:, 2 * i:2 * i + 2, :], ACT.Copy).then_inc(s_oahi, 1)
                if i:
                    split_hi(act, po, 3 + i)
            split_hi(act, po, 7)
            for i in range(4):
                act.wait_ge(s_mg, l * 4 + (i + 1))
                act.activation(xn_hi[:, 2 * i:2 * i + 2, :], merged[:, 2 * i:2 * i + 2, :],
                               ACT.Copy).then_inc(s_mhi, 1)
                if i:
                    split_hi(act, po, 7 + i)
            split_hi(act, po, 11)

        def out1_dve(dve, po, l):
            dve.wait_ge(s_oroot, l + 1)
            dve.reciprocal(oinv[:, :], oroot[:, :])
            dve.drain()

            def diagonal(i):
                if i >= 2:
                    dve.wait_ge(s_orow, l * 4 + (i - 1))
                dve.tensor_tensor(odiag[i % 2][:, :, :], over(ident, 4), bc(oinv[:, 4 * i:4 * i + 4], P),
                                  ALU.mult).then_inc(s_odiag, 1)
            diagonal(0)
            diagonal(1)
            for i in range(4):
                s = slice(2 * i, 2 * i + 2)
                dve.wait_ge(s_orow, l * 4 + (i + 1))
                dve.tensor_tensor(qT[:, s, :], qT[:, s, :], pair[4 + i], ALU.mult)
                dve.drain()
                dve.scalar_tensor_tensor(out=zs[:, s, :], in0=qT[:, s, :], scalar=vec[:, V_DN_OUT:V_DN_OUT + 1],
                                         in1=zs[:, s, :], op0=ALU.mult, op1=ALU.mult).then_inc(s_oa, 1)
                if i < 2:
                    diagonal(i + 2)
                sb = slice(8 + 2 * i, 10 + 2 * i)
                dve.wait_ge(s_used, po.base + (i + 1 + START))
                dve.tensor_tensor(gates[:, sb, :], pair[i], gates[:, sb, :], ALU.mult)
                dve.wait_ge(s_oahi, l * 4 + (i + 1))
                dve.tensor_tensor(oa_lo[:, s, :], zs[:, s, :], oa_hi[:, s, :].bitcast(F32),
                                  ALU.subtract).then_inc(s_oalo, 1)
                if i == 2:
                    dve.wait_ge(s_lo, po.base + (5 + START))
                    split_lo(dve, po, 5)
            split_lo(dve, po, 6)
            split_lo(dve, po, 7)
            dve.drain()
            for i in range(4):
                s = slice(2 * i, 2 * i + 2)
                dve.wait_ge(s_used, po.base + (i + 5 + START))
                dve.tensor_tensor(gates[:, s, :], pair[4 + i], gates[:, s, :], ALU.mult)
                dve.drain()
                dve.tensor_tensor(merged[:, s, :], gates[:, s, :], gates[:, 8 + 2 * i:10 + 2 * i, :],
                                  ALU.add).then_inc(s_mg, 1)
                dve.wait_ge(s_mhi, l * 4 + (i + 1))
                dve.tensor_tensor(xn_lo[:, s, :], merged[:, s, :], xn_hi[:, s, :].bitcast(F32),
                                  ALU.subtract).then_inc(s_mlo, 1)
                if i:
                    split_lo(dve, po, 7 + i)
            split_lo(dve, po, 11)
            for i in range(4):
                s = slice(2 * i, 2 * i + 2)
                dve.wait_ge(s_used, po.base + (9 + i + START))
                dve.tensor_tensor(x[:, s, :], pair[4 + i], x[:, s, :], ALU.add).then_inc(s_x, 1)

        def mixer1_pe(pe, pm, po, q, l):
            mixer1_proj_pe(pe, pm, q, l)
            for G in range(2):
                delta_pe(pe, l, G)
            out1_pe(pe, po, l)

        def mixer1_act(act, pm, po, q, l):
            mixer1_proj_act(act, pm, q, l)
            for G in range(2):
                delta_act(act, po, l, G)
            out1_act(act, po, l)

        def mixer1_dve(dve, pm, po, q, l):
            mixer1_proj_dve(dve, pm, q, l)
            for G in range(2):
                delta_dve(dve, po, l, G)
            out1_dve(dve, po, l)

        def mixer1_pool(pool, po, l):
            for G in range(2):
                delta_pool(pool, l, G)
            split_lo(pool, po, 3)
            split_lo(pool, po, 4)

        mixer_sp, mixer_pe, mixer_act, mixer_dve = [mixer1_sp], [mixer1_pe], [mixer1_act], [mixer1_dve]

        slopes = [2.0 ** (-8.0 * (i + 1) / 18) for i in range(18)]
        gates2 = put("gates2", [3 * KC, T], at=shared)
        v2 = put("values2", [NT, 24 * 64], at=shared + 24576)
        mob = put("moba_qk", [6, T], at=shared + 36864)
        dil = put("dil_qk", [12, T], at=shared + 43008)
        qm = put("mla_q", [6, T], at=shared + 55296)
        km = put("mla_k", [6, T], at=shared + 61440)
        o_mob = [put(f"o_mob{i}", [3, T], F32R, at=shared + 67584 + 3072 * i) for i in range(2)]
        o_mla = [put(f"o_mla{i}", [3, T], F32R, at=shared + 73728 + 3072 * i) for i in range(2)]
        o_dil = [put(f"o_dil{i}", [2, T], F32R, at=shared + 36864 + 2048 * i) for i in range(2)]
        turned = put("turned", [2, T], at=shared + 40960)
        S = put("scores", [3, 384], at=shared + 79872)
        PT = put("probs_t", [3, 384], at=shared + 84480)
        kr = put("mla_k_rope", [T], at=shared + 89088)
        stat_at = shared + 90112
        nmax = put("neg_max", [2], at=stat_at)
        den = put("denominator", [2], at=stat_at + 64)
        rden = put("reciprocal", [2], at=stat_at + 128)
        latent = put("latent", [3, T], at=shared + 55296)
        lsq = put("latent_sq", [3, T], at=shared + 58368)
        lroot = put("latent_root", [2, T], at=shared + 61440)
        linv = put("latent_inv", [2, T], at=shared + 63488)
        c_hi = put("latent_hi", [3, T], F32R, at=shared + 73728)
        c_lo = put("latent_lo", [3, T], F32R, at=shared + 76800)
        merged2 = put("merged2", [KC, T], at=shared + 43008)
        part = [put(f"part{i}", [2, T], at=shared + 55296 + 2048 * i) for i in range(6)]

        s2_read = sem("proj2_read")
        s_lsq = sem("latent_squares")
        s_lss = sem("latent_sums")
        s_lroot = sem("latent_root")
        s_lat = sem("latent_normed")
        s_lhi = sem("latent_upper")
        s_llo = sem("latent_lower")
        s_up = sem("up_products")
        s_upr = sem("up_read")
        s_turn = sem("turned_pe")
        s_rope = sem("rope_done")
        s_A = sem("unit_scores")
        s_B = sem("unit_max")
        s_C = sem("unit_exp")
        s_D = sem("unit_probs")
        s_E = sem("unit_transposed")
        s_F = sem("unit_copied")
        s_G = sem("unit_out")
        s_H = sem("unit_out_hi")
        s_L = sem("unit_out_lo")
        s2_mg = sem("merged2_ready")
        s2_mhi = sem("merged2_upper")
        s2_mlo = sem("merged2_lower")
        N2 = len(MIX2)
        UP = 16

        def unit_plan():
            units = []
            for h in range(6):
                lo = 64 * (h % 2)
                units.append((8 + h, [(mob[lo:lo + 64, h // 2, :], mob[lo:lo + 64, 3 + h // 2, :], 384 + 64 * h,
                                       "all", slopes[12 + h])], o_mob, h // 2))
            for h in range(6):
                units.append((UP + 2 + h, [(qm[0:96, h, :], km[0:96, h, :], 64 * h, "causal", 1.0)], o_mla, h // 2))
            for i in range(4):
                heads = []
                for g, table in enumerate(("window", "step4", "step16")):
                    h = 4 * g + i
                    lo = 64 * (h % 2)
                    heads.append((dil[lo:lo + 64, h // 2, :], dil[lo:lo + 64, 6 + h // 2, :], 768 + 64 * h, table,
                                  slopes[h]))
                units.append((UP + 8 + i, heads, o_dil, i // 2))
            return units
        units = unit_plan()

        def unit_at(j):
            return [n for n, u in enumerate(units) if u[0] == j]

        def mixer2_sp(sp, pm, po, l):
            def proj(kind, at, slot):
                if kind == "up":
                    return [(slot_view(slot, 2, 576), rows(a["w_uq_2"][l])),
                            (slot[:, 1152:1920], a["w_ukv_2"][l])]
                n = 128 if kind == "mv2" else 256
                return [(slot_view(slot, KC, n), cols(a["w_in_2"][l], at, n))]

            def way_out(kind, at, slot):
                v = slot_view(slot, KC, 256)
                if kind == "out":
                    return [(v, cols(a["w_out_2"][l], at))]
                return [(v[:, 0:3, :], cols(a["w_br_mla_2"][l], at)), (v[:, 3:6, :], cols(a["w_br_moba_2"][l], at)),
                        (v[:, 6:8, :], cols(a["w_br_dil_2"][l], at))]
            bring_phase(sp, pm, proj)
            bring_phase(sp, po, way_out)

        def scores_pe(pe, l, n):
            if n:
                pe.wait_ge(s_B, l * 16 + n)
            if n == 6:
                pe.wait_ge(s_rope, l * 4 + 4)
            for b, (q, k, _, _, _) in enumerate(units[n][1]):
                if b == 1:
                    pe.wait_ge(s_F, l * 16 + n)
                pe.matmul(bank[3 + b][:, 0:P], q[:, 0:P], k[:, 0:P], start=True, stop=True)
                mm = pe.matmul(bank[3 + b][:, P:384], q[:, P:T], k[:, 0:T], start=True, stop=True)
            mm.then_inc(s_A, 1)

        T_BANK = (6, 4, 5)

        def transposes_pe(pe, l, n):
            pe.wait_ge(s_D, l * 16 + (n + 1))
            for b in range(len(units[n][1])):
                for i in range(3):
                    mm = pe.transpose(bank[T_BANK[b]][:, P * i:P * i + P], S[:, b, P * i:P * i + P], ident)
            mm.then_inc(s_E, 1)

        def values_pe(pe, l, n):
            _, heads, _, _ = units[n]
            lo = 64 * (n % 2)
            if n >= 2 and n % 2 == 0:
                pe.wait_ge(s_L, l * 8 + n // 2)
            pe.wait_ge(s_F, l * 16 + (n + 1))
            for b, (_, _, v, _, _) in enumerate(heads):
                last = b == len(heads) - 1
                pe.matmul(bank[7][lo:lo + 64, 0:T], v2[:, 0, v:v + 64], PT[:, b, 0:T], start=(b == 0), stop=False,
                          skip_group_check=True)
                mm = pe.matmul(bank[7][lo:lo + 64, P:T], v2[:, 1, v:v + 64], PT[:, b, T:384], start=False, stop=last,
                               skip_group_check=True)
            mm.then_inc(s_G, 1)

        def exp_act(act, l, n):
            k = len(units[n][1])
            act.wait_ge(s_B, l * 16 + (n + 1))
            act.activation(S[:, 0:k, 0:P], S[:, 0:k, 0:P], ACT.Exp, bias=nmax[:, 0:1], accum_out=den[:, 0:1])
            act.activation(S[:, 0:k, P:384], S[:, 0:k, P:384], ACT.Exp, bias=nmax[:, 1:2],
                           accum_out=den[:, 1:2]).then_inc(s_C, 1)

        def copy_act(act, l, n):
            act.wait_ge(s_E, l * 16 + (n + 1))
            for b in range(len(units[n][1])):
                ins = act.activation(PT[:, b, :], bank[T_BANK[b]][:, 0:384], ACT.Copy)
            ins.then_inc(s_F, 1)

        def out_hi_act(act, l, n):
            act.wait_ge(s_G, l * 16 + (n + 1))
            act.activation(units[n][2][0][:, units[n][3], :], bank[7][:, 0:T], ACT.Copy).then_inc(s_H, 1)

        def out_lo_dve(dve, l, n):
            hi, lo = units[n][2]
            i = units[n][3]
            dve.wait_ge(s_H, l * 8 + (n // 2 + 1))
            dve.tensor_tensor(lo[:, i, :], bank[7][:, 0:T], hi[:, i, :].bitcast(F32), ALU.subtract).then_inc(s_L, 1)

        def max_dve(dve, l, n):
            heads = units[n][1]
            k = len(heads)
            dve.wait_ge(s_A, l * 16 + (n + 1))
            for b, (_, _, _, table, slope) in enumerate(heads):
                dve.scalar_tensor_tensor(out=S[:, b, :], in0=C[table], scalar=float(slope), in1=bank[3 + b][:, 0:384],
                                         op0=ALU.mult, op1=ALU.add)
            dve.drain()
            axis = AX.X if k == 1 else AX.XY
            cut = (lambda s: S[:, 0, s]) if k == 1 else (lambda s: S[:, 0:k, s])
            dve.tensor_reduce(nmax[:, 0:1], cut(slice(0, P)), axis, ALU.max, negate=True)
            dve.tensor_reduce(nmax[:, 1:2], cut(slice(P, 384)), axis, ALU.max, negate=True).then_inc(s_B, 1)

        def probs_dve(dve, l, n):
            k = len(units[n][1])
            dve.wait_ge(s_C, l * 16 + (n + 1))
            dve.reciprocal(rden[:, :], den[:, :])
            dve.drain()
            dve.tensor_scalar(S[:, 0:k, 0:P], S[:, 0:k, 0:P], rden[:, 0:1], None, ALU.mult)
            dve.tensor_scalar(S[:, 0:k, P:384], S[:, 0:k, P:384], rden[:, 1:2], None, ALU.mult).then_inc(s_D, 1)

        def mixer2_pe(pe, pm, po, q, l):
            norm_pe(pe, q)
            first_item(pe, pm, q)
            for j, (kind, _) in enumerate(MIX2):
                if j == 0:
                    continue
                slot = j % RING
                pe.wait_ge(s_lo, pm.base + (j + 1 + START))
                if kind == "up":
                    up_pe(pe, l)
                    continue
                if j >= RING:
                    done = sum(1 for i in range(j - 2) if i != UP)
                    pe.wait_ge(s2_read, l * (N2 - 1) + done)
                for half in range(2):
                    mm = project2(pe, kind, slot, half)
                    if half == 1:
                        mm.then_inc(s_used, 1)
                    if half == 0:
                        for n in unit_at(j - 2):
                            values_pe(pe, l, n)
                for n in unit_at(j - 1):
                    transposes_pe(pe, l, n)
                for n in unit_at(j):
                    scores_pe(pe, l, n)
                if j == 3:
                    pe.wait_ge(s_lsq, l + 1)
                    pe.matmul(bank[7][:, 0:T], ones, lsq[:, 0, :], start=True, stop=False)
                    pe.matmul(bank[7][:, 0:T], ones, lsq[:, 1, :], start=False, stop=True)
                    pe.matmul(bank[7][:, T:2 * T], ones, lsq[:, 2, :], start=True, stop=True).then_inc(s_lss, 1)
                if j == UP + 1:
                    turn = C["turn"][0:96, :]
                    pe.wait_ge(s_upr, l * 8 + 8)
                    pe.matmul(bank[3][0:96, 0:T], turn, kr[0:96, :], start=True, stop=True).then_inc(s_turn, 1)
                    for i in range(3):
                        pe.matmul(bank[4 + i][0:96, :], turn, qm[0:96, 2 * i:2 * i + 2, :], start=True,
                                  stop=True).then_inc(s_turn, 1)
            out2_pe(pe, po, l)

        def project2(pe, kind, slot, half):
            n = 128 if kind == "mv2" else 256
            hi, lo = slot_view(w_hi[slot], KC, n), slot_view(w_lo[slot], KC, n)
            out = pair[slot][:, half, 0:n] if kind in ("mv", "mv2", "dv") else pair[slot][:, half, :]
            for kc in range(KC):
                if kind in ("mv", "mv2", "dv"):
                    tk = slice(P * half, P * half + P)
                    mm = product(pe, out, xn_hi[:, kc, tk], xn_lo[:, kc, tk], hi[:, kc, :], lo[:, kc, :],
                                 kc == 0, kc == KC - 1)
                else:
                    at = 64 if kind == "ckv" and half else P * half
                    mm = product(pe, out, hi[:, kc, at:at + P], lo[:, kc, at:at + P], xn_hi[:, kc, :],
                                 xn_lo[:, kc, :], kc == 0, kc == KC - 1)
            return mm

        def up_pe(pe, l):
            slot = UP % RING
            pe.wait_ge(s_llo, l + 1)
            pe.wait_ge(s_L, l * 8 + 3)
            def window(t, at):
                return t[slot][:, at:at + P]
            for i in range(6):
                b = (3, 4, 5, 6, 7, 3)[i]
                if i == 5:
                    pe.wait_ge(s_upr, l * 8 + 1)
                for hh in range(2):
                    h = 2 * (i % 3) + hh
                    out = pair[b][:, hh, :]
                    if i < 3:
                        for kc in range(2):
                            at = 576 * kc + 96 * h
                            mm = product(pe, out, window(w_hi, at), window(w_lo, at), c_hi[:, kc, :], c_lo[:, kc, :],
                                         kc == 0, kc == 1)
                    else:
                        at = 1152 + P * h
                        mm = product(pe, out, window(w_hi, at), window(w_lo, at), c_hi[:, 2, :], c_lo[:, 2, :],
                                     True, True)
                mm.then_inc(s_up, 1)
            for t in range(NT):
                pe.wait_ge(s_upr, l * 8 + (t + 2))
                w = [x_[slot][:, 1152:1920].rearrange("p (h n) -> p h n", h=6)[:, :, 64:128] for x_ in (w_hi, w_lo)]
                tk = slice(P * t, P * t + P)
                mm = product(pe, bank[4 + t][:, 0:384].rearrange("p (h n) -> p h n", h=6), c_hi[:, 2, tk],
                             c_lo[:, 2, tk], w[0], w[1], True, True)
                mm.then_inc(s_used if t else s_up, 1)

        def mixer2_act(act, pm, po, q, l):
            norm_act(act, pm, q)
            for j, (kind, _) in enumerate(MIX2):
                b = pair[j % RING]
                if j == N2 - 1:
                    split_hi(act, po, 0)
                if kind == "up":
                    for i in range(8):
                        if i < 7:
                            act.wait_ge(s_up, l * 7 + (i + 1))
                        else:
                            act.wait_ge(s_used, pm.base + (j + 1 + START))
                        if i < 6:
                            dst, src = (qm, km)[i // 3], pair[(3, 4, 5, 6, 7, 3)[i]]
                            act.activation(dst[:, 2 * (i % 3):2 * (i % 3) + 2, :], src, ACT.Copy).then_inc(s_upr, 1)
                        else:
                            act.activation(v2[:, i - 6, 0:384], bank[i - 2][:, 0:384], ACT.Copy).then_inc(s_upr, 1)
                else:
                    act.wait_ge(s_used, pm.base + (j + 1 + START))
                    if kind == "cq":
                        act.activation(latent[:, 0:2, :], b, ACT.Copy)
                        ins = act.activation(lsq[:, 0:2, :], b, ACT.Square)
                    elif kind == "ckv":
                        act.activation(latent[:, 2, :], b[:, 0, :], ACT.Copy)
                        act.activation(lsq[:, 2, :], b[:, 0, :], ACT.Square).then_inc(s_lsq, 1)
                        ins = act.activation(kr[:, :], b[:, 1, :], ACT.Copy)
                    elif kind == "mob":
                        for c in range(2):
                            t = 2 * (j - 2) + c
                            ins = act.activation(mob[:, t, :], b[:, c, :], ACT.Copy, scale=0.125 if t < 3 else 1.0)
                    elif kind == "dil":
                        t = 2 * (j - 7)
                        ins = act.activation(dil[:, t:t + 2, :], b, ACT.Copy, scale=0.125 if t < 6 else 1.0)
                    elif kind in ("mv", "mv2", "dv"):
                        n = 128 if kind == "mv2" else 256
                        at = {"mv": 384, "mv2": 640}.get(kind, 768 + 256 * (j - 13))
                        ins = act.activation(v2[:, :, at:at + n], b[:, :, 0:n], ACT.Copy)
                    else:
                        t = 2 * (j - UP - 1)
                        ins = act.activation(gates2[:, t:t + 2, :], b, ACT.Copy)
                    ins.then_inc(s2_read, 1)
                for n in unit_at(j - 2):
                    if n % 2:
                        out_hi_act(act, l, n)
                for n in unit_at(j - 1):
                    copy_act(act, l, n)
                for n in unit_at(j):
                    exp_act(act, l, n)
                if j + 3 < N2:
                    split_hi(act, pm, j + 3)
                if j == 3:
                    act.wait_ge(s_lss, l + 1)
                    act.activation(lroot[:, 0, :], bank[7][:, 0:T], ACT.Sqrt, bias=eps_col[:, 3:4], scale=96.0 / 256)
                    act.activation(lroot[:, 1, :], bank[7][:, T:2 * T], ACT.Sqrt, bias=eps_col[:, 0:1],
                                   scale=1.0 / P).then_inc(s_lroot, 1)
                if j == 5:
                    act.wait_ge(s_lat, l + 1)
                    act.activation(c_hi[:, :, :], latent[:, :, :], ACT.Copy).then_inc(s_lhi, 1)
            out2_act(act, po, l)

        def mixer2_dve(dve, pm, po, q, l):
            norm_dve(dve, pm, q, V_MIX)
            for j, (kind, _) in enumerate(MIX2):
                if j == N2 - 1:
                    split_lo(dve, po, 0)
                for n in unit_at(j - 2):
                    if n % 2:
                        out_lo_dve(dve, l, n)
                if j == UP + 1:
                    for i in range(4):
                        if i:
                            dve.drain()
                        dve.wait_ge(s_turn, l * 4 + (i + 1))
                        m = 1 if i == 0 else 2
                        t = kr[0:96, :].unsqueeze(1) if i == 0 else qm[0:96, 2 * i - 2:2 * i, :]
                        src = pair[3 + i][0:96, 0:m, :]
                        dve.tensor_tensor(turned[0:96, 0:m, :], src, over(C["sin"], m)[0:96], ALU.mult)
                        dve.tensor_tensor(t, t, over(C["cos"], m)[0:96], ALU.mult)
                        dve.drain()
                        ins = dve.tensor_tensor(t, t, turned[0:96, 0:m, :], ALU.add)
                        if i == 0:
                            dve.drain()
                            ins = dve.tensor_copy(km[64:96, :, :], kr[64:96, :].unsqueeze(1).to_broadcast([32, 6, T]))
                        ins.then_inc(s_rope, 1)
                for n in unit_at(j):
                    max_dve(dve, l, n)
                    probs_dve(dve, l, n)
                if j + 3 < N2:
                    split_lo(dve, pm, j + 3)
                if j == 3:
                    dve.wait_ge(s_lroot, l + 1)
                    dve.reciprocal(linv[:, :, :], lroot[:, :, :])
                    dve.drain()
                    for i in range(3):
                        ins = dve.scalar_tensor_tensor(out=latent[:, i, :], in0=latent[:, i, :],
                                                       scalar=vec[:, V_QN + i:V_QN + i + 1], in1=linv[:, i // 2, :],
                                                       op0=ALU.mult, op1=ALU.mult)
                    ins.then_inc(s_lat, 1)
                if j == 5:
                    dve.wait_ge(s_lhi, l + 1)
                    dve.tensor_tensor(c_lo[:, :, :], latent[:, :, :], c_hi[:, :, :].bitcast(F32),
                                      ALU.subtract).then_inc(s_llo, 1)
            out2_dve(dve, po, l)

        def out2_pe(pe, po, l):
            outs = ((o_mla, 0, 3), (o_mob, 3, 3), (o_dil, 6, 2))
            pe.wait_ge(s2_read, l * (N2 - 1) + (N2 - 1))
            for j in range(4):
                pe.wait_ge(s_lo, po.base + (j + 1 + START))
                if j >= 2:
                    pe.wait_ge(s2_mg, l * 4 + (j - 1))
                for b, ((hi, lo), k0, k) in enumerate(outs):
                    if j == 0 and b == 2:
                        values_pe(pe, l, 15)
                        pe.wait_ge(s_L, l * 8 + 8)
                    mm = features(pe, j % RING, pair[3 * (j % 2) + b], hi, lo, k=k, off=256 * k0)
                mm.then_inc(s_used, 1)
            by_tiles(pe, po, 4, pair[6], xn_hi, xn_lo, s2_mlo, l * 4)
            for j in range(5, 8):
                pe.wait_ge(s_lo, po.base + (j + 1 + START))
                features(pe, j % RING, pair[(6, 7, 0, 1)[j - 4]], xn_hi, xn_lo).then_inc(s_used, 1)

        def out2_act(act, po, l):
            def sigmoid(j):
                gate = gates2[:, :, :].rearrange("p (i k) t -> p i (k t)", i=3)[:, :, 2 * T * j:2 * T * j + 2 * T]
                act.activation(gate, gate, ACT.Sigmoid).then_inc(s2_gate, 1)
            split_hi(act, po, 1)
            out_hi_act(act, l, 15)
            act.drain()
            sigmoid(0)
            split_hi(act, po, 2)
            for j in range(1, 4):
                sigmoid(j)
            for j in range(5):
                split_hi(act, po, j + 3)
                if j < 4:
                    s = slice(2 * j, 2 * j + 2)
                    act.wait_ge(s2_mg, l * 4 + (j + 1))
                    act.activation(xn_hi[:, s, :], merged2[:, s, :], ACT.Copy).then_inc(s2_mhi, 1)

        def out2_dve(dve, po, l):
            split_lo(dve, po, 1)
            out_lo_dve(dve, l, 15)
            split_lo(dve, po, 2)
            for j in range(4):
                s = slice(2 * j, 2 * j + 2)
                dve.wait_ge(s2_gate, l * 4 + (j + 1))
                dve.wait_ge(s_used, po.base + (j + 1 + START))
                p = part[3 * (j % 2):3 * (j % 2) + 3]
                for i in range(3):
                    dve.tensor_tensor(p[i][:, :, :], pair[3 * (j % 2) + i],
                                      gates2[:, KC * i + 2 * j:KC * i + 2 * j + 2, :], ALU.mult)
                dve.drain()
                dve.tensor_tensor(p[0][:, :, :], p[0][:, :, :], p[1][:, :, :], ALU.add)
                dve.drain()
                dve.tensor_tensor(merged2[:, s, :], p[0][:, :, :], p[2][:, :, :], ALU.add).then_inc(s2_mg, 1)
                dve.wait_ge(s2_mhi, l * 4 + (j + 1))
                dve.tensor_tensor(xn_lo[:, s, :], merged2[:, s, :], xn_hi[:, s, :].bitcast(F32),
                                  ALU.subtract).then_inc(s2_mlo, 1)
                if j >= 2:
                    if j == 2:
                        dve.wait_ge(s_lo, po.base + (5 + START))
                    split_lo(dve, po, j + 3)
            split_lo(dve, po, 7)
            for i in range(4):
                s = slice(2 * i, 2 * i + 2)
                dve.wait_ge(s_used, po.base + (5 + i + START))
                dve.tensor_tensor(x[:, s, :], pair[(6, 7, 0, 1)[i]], x[:, s, :], ALU.add).then_inc(s_x, 1)

        s2_gate = sem("gates2_ready")
        mixer_sp.append(mixer2_sp)
        mixer_pe.append(mixer2_pe)
        mixer_act.append(mixer2_act)
        mixer_dve.append(mixer2_dve)

        W = a
        ffn_weights = {
            (0, 0): lambda l: (W["ffn1_w_in"][l], 0, W["ffn1_w_in"][l], F, W["ffn1_w_out"][l]),
            (0, 1): lambda l: (W["ffn2_w_in"][l], 0, W["ffn2_w_in"][l], F, W["ffn2_w_out"][l]),
            (1, 0): lambda l: (W["ffn1_w_gate_2"][l], 0, W["ffn1_w_up_2"][l], 0, W["ffn1_w_down_2"][l]),
            (1, 1): lambda l: (W["ffn2_w_gate_2"][l], 0, W["ffn2_w_up_2"][l], 0, W["ffn2_w_down_2"][l]),
        }
        gain_rows = {0: [("ffn1_norm", KC), ("mix_norm", KC), ("ffn2_norm", KC), ("dn_out_norm", 1),
                         ("sb_q_norm", 1), ("sb_k_norm", 1)],
                     1: [("ffn1_norm_2", KC), ("mix_norm_2", KC), ("ffn2_norm_2", KC), ("q_norm_2", 2),
                         ("kv_norm_2", 1)]}

        block = ctx.enter_context(nc.Block())

        @block.sync
        def _(sp):
            sp.dma_start(consts[:, 0:2 * P], consts_dram[:, 0:2 * P]).then_inc(s_const, 16)
            sp.dma_start(stage[:, :, :], W["x"].rearrange("b (t p) d -> p (b t) d", p=P)).then_inc(s_const, 16)
            for b in blocks:
                with sp.Fori(0, LAYERS, 1) as l:
                    ffn_sp(sp, in_layer(plans[b], 0, l), *ffn_weights[b, 0](l))
                    mixer_sp[b](sp, in_layer(plans[b], 1, l), in_layer(plans[b], 2, l), l)
                    ffn_sp(sp, in_layer(plans[b], 3, l), *ffn_weights[b, 1](l))
            for t in range(NT):
                sp.wait_ge(s_y, 2 * t + 2)
                sp.dma_start(out_dram.rearrange("b (t p) d -> p (b t) d", p=P)[:, t, :],
                             stage[:, t, :]).then_inc(s_stored, 16)
            sp.wait_ge(s_stored, 16 * NT)

        @block.tensor
        def _(pe):
            pe.wait_ge(s_const, 32)
            for g in range(4):
                if g >= 2:
                    pe.wait_ge(s_x, g - 1)
                for kc in (2 * g, 2 * g + 1):
                    for t in range(NT):
                        mm = pe.transpose(pair[g % 2][:, kc % 2, P * t:P * t + P],
                                          stage[:, t, P * kc:P * kc + P], ident)
                mm.then_inc(s_xT, 1)
            pe.wait_ge(s_gains, 16 * n_gains)
            for b in range(4):
                n = ROWS1 if b < 2 else ROWS2
                pe.transpose(bank[7][:, P * b:P * b + n], vrows[0:n, b, :],
                             ident[0:n, 0:n]).then_inc(s_used if b < START else s_vT, 1)
            for b in blocks:
                with pe.Fori(0, LAYERS, 1) as l:
                    ffn_pe(pe, in_layer(plans[b], 0, l), norm_index(b, l, 0), ffn_index(b, l, 0))
                    mixer_pe[b](pe, in_layer(plans[b], 1, l), in_layer(plans[b], 2, l), norm_index(b, l, 1), l)
                    ffn_pe(pe, in_layer(plans[b], 3, l), norm_index(b, l, 2),
                           ffn_index(b, l, 1))
            q = last_norm
            norm_pe(pe, q)
            for g in range(4):
                t, h = g // 2, g % 2
                pe.wait_ge(s_xn, q * KC + (4 * h + 4))
                for kc in range(4):
                    mm = pe.transpose(bank[g][:, P * kc:P * kc + P], work[:, 4 * h + kc, P * t:P * t + P], ident)
                mm.then_inc(s_yT, 1)

        @block.scalar
        def _(act):
            for b in (0, 1):
                at = 0
                for name, n in gain_rows[b]:
                    act.dma_start(vrows[at:at + n, 2 * b:2 * b + 2, :],
                                  W[name].rearrange("l (k p) -> k l p", p=P)).then_inc(s_gains, 16)
                    at += n
                if b == 0:
                    act.dma_start(vrows[at:at + 96, 0:2, :],
                                  W["dn_conv_w"].rearrange("l j (k p) -> (j k) l p", p=P)).then_inc(s_gains, 16)
                else:
                    act.dma_start(vrows[at:at + KC, 3, :],
                                  W["final_norm_2"].rearrange("(k p) -> k p", p=P)).then_inc(s_gains, 16)
                    act.dma_start(vrows[at:at + KC, 2, :],
                                  W["final_norm_2"].rearrange("(k p) -> k p", p=P)).then_inc(s_gains, 16)
            for i, name in enumerate(("dn_dt_bias", "dn_a_log")):
                act.dma_start(dta[:, :, i, :], W[name].partition_broadcast(P)).then_inc(s_rest, 16)
            act.dma_start(consts[:, 2 * P:ncol], consts_dram[:, 2 * P:ncol]).then_inc(s_rest, 16)
            act.wait_ge(s_setup, 1)
            for b in blocks:
                with act.Fori(0, LAYERS, 1) as l:
                    ffn_act(act, in_layer(plans[b], 0, l), norm_index(b, l, 0), ffn_index(b, l, 0))
                    mixer_act[b](act, in_layer(plans[b], 1, l), in_layer(plans[b], 2, l), norm_index(b, l, 1), l)
                    ffn_act(act, in_layer(plans[b], 3, l), norm_index(b, l, 2),
                            ffn_index(b, l, 1))
            q = last_norm
            for g in range(4):
                act.wait_ge(s_x, 4 * q + g + 1)
                act.activation(work[:, 2 * g:2 * g + 2, :], x[:, 2 * g:2 * g + 2, :], ACT.Square).then_inc(s_sq, 1)
            norm_root(act, q)
            for g in range(4):
                act.wait_ge(s_yT, g + 1)
                act.activation(stage[:, g // 2, 512 * (g % 2):512 * (g % 2) + 512], bank[g][:, :],
                               ACT.Copy).then_inc(s_y, 1)

        @block.vector
        def _(dve):
            for i, v in enumerate((EPS, P * EPS, 1.0, 96 * EPS)):
                ins = dve.memset(eps_col[:, i:i + 1], v)
            ins.then_inc(s_setup, 1)
            dve.memset(zeros[:, :].bitcast(F32), 0.0).then_inc(s_setup, 1)
            for i in range(START):
                dve.memset(spare[:, i:i + 1], 0.0).then_inc(s_lo, 1)
            for g in range(4):
                dve.wait_ge(s_xT, g + 1)
                dve.tensor_copy(x[:, 2 * g:2 * g + 2, :], pair[g % 2]).then_inc(s_x, 1)
            dve.wait_ge(s_vT, 1)
            for b in range(4):
                n = ROWS1 if b < 2 else ROWS2
                ins = dve.tensor_copy(vecs[:, b, 0:n], bank[7][:, P * b:P * b + n])
            ins.then_inc(s_vecs, 1)
            for b in blocks:
                with dve.Fori(0, LAYERS, 1) as l:
                    n = ROWS1 if b == 0 else ROWS2
                    dve.drain()
                    dve.tensor_copy(vec[:, 0:n], vecs[:, ds(l + 2 * b, 1), 0:n].rearrange("p a n -> p (a n)"))
                    dve.drain()
                    ffn_dve(dve, in_layer(plans[b], 0, l), norm_index(b, l, 0), ffn_index(b, l, 0), V_FFN1)
                    mixer_dve[b](dve, in_layer(plans[b], 1, l), in_layer(plans[b], 2, l), norm_index(b, l, 1), l)
                    ffn_dve(dve, in_layer(plans[b], 3, l), norm_index(b, l, 2),
                            ffn_index(b, l, 1), V_FFN2)
            q = last_norm
            dve.drain()
            dve.tensor_copy(vec[:, 0:ROWS2], vecs[:, 3, 0:ROWS2])
            dve.drain()
            norm_scale(dve, q)
            for kc in range(KC):
                norm_tile(dve, q, V_FINAL, kc)

        @block.gpsimd
        def _(pool):
            pool.wait_ge(s_rest, 16 * n_rest)
            with pool.Fori(0, LAYERS, 1) as l:
                mixer1_pool(pool, in_layer(plans[0], 2, l), l)
            with pool.Fori(0, LAYERS, 1) as l:
                po = in_layer(plans[1], 2, l)
                pool.wait_ge(s_lo, po.base + (3 + START))
                split_lo(pool, po, 3)
                split_lo(pool, po, 4)

def kernel(**inputs):
    import concourse.bacc as bacc
    from concourse.bass_utils import run_bass_kernel_spmd

    nc = bacc.Bacc("TRN2", target_bir_lowering=False, num_devices=1)
    arrays = {f"in_{n}": np.ascontiguousarray(inputs[n]) for n in INPUTS}
    arrays["in_consts"] = const_table()[0]
    drams = {n: nc.dram_tensor(n, v.shape, mybir.dt.from_np(v.dtype), kind="ExternalInput").ap()
             for n, v in arrays.items()}
    out = nc.dram_tensor("out_0", (1, T, D), F32, kind="ExternalOutput").ap()
    build(nc, {n: drams[f"in_{n}"] for n in INPUTS}, drams["in_consts"], out)
    return run_bass_kernel_spmd(nc, [arrays], core_ids=[0]).results[0]["out_0"]
```
